# Optimizing a Trainium2 kernel written in Bass

```python
import jax
import jax.numpy as jnp
from jax import lax
import numpy as np
import jax, jax.numpy as jnp

D_MODEL = 1024
BATCH = 1
SEQ = 1024
DEPTH = 1

HEAD_DIM = 64
RWKV_WIDTH = D_MODEL // 2
RWKV_HEADS = RWKV_WIDTH // HEAD_DIM
DECAY_LORA = 64
ICLR_LORA = 64
RWKV_GN_EPS = 64e-5
NSA_WIDTH = D_MODEL // 4
NSA_HEADS = NSA_WIDTH // HEAD_DIM
N_BRANCH = 3
CMP_BLOCK = 32
CMP_STRIDE = 16
SEL_BLOCK = 64
SEL_TOPK = 16
WINDOW = 512
MEM_LEN = 256
MEM_WIDTH = D_MODEL // 4
MEM_HEADS = 4
MEM_HEAD_DIM = MEM_WIDTH // MEM_HEADS
MIX_WIDTH = RWKV_WIDTH + NSA_WIDTH + MEM_WIDTH
ROPE_THETA = 500000.0
ROPE_DIM = HEAD_DIM // 4
Q_BLOCK = 128
NORM_EPS = 1e-6
NEG_INF = -1e30
FORCE_SCORE = 1e4

RWKV_SIZES = (RWKV_WIDTH, RWKV_WIDTH, RWKV_WIDTH, RWKV_WIDTH, DECAY_LORA, ICLR_LORA)
NSA_SIZES = (NSA_WIDTH, NSA_WIDTH, NSA_HEADS * N_BRANCH) + (HEAD_DIM,) * 6
MEM_SIZES = (MEM_WIDTH, MEM_WIDTH)
RWKV_COLS = sum(RWKV_SIZES)
NSA_COLS = sum(NSA_SIZES)
MEM_COLS = sum(MEM_SIZES)
IN_COLS = RWKV_COLS + NSA_COLS + MEM_COLS


def split_cols(p, sizes):
    offs = [int(o) for o in np.cumsum(sizes)[:-1]]
    return jnp.split(p, offs, axis=-1)

def rms_norm(x, g, eps=NORM_EPS):
    xf = x.astype(jnp.float32)
    y = xf * lax.rsqrt(jnp.mean(xf * xf, axis=-1, keepdims=True) + eps)
    return (y * g.astype(jnp.float32)).astype(x.dtype)

def partial_rope(x, pos):
    half = ROPE_DIM // 2
    inv_freq = ROPE_THETA ** (-jnp.arange(half, dtype=jnp.float32) / half)
    ang = pos.astype(jnp.float32)[:, None] * inv_freq[None, :]
    cos = jnp.cos(ang)[:, None, :]
    sin = jnp.sin(ang)[:, None, :]
    xf = x.astype(jnp.float32)
    x1 = xf[..., :half]
    x2 = xf[..., half:ROPE_DIM]
    out = jnp.concatenate([x1 * cos - x2 * sin, x2 * cos + x1 * sin, xf[..., ROPE_DIM:]], axis=-1)
    return out.astype(x.dtype)

def masked_softmax(s, mask):
    s = jnp.where(mask, s.astype(jnp.float32), NEG_INF)
    m = jnp.max(s, axis=-1, keepdims=True)
    e = jnp.exp(s - m) * mask
    return e / jnp.maximum(jnp.sum(e, axis=-1, keepdims=True), 1e-30)

def head_rms_norm(o, g):
    of = o.astype(jnp.float32)
    y = of * lax.rsqrt(jnp.mean(of * of, axis=-1, keepdims=True) + NORM_EPS)
    return (y * g.astype(jnp.float32)).astype(o.dtype)

def rwkv7_scan(r, decay, k, v, kk, a):
    B, T, H, N = r.shape

    def step(S, inp):
        r_t, w_t, k_t, v_t, kk_t, a_t = inp
        sa = jnp.einsum('bhvk,bhk->bhv', S, -kk_t)
        S = (S * w_t[:, :, None, :]
             + sa[..., None] * (kk_t * a_t)[:, :, None, :]
             + v_t[..., None] * k_t[:, :, None, :])
        y = jnp.einsum('bhvk,bhk->bhv', S, r_t)
        return S, y

    xs = tuple(jnp.moveaxis(u, 1, 0) for u in (r, decay, k, v, kk, a))
    S0 = jnp.zeros((B, H, N, N), jnp.float32)
    _, y = lax.scan(step, S0, xs)
    return jnp.moveaxis(y, 0, 1)

def rwkv7_group(p, mu, w0, w_up, a0, a_up, k_k, k_a, r_k, ln_w, ln_b):
    B, T, _ = p.shape
    H, N = RWKV_HEADS, HEAD_DIM
    pf = p.astype(jnp.float32)
    prev = jnp.pad(pf, ((0, 0), (1, 0), (0, 0)))[:, :-1]
    pf = pf + mu * (prev - pf)
    r, k, v, gate, wd, ad = split_cols(pf, RWKV_SIZES)
    w_log = -jax.nn.softplus(-(w0 + jnp.tanh(wd) @ w_up)) - 0.5
    decay = jnp.exp(-jnp.exp(w_log))
    a = jax.nn.sigmoid(a0 + ad @ a_up)
    kk = k * k_k
    k = k * (1.0 + (a - 1.0) * k_a)
    r, k, v, kk, a, decay = (u.reshape(B, T, H, N) for u in (r, k, v, kk, a, decay))
    kk = kk / jnp.maximum(jnp.sqrt(jnp.sum(kk * kk, axis=-1, keepdims=True)), 1e-12)
    y = rwkv7_scan(r, decay, k, v, kk, a)
    mean = jnp.mean(y, axis=-1, keepdims=True)
    var = jnp.mean(jnp.square(y - mean), axis=-1, keepdims=True)
    y = (y - mean) * lax.rsqrt(var + RWKV_GN_EPS) * ln_w.reshape(H, N) + ln_b.reshape(H, N)
    y = y + jnp.sum(r * k * r_k, axis=-1, keepdims=True) * v
    y = y.reshape(B, T, RWKV_WIDTH) * jax.nn.silu(gate)
    return y.astype(p.dtype)

def nsa_group(p, pos, cmp_pos, ck_w1, ck_w2, cv_w1, cv_w2, gate_b, out_g):
    B, T, _ = p.shape
    Hn, D = NSA_HEADS, HEAD_DIM
    q, gate, glog, kc, vc, ks, vs, kw, vw = split_cols(p, NSA_SIZES)
    q = q.reshape(B, T, Hn, D)
    q_rope = partial_rope(q, pos)
    ks = partial_rope(ks[:, :, None, :], pos)[:, :, 0]
    kw = partial_rope(kw[:, :, None, :], pos)[:, :, 0]
    scale = HEAD_DIM ** -0.5

    n_cmp = (T - CMP_BLOCK) // CMP_STRIDE + 1
    blk = jnp.arange(n_cmp)[:, None] * CMP_STRIDE + jnp.arange(CMP_BLOCK)[None, :]

    def compress(u, w1, w2):
        ub = (u[:, blk] + cmp_pos).reshape(B, n_cmp, CMP_BLOCK * D)
        return jax.nn.silu(ub @ w1) @ w2

    k_cmp = compress(kc, ck_w1, ck_w2)
    v_cmp = compress(vc, cv_w1, cv_w2)
    cmp_end = blk[:, -1]

    n_sel = T // SEL_BLOCK
    n_top = min(SEL_TOPK, n_sel)
    sel_start = jnp.arange(n_sel) * SEL_BLOCK
    overlap = jnp.clip(jnp.minimum(blk[:, -1:] + 1, sel_start[None, :] + SEL_BLOCK)
                       - jnp.maximum(blk[:, :1], sel_start[None, :]), 0, None)
    overlap = overlap.astype(jnp.float32) / CMP_BLOCK
    k_sel_blk = ks.reshape(B, n_sel, SEL_BLOCK, D)
    v_sel_blk = vs.reshape(B, n_sel, SEL_BLOCK, D)
    blk_id = jnp.arange(n_sel)

    kw_pad = jnp.pad(kw, ((0, 0), (WINDOW, 0), (0, 0)))
    vw_pad = jnp.pad(vw, ((0, 0), (WINDOW, 0), (0, 0)))

    def per_block(qb):
        t0 = qb * Q_BLOCK
        tq = t0 + jnp.arange(Q_BLOCK)
        qn = lax.dynamic_slice_in_dim(q, t0, Q_BLOCK, axis=1)
        qr = lax.dynamic_slice_in_dim(q_rope, t0, Q_BLOCK, axis=1)
        s_c = jnp.einsum('bqhd,bcd->bhqc', qn, k_cmp) * scale
        p_c = masked_softmax(s_c, cmp_end[None, :] <= tq[:, None])
        o_c = jnp.einsum('bhqc,bcd->bqhd', p_c.astype(v_cmp.dtype), v_cmp)
        imp = jnp.einsum('bhqc,cs->bqs', p_c, overlap)
        cur = tq // SEL_BLOCK
        valid = blk_id[None, :] <= cur[:, None]
        forced = (blk_id[None, :] == 0) | (blk_id[None, :] == cur[:, None]) | (blk_id[None, :] == cur[:, None] - 1)
        score = jnp.where(forced, FORCE_SCORE, jnp.where(valid, imp, -1.0))
        _, idx = lax.top_k(score, n_top)
        kg = jax.vmap(lambda kb, ib: kb[ib])(k_sel_blk, idx).reshape(B, Q_BLOCK, n_top * SEL_BLOCK, D)
        vg = jax.vmap(lambda vb, ib: vb[ib])(v_sel_blk, idx).reshape(B, Q_BLOCK, n_top * SEL_BLOCK, D)
        kpos = (idx[..., None] * SEL_BLOCK + jnp.arange(SEL_BLOCK)).reshape(B, Q_BLOCK, n_top * SEL_BLOCK)
        s_s = jnp.einsum('bqhd,bqkd->bhqk', qr, kg) * scale
        p_s = masked_softmax(s_s, (kpos <= tq[None, :, None])[:, None])
        o_s = jnp.einsum('bhqk,bqkd->bqhd', p_s.astype(vg.dtype), vg)
        kwb = lax.dynamic_slice_in_dim(kw_pad, t0, Q_BLOCK + WINDOW, axis=1)
        vwb = lax.dynamic_slice_in_dim(vw_pad, t0, Q_BLOCK + WINDOW, axis=1)
        wpos = t0 - WINDOW + jnp.arange(Q_BLOCK + WINDOW)
        diff = tq[:, None] - wpos[None, :]
        m_w = (diff >= 0) & (diff < WINDOW) & (wpos[None, :] >= 0)
        s_w = jnp.einsum('bqhd,bkd->bhqk', qr, kwb) * scale
        p_w = masked_softmax(s_w, m_w)
        o_w = jnp.einsum('bhqk,bkd->bqhd', p_w.astype(vwb.dtype), vwb)
        return o_c, o_s, o_w

    o_c, o_s, o_w = lax.map(per_block, jnp.arange(T // Q_BLOCK))
    o_c, o_s, o_w = (jnp.moveaxis(o, 0, 1).reshape(B, T, Hn, D) for o in (o_c, o_s, o_w))
    g = jax.nn.sigmoid(glog.reshape(B, T, Hn, N_BRANCH) + gate_b.reshape(Hn, N_BRANCH))
    o = g[..., 0:1] * o_c + g[..., 1:2] * o_s + g[..., 2:3] * o_w
    o = head_rms_norm(o, out_g.reshape(Hn, D))
    return o.reshape(B, T, NSA_WIDTH) * jax.nn.silu(gate)

def memory_group(p, mem_k, mem_v, out_g):
    B, T, _ = p.shape
    q, gate = split_cols(p, MEM_SIZES)
    q = q.reshape(B, T, MEM_HEADS, MEM_HEAD_DIM)
    s = jnp.einsum('bthd,bmhd->bhtm', q, mem_k) * (MEM_HEAD_DIM ** -0.5)
    prob = jax.nn.softmax(s.astype(jnp.float32), axis=-1)
    o = jnp.einsum('bhtm,bmhd->bthd', prob.astype(mem_v.dtype), mem_v)
    o = head_rms_norm(o, out_g.reshape(MEM_HEADS, MEM_HEAD_DIM))
    return o.reshape(B, T, MEM_WIDTH) * jax.nn.silu(gate)

def first_inputs(seed: int = 0) -> dict:
    key = jax.random.key(seed)
    ks = jax.random.split(key, 32)
    L = DEPTH
    f32 = jnp.float32

    def nrm(k, shape, scale):
        return jax.random.normal(k, shape, f32) * scale

    def gain(k, shape):
        return 1.0 + 0.05 * jax.random.normal(k, shape, f32)

    cmp_in = CMP_BLOCK * HEAD_DIM
    return {
        'x': nrm(ks[0], (BATCH, SEQ, D_MODEL), 1.0),
        'mem': nrm(ks[1], (BATCH, MEM_LEN, D_MODEL), 1.0),
        'norm_in_g': gain(ks[2], (L, D_MODEL)),
        'w_in': nrm(ks[3], (L, D_MODEL, IN_COLS), D_MODEL ** -0.5),
        'rwkv_mu': jax.random.uniform(ks[4], (L, RWKV_COLS), f32, 0.2, 0.8),
        'rwkv_w0': jax.random.uniform(ks[5], (L, RWKV_WIDTH), f32, -5.0, -1.0),
        'rwkv_w_up': nrm(ks[6], (L, DECAY_LORA, RWKV_WIDTH), 0.1 * DECAY_LORA ** -0.5),
        'rwkv_a0': nrm(ks[7], (L, RWKV_WIDTH), 0.5),
        'rwkv_a_up': nrm(ks[8], (L, ICLR_LORA, RWKV_WIDTH), ICLR_LORA ** -0.5),
        'rwkv_k_k': 0.85 + 0.05 * jax.random.normal(ks[9], (L, RWKV_WIDTH), f32),
        'rwkv_k_a': 1.0 + 0.05 * jax.random.normal(ks[10], (L, RWKV_WIDTH), f32),
        'rwkv_r_k': nrm(ks[11], (L, RWKV_HEADS, HEAD_DIM), 0.1),
        'rwkv_ln_w': gain(ks[12], (L, RWKV_WIDTH)),
        'rwkv_ln_b': nrm(ks[13], (L, RWKV_WIDTH), 0.02),
        'nsa_cmp_pos': nrm(ks[14], (L, CMP_BLOCK, HEAD_DIM), 0.1),
        'nsa_cmp_k_w1': nrm(ks[15], (L, cmp_in, HEAD_DIM), cmp_in ** -0.5),
        'nsa_cmp_k_w2': nrm(ks[16], (L, HEAD_DIM, HEAD_DIM), HEAD_DIM ** -0.5),
        'nsa_cmp_v_w1': nrm(ks[17], (L, cmp_in, HEAD_DIM), cmp_in ** -0.5),
        'nsa_cmp_v_w2': nrm(ks[18], (L, HEAD_DIM, HEAD_DIM), HEAD_DIM ** -0.5),
        'nsa_gate_b': nrm(ks[19], (L, NSA_HEADS * N_BRANCH), 0.1),
        'nsa_out_g': gain(ks[20], (L, NSA_WIDTH)),
        'mem_norm_g': gain(ks[21], (L, D_MODEL)),
        'w_mem_kv': nrm(ks[22], (L, D_MODEL, 2 * MEM_WIDTH), D_MODEL ** -0.5),
        'mem_out_g': gain(ks[23], (L, MEM_WIDTH)),
        'w_out': nrm(ks[24], (L, MIX_WIDTH, D_MODEL), MIX_WIDTH ** -0.5),
        'norm_final_g': gain(ks[25], (D_MODEL,)),
    }

def first_block(x, mem, norm_in_g, w_in, rwkv_mu, rwkv_w0, rwkv_w_up, rwkv_a0, rwkv_a_up,
              rwkv_k_k, rwkv_k_a, rwkv_r_k, rwkv_ln_w, rwkv_ln_b, nsa_cmp_pos, nsa_cmp_k_w1,
              nsa_cmp_k_w2, nsa_cmp_v_w1, nsa_cmp_v_w2, nsa_gate_b, nsa_out_g, mem_norm_g,
              w_mem_kv, mem_out_g, w_out, norm_final_g):
    B, T, _ = x.shape
    M = mem.shape[1]
    pos = jnp.arange(T)
    for l in range(DEPTH):
        h = rms_norm(x, norm_in_g[l])
        p = h @ w_in[l]
        p_rwkv, p_nsa, p_mem = jnp.split(p, [RWKV_COLS, RWKV_COLS + NSA_COLS], axis=-1)
        y_rwkv = rwkv7_group(p_rwkv, rwkv_mu[l], rwkv_w0[l], rwkv_w_up[l], rwkv_a0[l], rwkv_a_up[l],
                             rwkv_k_k[l], rwkv_k_a[l], rwkv_r_k[l], rwkv_ln_w[l], rwkv_ln_b[l])
        y_nsa = nsa_group(p_nsa, pos, nsa_cmp_pos[l], nsa_cmp_k_w1[l], nsa_cmp_k_w2[l],
                          nsa_cmp_v_w1[l], nsa_cmp_v_w2[l], nsa_gate_b[l], nsa_out_g[l])
        kv = rms_norm(mem, mem_norm_g[l]) @ w_mem_kv[l]
        mem_k, mem_v = jnp.split(kv.reshape(B, M, 2, MEM_HEADS, MEM_HEAD_DIM), 2, axis=2)
        y_mem = memory_group(p_mem, mem_k[:, :, 0], mem_v[:, :, 0], mem_out_g[l])
        y = jnp.concatenate([y_rwkv.astype(x.dtype), y_nsa.astype(x.dtype), y_mem.astype(x.dtype)], axis=-1)
        x = x + y @ w_out[l]
    return rms_norm(x, norm_final_g)


RET_WIDTH = D_MODEL // 2
RET_HEADS = 4
RET_HEAD_DIM = RET_WIDTH // RET_HEADS
CONV_WIDTH = D_MODEL - RET_WIDTH
CONV_GROUPS = 8
CONV_K = 3
MIX_WIDTH_2 = RET_WIDTH + CONV_WIDTH
IN_COLS_2 = 4 * RET_WIDTH + 3 * CONV_WIDTH
CHUNK = 128
ROPE_BASE = 10000.0
N_GROUPS = 8
EXPERTS_PER_GROUP = 8
N_EXPERTS = N_GROUPS * EXPERTS_PER_GROUP
TOP_K = 2
EXPERT_FF = D_MODEL // 2
MOE_BLOCK = 128
EPS = 1e-6


def rmsnorm(x, w):
    xf = x.astype(jnp.float32)
    y = xf * lax.rsqrt(jnp.mean(xf * xf, axis=-1, keepdims=True) + EPS)
    return (y * w.astype(jnp.float32)).astype(x.dtype)

def rotary(x, pos):
    half = x.shape[-1] // 2
    inv = ROPE_BASE ** (-jnp.arange(half, dtype=jnp.float32) / half)
    ang = pos.astype(jnp.float32)[:, None] * inv[None, :]
    cos = jnp.cos(ang)[None, :, None, :]
    sin = jnp.sin(ang)[None, :, None, :]
    xf = x.astype(jnp.float32)
    x1, x2 = xf[..., :half], xf[..., half:]
    return jnp.concatenate([x1 * cos - x2 * sin, x2 * cos + x1 * sin], axis=-1)

def retention_chunkwise(q, k, v):
    b, s, h, d = q.shape
    nc = s // CHUNK
    log_g = jnp.log1p(-(2.0 ** (-5.0 - jnp.arange(h, dtype=jnp.float32))))
    idx = jnp.arange(CHUNK, dtype=jnp.float32)
    rel = idx[:, None] - idx[None, :]
    causal = rel >= 0
    intra_decay = jnp.where(causal[None], jnp.exp(log_g[:, None, None] * jnp.where(causal, rel, 0.0)[None]), 0.0)
    k_decay = jnp.exp(log_g[:, None] * (CHUNK - 1 - idx)[None, :])
    q_decay = jnp.exp(log_g[:, None] * (idx + 1)[None, :])
    chunk_decay = jnp.exp(log_g * CHUNK)

    qc = q.reshape(b, nc, CHUNK, h, d)
    kc = k.reshape(b, nc, CHUNK, h, d)
    vc = v.reshape(b, nc, CHUNK, h, d)

    scores = jnp.einsum('bnihd,bnjhd->bnhij', qc, kc) * intra_decay[None, None]
    o_intra = jnp.einsum('bnhij,bnjhd->bnihd', scores, vc)

    kv = jnp.einsum('bnjhd,hj,bnjhe->bnhde', kc, k_decay, vc)

    def step(state, kv_n):
        return chunk_decay[None, :, None, None] * state + kv_n, state

    _, prev = lax.scan(step, jnp.zeros((b, h, d, d), jnp.float32), jnp.moveaxis(kv, 1, 0))
    prev = jnp.moveaxis(prev, 0, 1)
    o_inter = jnp.einsum('bnihd,bnhde->bnihe', qc, prev) * q_decay.T[None, None, :, :, None]
    return (o_intra + o_inter).reshape(b, s, h, d)

def head_groupnorm(o, w):
    b, s, h, d = o.shape
    mu = jnp.mean(o, axis=-1, keepdims=True)
    var = jnp.mean(jnp.square(o - mu), axis=-1, keepdims=True)
    y = (o - mu) * lax.rsqrt(var + EPS)
    return y.reshape(b, s, h * d) * w.astype(jnp.float32)

def causal_depthwise_conv(u, w):
    return lax.conv_general_dilated(
        u, w[:, None, :], window_strides=(1,), padding=[(CONV_K - 1, 0)],
        dimension_numbers=('NWC', 'WIO', 'NWC'), feature_group_count=u.shape[-1])

def mixer(h, w_in, ret_gn_w, conv_w, w_o):
    b, s, _ = h.shape
    proj = h @ w_in
    R, C = RET_WIDTH, CONV_WIDTH
    q, k, v, g, gb, gc, u = jnp.split(proj, [R, 2 * R, 3 * R, 4 * R, 4 * R + C, 4 * R + 2 * C], axis=-1)
    pos = jnp.arange(s)
    q = rotary(q.reshape(b, s, RET_HEADS, RET_HEAD_DIM), pos) * (RET_HEAD_DIM ** -0.5)
    k = rotary(k.reshape(b, s, RET_HEADS, RET_HEAD_DIM), pos)
    v = v.reshape(b, s, RET_HEADS, RET_HEAD_DIM).astype(jnp.float32)
    ret = retention_chunkwise(q, k, v)
    ret = (jax.nn.silu(g.astype(jnp.float32)) * head_groupnorm(ret, ret_gn_w)).astype(h.dtype)
    conv = gb * causal_depthwise_conv(gc * u, conv_w)
    return jnp.concatenate([ret, conv], axis=-1) @ w_o

def expert_dispatch(t, expert, gate, w_gate, w_up, w_down):
    n, d = t.shape
    e_total = w_gate.shape[0]
    n_slots = n * TOP_K
    flat_e = expert.reshape(-1)
    flat_tok = jnp.repeat(jnp.arange(n, dtype=jnp.int32), TOP_K)
    flat_w = gate.reshape(-1)
    order = jnp.argsort(flat_e)
    se, stok, sw = flat_e[order], flat_tok[order], flat_w[order]
    counts = jnp.bincount(flat_e, length=e_total)
    starts = jnp.cumsum(counts) - counts
    padded = ((counts + MOE_BLOCK - 1) // MOE_BLOCK) * MOE_BLOCK
    pad_ends = jnp.cumsum(padded)
    pad_starts = pad_ends - padded
    dest = pad_starts[se] + (jnp.arange(n_slots) - starts[se])
    n_blocks = -(-n_slots // MOE_BLOCK) + e_total
    cap = n_blocks * MOE_BLOCK
    buf_tok = jnp.full((cap,), n, jnp.int32).at[dest].set(stok)
    buf_w = jnp.zeros((cap,), t.dtype).at[dest].set(sw.astype(t.dtype))
    block_e = jnp.minimum(jnp.searchsorted(pad_ends, jnp.arange(n_blocks) * MOE_BLOCK, side='right'), e_total - 1)
    t_pad = jnp.concatenate([t, jnp.zeros((1, d), t.dtype)], axis=0)

    def run_block(args):
        tok, e = args
        xb = t_pad[tok]
        hb = jax.nn.silu(xb @ w_gate[e]) * (xb @ w_up[e])
        return hb @ w_down[e]

    yb = lax.map(run_block, (buf_tok.reshape(n_blocks, MOE_BLOCK), block_e))
    y = jax.ops.segment_sum(yb.reshape(cap, d) * buf_w[:, None], buf_tok, num_segments=n + 1)
    return y[:n]

def hier_moe(h, rg_w, rg_b, re_w, re_b, w_gate, w_up, w_down):
    b, s, d = h.shape
    t = h.reshape(b * s, d)
    g_prob = jax.nn.softmax((t @ rg_w).astype(jnp.float32) + rg_b.astype(jnp.float32), axis=-1)
    p_group, g_sel = lax.top_k(g_prob, 1)
    p_group, g_sel = p_group[:, 0], g_sel[:, 0]
    e_logits_all = jnp.einsum('nd,gde->nge', t, re_w).astype(jnp.float32) + re_b.astype(jnp.float32)[None]
    e_logits = jnp.take_along_axis(e_logits_all, g_sel[:, None, None], axis=1)[:, 0]
    e_prob = jax.nn.softmax(e_logits, axis=-1)
    top_p, top_i = lax.top_k(e_prob, TOP_K)
    top_p = top_p / jnp.sum(top_p, axis=-1, keepdims=True)
    gate = p_group[:, None] * top_p
    expert = g_sel[:, None] * EXPERTS_PER_GROUP + top_i
    return expert_dispatch(t, expert, gate, w_gate, w_up, w_down).reshape(b, s, d)

def second_inputs(seed: int = 0) -> dict:
    key = jax.random.key(seed)
    ks = jax.random.split(key, 16)
    f32 = jnp.float32
    nrm = lambda k, shape, scale: jax.random.normal(k, shape, f32) * scale
    return {
        "x": nrm(ks[0], (BATCH, SEQ, D_MODEL), 1.0),
        "norm1_w": 1.0 + nrm(ks[1], (DEPTH, D_MODEL), 0.02),
        "w_in": nrm(ks[2], (DEPTH, D_MODEL, IN_COLS_2), D_MODEL ** -0.5),
        "ret_gn_w": 1.0 + nrm(ks[3], (DEPTH, RET_WIDTH), 0.02),
        "conv_w": nrm(ks[4], (DEPTH, CONV_K, CONV_WIDTH), CONV_K ** -0.5),
        "w_o": nrm(ks[5], (DEPTH, MIX_WIDTH_2, D_MODEL), MIX_WIDTH_2 ** -0.5),
        "norm2_w": 1.0 + nrm(ks[6], (DEPTH, D_MODEL), 0.02),
        "router_g_w": nrm(ks[7], (DEPTH, D_MODEL, N_GROUPS), D_MODEL ** -0.5),
        "router_g_b": nrm(ks[8], (DEPTH, N_GROUPS), 0.01),
        "router_e_w": nrm(ks[9], (DEPTH, N_GROUPS, D_MODEL, EXPERTS_PER_GROUP), D_MODEL ** -0.5),
        "router_e_b": nrm(ks[10], (DEPTH, N_GROUPS, EXPERTS_PER_GROUP), 0.01),
        "w_gate": nrm(ks[11], (DEPTH, N_EXPERTS, D_MODEL, EXPERT_FF), D_MODEL ** -0.5),
        "w_up": nrm(ks[12], (DEPTH, N_EXPERTS, D_MODEL, EXPERT_FF), D_MODEL ** -0.5),
        "w_down": nrm(ks[13], (DEPTH, N_EXPERTS, EXPERT_FF, D_MODEL), EXPERT_FF ** -0.5),
        "final_norm_w": 1.0 + nrm(ks[14], (D_MODEL,), 0.02),
    }

def second_block(x, norm1_w, w_in, ret_gn_w, conv_w, w_o, norm2_w, router_g_w, router_g_b,
              router_e_w, router_e_b, w_gate, w_up, w_down, final_norm_w):
    for l in range(DEPTH):
        h = rmsnorm(x, norm1_w[l])
        x = x + mixer(h, w_in[l], ret_gn_w[l], conv_w[l], w_o[l])
        h = rmsnorm(x, norm2_w[l])
        x = x + hier_moe(h, router_g_w[l], router_g_b[l], router_e_w[l], router_e_b[l],
                         w_gate[l], w_up[l], w_down[l])
    return rmsnorm(x, final_norm_w)


def setup_inputs(seed=0):
    out = dict(first_inputs(seed))
    for name, value in second_inputs(seed + 1).items():
        if name != "x":
            out[name + "_2"] = value
    return out


def reference(
    x, mem, norm_in_g, w_in, rwkv_mu, rwkv_w0, rwkv_w_up, rwkv_a0, rwkv_a_up, rwkv_k_k,
    rwkv_k_a, rwkv_r_k, rwkv_ln_w, rwkv_ln_b, nsa_cmp_pos, nsa_cmp_k_w1, nsa_cmp_k_w2,
    nsa_cmp_v_w1, nsa_cmp_v_w2, nsa_gate_b, nsa_out_g, mem_norm_g, w_mem_kv, mem_out_g, w_out,
    norm_final_g, norm1_w_2, w_in_2, ret_gn_w_2, conv_w_2, w_o_2, norm2_w_2, router_g_w_2,
    router_g_b_2, router_e_w_2, router_e_b_2, w_gate_2, w_up_2, w_down_2, final_norm_w_2,
):
    x = first_block(
        x, mem, norm_in_g, w_in, rwkv_mu, rwkv_w0, rwkv_w_up, rwkv_a0, rwkv_a_up, rwkv_k_k,
        rwkv_k_a, rwkv_r_k, rwkv_ln_w, rwkv_ln_b, nsa_cmp_pos, nsa_cmp_k_w1, nsa_cmp_k_w2,
        nsa_cmp_v_w1, nsa_cmp_v_w2, nsa_gate_b, nsa_out_g, mem_norm_g, w_mem_kv, mem_out_g,
        w_out, norm_final_g,
    )
    return second_block(
        x, norm1_w_2, w_in_2, ret_gn_w_2, conv_w_2, w_o_2, norm2_w_2, router_g_w_2,
        router_g_b_2, router_e_w_2, router_e_b_2, w_gate_2, w_up_2, w_down_2, final_norm_w_2,
    )


_drawn_inputs = setup_inputs


def setup_inputs(seed=0):
    import zlib

    import numpy as np

    out = dict(_drawn_inputs(seed))
    spreads = {}
    factors = {'rwkv_w_up': 8.0,
     'rwkv_ln_b': 4.623,
     'nsa_gate_b': 3.035,
     'ret_gn_w_2': 4.198,
     'norm2_w_2': 2.793,
     'router_g_b_2': 5.733,
     'router_e_b_2': 7.725,
     'final_norm_w_2': 2.856}
    for name, (base, spread) in spreads.items():
        noise = np.random.default_rng([zlib.crc32(name.encode()), seed]).standard_normal(out[name].shape)
        drawn = base * np.exp(spread * noise) if base else spread * noise
        out[name] = jnp.asarray(drawn.astype(out[name].dtype))
    for name, factor in factors.items():
        out[name] = (out[name] * factor).astype(out[name].dtype)
    return out
```

```python
from contextlib import ExitStack

import numpy as np

import concourse.bass as bass
from concourse import mybir

F32 = mybir.dt.float32
I32 = mybir.dt.int32
U32 = mybir.dt.uint32
F32R = mybir.dt.float32r
BF16 = mybir.dt.bfloat16
ALU = mybir.AluOpType
ACT = mybir.ActivationFunctionType
AX = mybir.AxisListType

T = 1024
D = 1024
CAP = 64
NEXP = 64
NOVER = 31
NBLK = NEXP + NOVER
ARENA = 50600
BIG = 1e30

R0, K0, V0, G0, WA, NQ, NG, KSW, KVC, MQ, MG = 0, 4, 8, 12, 16, 17, 19, 21, 22, 23, 25
NGRP = 27

PAR = {}
_at = 0
for _n, _k in (("mu", 17), ("w0", 4), ("a0", 4), ("kk", 4), ("ka", 4), ("rk", 4), ("lnw", 4), ("lnb", 4),
               ("nin", 8), ("nmem", 8), ("nsag", 2), ("memg", 2), ("gn", 4), ("cw", 12), ("n1", 8)):
    PAR[_n] = _at
    _at += _k
NPAR = _at

CON = {}
_at = 0
for _n, _k in (("id", 128), ("sc", 512), ("m1", 128), ("m1t", 128), ("lv", 640), ("blk", 128),
               ("blkm", 128), ("perm", 128), ("diag", 128), ("far", 128), ("ones", 128), ("on128", 128), ("id2", 64)):
    CON[_n] = _at
    _at += _k
NCON = _at


RC_DM, RC_QD, RC_KD, NRC = 0, 512, 1024, 1028
CN2 = {}
_at = 0
for _n, _k in (("i64", 64), ("i96", NBLK), ("im", 128), ("tri", 128), ("tok", 8), ("dst", 16), ("half", 1), ("ip", 1)):
    CN2[_n] = (_at, _k)
    _at += _k
NC2 = _at


def retention_log(h):
    return np.log1p(-(np.float32(2.0) ** (np.float32(-5.0) - np.float32(h)))).astype(np.float32)


class Done:

    def __init__(self, sem, n=None):
        self.sem, self.n, self.used = sem, n, n is not None


def flat(waits):
    out = []
    for w in waits:
        out += flat(w) if isinstance(w, (list, tuple)) else [] if w is None else [w]
    return out


class Queue:

    def __init__(self, sem, raises=True):
        self.sem, self.items = sem, []
        self.last = None

    def add(self, fn, waits, d, step):
        ws = flat(waits)
        for x in ws:
            x.used = True
        self.items.append((fn, ws, d, step))
        self.last = d
        return d

    def do(self, fn, *waits):
        return self.add(fn, waits, Done(self.sem), 1)

    def dma(self, lane, fn, *waits):
        lane[1] += 16
        return self.add(fn, waits, Done(lane[0], lane[1]), 16)

    def when(self, load, limit, body):
        self.items.append((load, limit, body, 0))

    def number(self, counts):
        for fn, ws, d, step in self.items:
            if step == 0:
                d.number(counts)
            elif d.n is None and d.used:
                counts[d.sem.name] = counts.get(d.sem.name, 0) + 1
                d.n = counts[d.sem.name]

    def emit(self, eng, seen=None):
        seen = {} if seen is None else seen
        for fn, ws, d, step in self.items:
            if step == 0:
                with eng.If_cmp(fn(eng), ws, "IS_GT"):
                    d.emit(eng, dict(seen))
                continue
            for w in ws:
                if seen.get(w.sem.name, 0) < w.n:
                    eng.wait_ge(w.sem, w.n)
                    seen[w.sem.name] = w.n
            if fn is None and not d.used:
                continue
            if fn is None:
                eng.nop().then_inc(d.sem, 1)
                continue
            ins = fn(eng)
            if step == 16:
                ins.then_inc(d.sem, 16)
            elif d.used:
                ins.then_inc(d.sem, 1)


class Ring:

    def __init__(self, bufs):
        self.bufs, self.free, self.at = bufs, [[] for _ in bufs], 0

    def take(self):
        i = self.at
        while self.free[i] is None:
            i = (i + 1) % len(self.bufs)
            assert i != self.at, "none is free"
        self.at = (i + 1) % len(self.bufs)
        f, self.free[i] = self.free[i], None
        return self.bufs[i], f, i

    def give(self, i, *ends):
        self.free[i] = list(ends)


def program(nc, inp, out):
    ctx = ExitStack()

    with nc.sbuf_tensor("arena", [128, ARENA], F32) as arena:
        pass
    edge = [0, ARENA]

    class Scope:

        def __init__(self, side=0):
            self.side, self.mark = side, edge[side]

        def close(self):
            edge[self.side] = self.mark

    low = Scope()

    def rounded(name, at, n):
        with nc.sbuf_tensor(name + "_at", [128, at], F32), nc.sbuf_tensor(name, [128, n], F32R) as r:
            return r

    def sb(name, shape, dt=F32, c=None):
        n = 1
        for k in shape[1:]:
            n *= k
        if dt is BF16:
            n //= 2
        n = (n + 7) // 8 * 8
        side = (c or low).side
        if side == 0:
            a = edge[0]
            edge[0] += n
        else:
            edge[1] -= n
            a = edge[1]
        assert edge[0] <= edge[1], (name, edge)
        n = int(np.prod(shape[1:])) // (2 if dt is BF16 else 1)
        v = rounded(name, a, n)[0:shape[0], 0:n] if dt is F32R else arena[0:shape[0], a:a + n]
        if dt is not F32 and dt is not F32R:
            v = v.bitcast(dt)
        if len(shape) > 2:
            ax = " ".join("abcd"[k] for k in range(len(shape) - 1))
            v = v.rearrange(f"p ({ax}) -> p {ax}", **{"abcd"[k]: shape[k + 1] for k in range(len(shape) - 1)})
        return v

    def again(at):
        return [rounded(f"r{at}_{c}", at + c * T, T)[:, :] for c in range(8)]

    def sem(name):
        return ctx.enter_context(nc.semaphore(name))

    def lane(name):
        return [sem(name), 0]

    pe, act, dve, pool, sp = (Queue(sem(n)) for n in ("s_pe", "s_act", "s_dve", "s_pool", "s_sp"))
    banks = Ring([ctx.enter_context(nc.psum_tensor(f"bank{i}", [128, 512], F32)) for i in range(8)])

    def mm(o, l, r, start, stop, *w, skip=False):
        return pe.do(lambda e: e.matmul(o, l, r, start=start, stop=stop, skip_group_check=skip), *w)

    def tr(o, i, ident, *w):
        return pe.do(lambda e: e.transpose(o, i, ident), *w)

    def tt(q, o, a, b, op, *w):
        return q.do(lambda e: e.tensor_tensor(o, a, b, op), *w)

    def ts(q, o, a, s1, s2, op0, op1, *w):
        if op1 is None:
            return q.do(lambda e: e.tensor_scalar(o, a, s1, None, op0), *w)
        return q.do(lambda e: e.tensor_scalar(o, a, s1, s2, op0, op1), *w)

    def stt(o, a, s, b, op0, op1, *w):
        return dve.do(lambda e: e.scalar_tensor_tensor(o, a, s, b, op0, op1), *w)

    def cp(q, o, a, *w):
        if q is act:
            return q.do(lambda e: e.activation(o, a, ACT.Copy), *w)
        return q.do(lambda e: e.tensor_copy(o, a), *w)

    def af(o, a, f, *w, **k):
        return act.do(lambda e: e.activation(o, a, f, **k), *w)

    def ms(q, o, v, *w):
        return q.do(lambda e: e.memset(o, v), *w)

    def red(o, a, op, *w, **k):
        return dve.do(lambda e: e.tensor_reduce(o, a, AX.X, op, **k), *w)

    def load(q, ln, o, i, *w):
        return q.dma(ln, lambda e: e.dma_start(o, i), *w)

    def split_hi(o, a, *w):
        return cp(dve, o, a, *w)

    def split_lo(o, a, hi, *w):
        return tt(pool, o, a, hi.bitcast(F32), ALU.subtract, *w)

    def mm3(o, l, r, start, stop, *w):
        (lh, ll), (rh, rl) = l, r
        mm(o, lh, rh, start, False, *w)
        mm(o, lh, rl, False, False)
        return mm(o, ll, rh, False, stop)

    outs = []

    def barrier():
        lasts = [q.last for q in (pe, act, dve, pool, sp)]
        for q in (pe, act, dve, pool, sp):
            q.add(None, [x for x in lasts if x is not None], Done(q.sem), 1)
            q.last = None
        for i in range(8):
            banks.free[i] = []

    par = sb("par", [128, NPAR])
    con = sb("con", [128, NCON])
    ev = [act, dve]
    l_par, l_con = lane("l_par"), lane("l_con")
    d_par = load(sp, l_par, par[:, :], inp["par"][:, :])
    d_con = load(act, l_con, con[:, :], inp["con"][:, :])
    for q in (pe, act, dve, pool):
        q.add(None, [d_par, d_con], Done(q.sem), 1)

    def P(name, i=0):
        return par[:, PAR[name] + i:PAR[name] + i + 1]

    def C(name, a=0, n=128):
        return con[:, CON[name] + a:CON[name] + a + n]

    ident = C("id")
    spill = nc.dram_tensor("spill", [NGRP, 128, T], F32).ap()
    d_sp = [None] * NGRP

    mid = Scope()
    at_yT = edge[0]
    yT = sb("yT", [128, 8, T])
    toks = Scope()
    vtok = sb("vtok", [128, 8, 140])
    mk = sb("mk", [128, 2, 256])
    mv = sb("mv", [128, 2, 256])
    hctx = Scope()
    memT = sb("memT", [128, 8, 256], c=hctx)
    at_hT = edge[0]
    hT = sb("hT", [128, 8, T], c=hctx)

    def transposed(dst, src, col, scale, *w):
        ends = []
        for half in range(2):
            b, f, bi = banks.take()
            for c in range(4):
                k = 4 * half + c
                t = tr(b[:, c * 128:(c + 1) * 128], src[:, k * 128:(k + 1) * 128], ident, *w, f)
            g = par[:, scale + 4 * half:scale + 4 * half + 4].unsqueeze(2).to_broadcast([128, 4, 128])
            t = tt(dve, dst[:, 4 * half:4 * half + 4, col:col + 128],
                   b[:, :].rearrange("p (c n) -> p c n", c=4), g, ALU.mult, t)
            banks.give(bi, t)
            ends.append(t)
        return ends

    def rms_scale(dst, ss, n, eps, *w):
        a = ts(dve, dst, ss, 1.0 / n, eps, ALU.mult, ALU.add, *w)
        a = af(dst, dst, ACT.Sqrt, a)
        return dve.do(lambda e: e.reciprocal(dst, dst), a)

    c0 = Scope()
    xt = sb("xt", [128, 10, D], c=c0)
    junk = sb("junk", [128, D], c=c0)
    ssq = sb("ssq", [128, 10], c=c0)
    rst = sb("rst", [128, 10], c=c0)
    d_x = [load(sp if j % 2 else act, lane(f"l_x{j}"), xt[:, j, :],
                inp["x"][j * 128:(j + 1) * 128, :] if j < 8 else inp["mem"][(j - 8) * 128:(j - 7) * 128, :])
           for j in range(10)]
    s_ = None
    for j in range(10):
        s_ = af(junk[:, :], xt[:, j, :], ACT.Square, d_x[j], s_, accum_out=ssq[:, j:j + 1])
    d_r = rms_scale(rst[:, :], ssq[:, :], D, 1e-6, s_)
    hdone = []
    for j in range(10):
        a = ts(pool if j % 2 else dve, xt[:, j, :], xt[:, j, :], rst[:, j:j + 1], None, ALU.mult, None, d_r)
        if j < 8:
            hdone += transposed(hT, xt[:, j, :], j * 128, PAR["nin"], a)
        else:
            hdone += transposed(memT, xt[:, j, :], (j - 8) * 128, PAR["nmem"], a)
    barrier()
    c0.close()

    c1 = Scope()
    NW = 4
    wr = Ring([sb(f"wr{i}", [128, 8, 128], c=c1) for i in range(NW)])
    l_w = [lane(f"l_w{i}") for i in range(NW)]
    raw = Ring([sb(f"raw{i}", [128, T + 1], c=c1) for i in range(3)])
    dif = Ring([sb(f"dif{i}", [128, T], c=c1) for i in range(2)])
    mix = Ring([sb(f"mix{i}", [128, T], c=c1) for i in range(3)])
    l_sp = [lane(f"l_sp{i}") for i in range(3)]
    wv = sb("wv", [128, 8, 140], c=c1)
    wmem = sb("wmem", [128, 8, 512], c=c1)
    d_wm = load(act, lane("l_wmem"), wmem[:, :, :], inp["wmem"].rearrange("(c p) n -> p c n", p=128))
    d_wv = load(act, lane("l_wv"), wv[:, :, :], inp["wv"])
    zs = [ms(dve, raw.bufs[i][:, 0:1], 0.0) for i in range(3)]
    wlo = Ring([sb(f"wlo{i}", [128, 2, 8, 128], F32R, c=c1) for i in range(2)])
    hH, hL = again(at_yT), again(at_hT)
    hs_ = []
    for c in range(8):
        a = split_hi(hH[c], hT[:, c, :], hdone)
        hs_.append(split_lo(hL[c], hT[:, c, :], hH[c], a))
    ORDER = [WA] + list(range(16)) + list(range(17, NGRP))
    wq = []

    def load_w1():
        if len(wq) < NGRP:
            w, f, wi = wr.take()
            wq.append((w, wi, load(sp, l_w[wi], w[:, :, :], inp["w1"][ORDER[len(wq)]], f)))

    wsplit = []

    def prepare_w1(n):
        if n < NGRP:
            w, wi, dw = wq[n]
            wl, wlf, wli = wlo.take()
            a = split_hi(wl[:, 0, :, :], w[:, :, :], dw, wlf)
            a = split_lo(wl[:, 1, :, :], w[:, :, :], wl[:, 0, :, :], a)
            wr.give(wi, a)
            load_w1()
            wsplit.append((wl, wli, a))

    for n in range(NW):
        load_w1()
    prepare_w1(0)
    for at_, g in enumerate(ORDER):
        half = []
        wl, wli, wsp = wsplit[at_]
        prepare_w1(at_ + 1)
        rb, rf, ri = raw.take()
        for n in range(2):
            b, f, bi = banks.take()
            for c in range(8):
                ns = slice(n * 512, (n + 1) * 512)
                t = mm3(b[:, :], (wl[:, 0, c, :], wl[:, 1, c, :]), (hH[c][:, ns], hL[c][:, ns]), c == 0, c == 7, wsp, hs_, f)
            e = cp(act, rb[:, 1 + n * 512:513 + n * 512], b[:, :], t, rf, zs)
            banks.give(bi, e)
            half.append(e)
        wlo.give(wli, t)
        if g <= WA:
            db, df, di = dif.take()
            a = tt(pool, db[:, :], rb[:, 0:T], rb[:, 1:T + 1], ALU.subtract, half[1], df)
            mb, mf, mi = mix.take()
            a = stt(mb[:, :], db[:, :], P("mu", g), rb[:, 1:T + 1], ALU.mult, ALU.add, a, mf)
            dif.give(di, a)
            raw.give(ri, a)
            d_sp[g] = load(sp, l_sp[mi], spill[g], mb[:, :], a)
            mix.give(mi, d_sp[g])
        else:
            mb, mf, mi = mix.take()
            a = cp(pool, mb[:, :], rb[:, 1:T + 1], half[1], mf)
            raw.give(ri, a)
            d_sp[g] = load(sp, l_sp[mi], spill[g], mb[:, :], a)
            mix.give(mi, d_sp[g])
    wvh = sb("wvh", [128, 2, 8, 140], F32R, c=c1)
    x = split_hi(wvh[:, 0, :, :], wv[:, :, :], d_wv)
    x = split_lo(wvh[:, 1, :, :], wv[:, :, :], wvh[:, 0, :, :], x)
    for j in range(8):
        b, f, bi = banks.take()
        for c in range(8):
            js = slice(j * 128, (j + 1) * 128)
            t = mm3(b[:, 0:140], (hH[c][:, js], hL[c][:, js]), (wvh[:, 0, c, :], wvh[:, 1, c, :]), c == 0, c == 7, x, f)
        d_vt = cp(act, vtok[:, j, :], b[:, 0:140], t)
        banks.give(bi, d_vt)
    b, f, bi = banks.take()
    for g in range(2):
        for c in range(8):
            t = mm(b[:, g * 256:(g + 1) * 256], wmem[:, c, g * 128:(g + 1) * 128], memT[:, c, :], c == 0, c == 7, d_wm, f)
    d_mk = cp(act, mk[:, :, :], b[:, :].rearrange("p (g n) -> p g n", g=2), t)
    banks.give(bi, d_mk)
    b, f, bi = banks.take()
    for g in range(2):
        for c in range(8):
            t = mm(b[:, g * 256:(g + 1) * 256], memT[:, c, g * 128:(g + 1) * 128], wmem[:, c, 256:512], c == 0, c == 7, f)
    d_mv = cp(act, mv[:, :, :], b[:, :].rearrange("p (g n) -> p g n", g=2), t)
    banks.give(bi, d_mv)

    spills = [d_sp[g] for g in range(NGRP)]
    sp.add(None, spills, Done(sp.sem), 1)
    barrier()
    c1.close()
    hctx.close()

    c2 = Scope()
    wdad = sb("wdad", [128, T], c=c2)
    up = sb("up", [128, 512], c=c2)
    rmask = sb("rmask", [128, T], BF16, c=c2)
    quad = Ring([sb(f"quad{i}", [128, 4, T], c=c2) for i in range(2)])
    l_q = [[lane(f"l_q{i}{k}") for k in range(4)] for i in range(2)]
    E1, E2, E3, E4, E5, E6 = (sb(f"E{i}", [128, T], c=c2) for i in range(6))
    AR = sb("AR", [128, 2, T], c=c2)
    Bt = sb("Bt", [128, T], c=c2)
    Kt = sb("Kt", [128, T], c=c2)
    TL = sb("TL", [128, 4, 4, 128], c=c2)
    SC = sb("SC", [128, 2, 4, 4, 128], c=c2)
    Tm = sb("Tm", [128, 2, 4, 128], c=c2)
    TT = sb("TT", [128, 2, 4, 128], c=c2)
    Fm = sb("Fm", [128, 2, 4, 128], c=c2)
    XX = sb("XX", [128, 2, 4, 64], c=c2)
    WU = sb("WU", [128, 2, 4, 128], c=c2)
    Gm = sb("Gm", [128, 16, 128], c=c2)
    Hm = sb("Hm", [128, 16, 128], c=c2)
    Sm = sb("Sm", [128, 2, 128], c=c2)
    Qs = sb("Qs", [128, T], c=c2)
    Yi = sb("Yi", [128, T], c=c2)
    rkb = Kt[:, 0:128]
    st16 = sb("st16", [128, 16], c=c2)
    nz1 = ms(pool, Gm[:, :, :], 0.0)
    nz2 = ms(pool, Hm[:, :, :], 0.0)
    a = ms(pool, rmask[:, :], 1.0)
    nz3 = ms(pool, rmask[:, 0:T:64], 0.0, a)
    d_wd = load(sp, lane("l_wd"), wdad[:, :], spill[WA])
    d_up = load(act, lane("l_up"), up[:, :], inp["up"][:, :])
    d_th = af(wdad[0:64, :], wdad[0:64, :], ACT.Tanh, d_wd)

    def inverse_norm(sq, heads, scale, eps, floor, st, *w):
        hd = 128 // heads
        b, f, bi = banks.take()
        for j in range(8):
            t = mm(b[:, heads * j:heads * j + heads], sq[:, j * 128:(j + 1) * 128],
                   (C("blk") if heads == 2 else C("ones"))[:, 0:128:hd], True, True, *w, f)
        n = 8 * heads
        x = ts(dve, st[:, 0:n], b[:, 0:n], scale, eps, ALU.mult, ALU.add, t)
        banks.give(bi, x)
        x = af(st[:, 0:n], st[:, 0:n], ACT.Sqrt, x)
        x = ts(dve, st[:, 0:n], st[:, 0:n], floor, None, ALU.max, None, x)
        x = dve.do(lambda e: e.reciprocal(st[:, 0:n], st[:, 0:n]), x)
        x = cp(act, sq.rearrange("p (a n) -> p a n", a=n), st[:, 0:n].unsqueeze(2).to_broadcast([128, n, hd]), x, t)
        res = []
        for half in range(2):
            b, f, bi = banks.take()
            for jj in range(4):
                j = 4 * half + jj
                t = mm(b[:, jj * 128:(jj + 1) * 128], sq[:, j * 128:(j + 1) * 128], ident, True, True, x, f)
            res.append((b, bi, t))
        return res

    def group_norm(y, tmp, mean_m, heads, eps, st, *w):
        ends = []
        for n in range(2):
            b, f, bi = banks.take()
            t = mm(b[:, :], mean_m, y[:, n * 512:(n + 1) * 512], True, True, *w, f)
            t = tt(dve, y[:, n * 512:(n + 1) * 512], y[:, n * 512:(n + 1) * 512], b[:, :], ALU.subtract, t)
            banks.give(bi, t)
            ends.append(t)
        x = af(tmp, y, ACT.Square, ends)
        r = inverse_norm(tmp, heads, heads / 128.0, eps, 0.0, st, x)
        for n in range(2):
            b, bi, t = r[n]
            x = tt(dve, y[:, n * 512:(n + 1) * 512], y[:, n * 512:(n + 1) * 512], b[:, :], ALU.mult, t, x)
            banks.give(bi, x)
        return x

    qloads = {}

    def load_pair(i):
        q, f, qi = quad.take()
        qloads[i] = (q, qi, [load(sp, l_q[qi][k], q[:, k, :], spill[(R0, K0, V0, G0)[k] + i], f) for k in range(4)])

    load_pair(0)
    prev = None
    for i in range(4):
        q, qi, dq = qloads[i]
        if i < 3:
            load_pair(i + 1)
        r, k, v, g = (q[:, n, :] for n in range(4))
        cs = slice(i * 128, (i + 1) * 128)
        sg = []
        for n in range(2):
            ns = slice(n * 512, (n + 1) * 512)
            b, f, bi = banks.take()
            t = mm(b[:, :], up[0:64, cs], wdad[0:64, ns], True, True, d_up, d_th, f)
            x = af(E1[:, ns], b[:, :], ACT.Sigmoid, t, prev, bias=P("w0", i))
            banks.give(bi, x)
            b, f, bi = banks.take()
            t = mm(b[:, :], up[64:128, cs], wdad[64:128, ns], True, True, d_up, d_wd, f)
            y = af(E2[:, ns], b[:, :], ACT.Sigmoid, t, prev, bias=P("a0", i))
            banks.give(bi, y)
        d_g = af(g, g, ACT.Silu, dq[3])
        d_L = ts(dve, E1[:, :], E1[:, :], -float(np.exp(np.float32(-0.5))), None, ALU.mult, None, x)
        d_cum = dve.do(lambda e: e.tensor_tensor_scan(E3[:, :], rmask[:, :], E1[:, :], 0.0, ALU.mult, ALU.add),
                       d_L, nz3)
        x = ts(dve, E4[:, :], k, P("kk", i), None, ALU.mult, None, dq[1])
        x2 = af(E5[:, :], E4[:, :], ACT.Square, x, prev)
        res = inverse_norm(E5[:, :], 2, 1.0, 0.0, 1e-12, st16, x2)
        for n in range(2):
            b, bi, t = res[n]
            x = tt(dve, E4[:, n * 512:(n + 1) * 512], E4[:, n * 512:(n + 1) * 512], b[:, :], ALU.mult, t, x)
            banks.give(bi, x)
        d_kk = x
        x = ts(dve, E5[:, :], E2[:, :], -1.0, P("ka", i), ALU.add, ALU.mult, y, res[1][2])
        d_k = stt(k, E5[:, :], 1.0, k, ALU.add, ALU.mult, x)
        a0_ = ts(pool, rkb[:, :], C("blk"), P("rk", i), None, ALU.mult, None, prev)
        x = tt(pool, E5[:, :], r, k, ALU.mult, d_k, dq[0])
        bon = []
        for n in range(2):
            b, f, bi = banks.take()
            bon.append((b, bi, mm(b[:, :], rkb[:, :], E5[:, n * 512:(n + 1) * 512], True, True, x, a0_, f)))
        for n in range(2):
            b, bi, t = bon[n]
            d_bon = tt(dve, E5[:, n * 512:(n + 1) * 512], v[:, n * 512:(n + 1) * 512], b[:, :], ALU.mult, t, bon[1][2], dq[2])
            banks.give(bi, d_bon)
        d_b = tt(pool, E2[:, :], E2[:, :], E4[:, :], ALU.mult, d_kk, x)
        x = tt(pool, E6[:, :], E3[:, :], E1[:, :], ALU.subtract, d_cum)
        e6 = af(E6[:, :], E6[:, :], ACT.Exp, x)
        d_A = stt(AR[:, 0, :], E4[:, :], -1.0, E6[:, :], ALU.mult, ALU.mult, e6, d_kk, d_b)
        e1 = af(E1[:, :], E3[:, :], ACT.Exp, d_cum, x)
        d_R = tt(dve, AR[:, 1, :], r, E1[:, :], ALU.mult, e1)
        e6 = af(E6[:, :], E3[:, :], ACT.Exp, d_A, scale=-1.0)
        d_B = tt(dve, Bt[:, :], E2[:, :], E6[:, :], ALU.mult, e6, d_b)
        d_K = tt(dve, Kt[:, :], k, E6[:, :], ALU.mult, e6, d_k, bon[1][2])
        pc = E1[:, 63:T:64]
        pcb = pc.unsqueeze(2).to_broadcast([128, 16, 64])
        c3 = lambda a: a.rearrange("p (c t) -> p c t", c=16)
        d_Bh = tt(dve, c3(E2[:, :]), c3(Bt[:, :]), pcb, ALU.mult, d_B)
        d_Kh = tt(pool, c3(E6[:, :]), c3(Kt[:, :]), pcb, ALU.mult, d_K, d_B)
        d_D = tt(pool, c3(E3[:, :]), C("id2", 0, 64).unsqueeze(1).to_broadcast([128, 16, 64]), pcb, ALU.mult, e6, e1)
        done_half = None
        gh = []
        for hf in range(2):
            dTL = []
            for jj in range(4):
                j = 4 * hf + jj
                js = slice(j * 128, (j + 1) * 128)
                b, f, bi = banks.take()
                tr(b[:, 0:128], AR[:, 0, js], ident, d_A, f)
                tr(b[:, 128:256], E2[:, js], ident, d_Bh)
                tr(b[:, 256:384], E6[:, js], ident, d_Kh)
                t = tr(b[:, 384:512], v[:, js], ident, dq[2])
                t = cp(act, TL[:, jj, :, :], b[:, :].rearrange("p (a n) -> p a n", a=4), t, done_half)
                banks.give(bi, t)
                dTL.append(t)
            dSC = [[None] * 4, [None] * 4]
            dT, dTT = [None] * 2, [None] * 2
            scm = con[:, CON["sc"]:CON["sc"] + 512]
            for h in range(2):
                hs = slice(64 * h, 64 * h + 64)
                for jj in range(4):
                    js = slice((4 * hf + jj) * 128, (4 * hf + jj + 1) * 128)
                    b, f, bi = banks.take()
                    mm(b[:, 0:256].rearrange("p (a n) -> p a n", a=2), Bt[hs, js], AR[hs, :, js], True, True, d_B, d_A, d_R, f)
                    t = mm(b[:, 256:512].rearrange("p (a n) -> p a n", a=2), Kt[hs, js], AR[hs, :, js], True, True, d_K)
                    t = tt(dve, SC[:, h, jj, :, :].rearrange("p a n -> p (a n)"), b[:, :], scm, ALU.mult, t, done_half)
                    banks.give(bi, t)
                    dSC[h][jj] = t
                b, f, bi = banks.take()
                for jj in range(4):
                    js = slice((4 * hf + jj) * 128, (4 * hf + jj + 1) * 128)
                    t = mm(b[:, jj * 128:(jj + 1) * 128], AR[hs, 0, js], Bt[hs, js], True, True, f)
                b4 = b[:, :].rearrange("p (a n) -> p a n", a=4)
                bc = lambda m: m.unsqueeze(1).to_broadcast([128, 4, 128])
                x = tt(dve, Tm[:, h, :, :], b4, bc(C("m1")), ALU.mult, t, done_half)
                banks.give(bi, x)
                dT[h] = tt(pool, Tm[:, h, :, :], Tm[:, h, :, :], bc(ident), ALU.add, x)
                x = tt(pool, TT[:, h, :, :], SC[:, h, :, 0, :], bc(C("m1t")), ALU.mult, dSC[h][3], done_half)
                dTT[h] = tt(pool, TT[:, h, :, :], TT[:, h, :, :], bc(ident), ALU.add, x)
            for lv in range(5):
                lm = bc(C("lv", lv * 128))
                dF = [None] * 2
                for h in range(2):
                    b, f, bi = banks.take()
                    for jj in range(4):
                        t = mm(b[:, jj * 128:(jj + 1) * 128], SC[:, h, jj, 0, :], Tm[:, h, jj, :], True, True,
                               dT[h], dSC[h][3], f)
                    dF[h] = tt(dve, Fm[:, h, :, :], b[:, :].rearrange("p (a n) -> p a n", a=4), lm, ALU.mult, t)
                    banks.give(bi, dF[h])
                for h in range(2):
                    if lv < 4:
                        b, f, bi = banks.take()
                        for jj in range(4):
                            t = mm(b[:, jj * 128:(jj + 1) * 128], TT[:, h, jj, :], Fm[:, h, jj, :], True, True,
                                   dF[h], dTT[h], f)
                    b2, f2, bi2 = banks.take()
                    for jj in range(4):
                        t2 = mm(b2[:, jj * 128:(jj + 1) * 128], Fm[:, h, jj, :], TT[:, h, jj, :], True, True,
                                dF[h], dTT[h], f2)
                    if lv < 4:
                        dT[h] = tt(dve, Tm[:, h, :, :], Tm[:, h, :, :], b[:, :].rearrange("p (a n) -> p a n", a=4),
                                   ALU.add, t, t2)
                        banks.give(bi, dT[h])
                    dTT[h] = tt(dve, TT[:, h, :, :], TT[:, h, :, :], b2[:, :].rearrange("p (a n) -> p a n", a=4),
                                ALU.add, t2)
                    banks.give(bi2, dTT[h])
            dWU = [None] * 2
            for h in range(2):
                hc = slice(64 * h, 64 * h + 64)
                b, f, bi = banks.take()
                for jj in range(4):
                    t = mm(b[:, jj * 64:jj * 64 + 64], SC[:, h, jj, 2, :], TL[:, jj, 3, hc], True, True, dTL[3], f)
                dX = cp(act, XX[:, h, :, :], b[:, 0:256].rearrange("p (a n) -> p a n", a=4), t, done_half)
                banks.give(bi, dX)
                b, f, bi = banks.take()
                for jj in range(4):
                    mm(b[:, jj * 128:jj * 128 + 64], TT[:, h, jj, :], TL[:, jj, 0, hc], True, True, dTT[h], f)
                    t = mm(b[:, jj * 128 + 64:jj * 128 + 128], TT[:, h, jj, :], XX[:, h, jj, :], True, True, dX)
                dWU[h] = cp(act, WU[:, h, :, :], b[:, :].rearrange("p (a n) -> p a n", a=4), t, done_half)
                banks.give(bi, dWU[h])
            by, fy, iy = banks.take()
            bq, fq, iq = banks.take()
            for h in range(2):
                hs = slice(64 * h, 64 * h + 64)
                for jj in range(4):
                    n = slice(jj * 128, (jj + 1) * 128)
                    mm(by[hs, n], WU[:, h, jj, 64:128], SC[:, h, jj, 1, :], True, False, dWU[h], fy)
                    ty = mm(by[hs, n], TL[:, jj, 3, hs], SC[:, h, jj, 3, :], False, True)
                    tq = mm(bq[hs, n], WU[:, h, jj, 0:64], SC[:, h, jj, 1, :], True, True, fq)
            hn = slice(hf * 512, (hf + 1) * 512)
            dYi = cp(act, Yi[:, hn], by[:, :], ty, prev)
            banks.give(iy, dYi)
            dQ = tt(dve, Qs[:, hn], bq[:, :], AR[:, 1, hn], ALU.add, tq, prev)
            banks.give(iq, dQ)
            for par_ in range(2):
                rs = slice(64 * par_, 64 * par_ + 64)
                bg, fg, ig = banks.take()
                bh, fh, ih = banks.take()
                for h in range(2):
                    hs = slice(64 * h, 64 * h + 64)
                    for jj in range(4):
                        n = slice(jj * 64, jj * 64 + 64)
                        tg = mm(bg[hs, n], WU[rs, h, jj, 0:64], TL[rs, jj, 1, hs], True, True, dWU[h], fg)
                        mm(bh[hs, n], TL[rs, jj, 1, hs], WU[rs, h, jj, 64:128], True, False, fh)
                        th = mm(bh[hs, n], TL[rs, jj, 2, hs], TL[rs, jj, 3, hs], False, True)
                for h in range(2):
                    hs = slice(64 * h, 64 * h + 64)
                    cc = slice(8 * hf + par_, 8 * hf + 8, 2)
                    x = tt(dve, Gm[hs, cc, hs], bg[hs, 0:256].rearrange("p (a n) -> p a n", a=4),
                           E3[hs, :].rearrange("p (c t) -> p c t", c=16)[:, cc, :], ALU.add, tg, d_D, nz1, prev)
                    y_ = cp(act, Hm[hs, cc, hs], bh[hs, 0:256].rearrange("p (a n) -> p a n", a=4), th, nz2, prev)
                banks.give(ig, x)
                banks.give(ih, y_)
                gh += [x, y_]
            done_half = th
        s0 = ms(dve, Sm[:, 0, :], 0.0, prev)
        ds = s0
        rd = [None, None]
        ends = []
        for c in range(16):
            if c % 8 == 0:
                by, fy, iy = banks.take()
            n = slice((c % 8) * 64, (c % 8) * 64 + 64)
            ty = mm(by[:, n], Sm[:, c % 2, :], Qs[:, c * 64:c * 64 + 64], True, True, ds, dQ, fy)
            if c < 15:
                b, f, bi = banks.take()
                t = mm(b[:, 0:128], Gm[:, c, :], Sm[:, c % 2, :], True, True, ds, gh, f)
                ds = tt(dve, Sm[:, (c + 1) % 2, :], b[:, 0:128], Hm[:, c, :], ALU.add, t)
                banks.give(bi, ds)
            if c % 8 == 7:
                hn = slice((c // 8) * 512, (c // 8) * 512 + 512)
                x = tt(dve, Yi[:, hn], Yi[:, hn], by[:, :], ALU.add, ty, dYi)
                banks.give(iy, x)
                ends.append(x)
        x = group_norm(Yi[:, :], E1[:, :], C("blkm"), 2, 64e-5, st16, ends, gh, ty)
        x = ts(dve, Yi[:, :], Yi[:, :], P("lnw", i), P("lnb", i), ALU.mult, ALU.add, x)
        x = tt(pool, Yi[:, :], Yi[:, :], E5[:, :], ALU.add, x, d_bon)
        x = tt(pool, yT[:, i, :], Yi[:, :], g, ALU.mult, x, d_g)
        quad.give(qi, x)
        prev = x
    barrier()
    c2.close()

    c3_ = Scope()
    tl = [sb(f"tl{i}", [128, T], c=c3_) for i in range(10)]
    groups = [NQ, NQ + 1, MQ, MQ + 1, KSW, KVC, NG, NG + 1, MG, MG + 1]
    d_tl = [load(sp if n % 2 else act, lane(f"l_tl{n}"), tl[n][:, :], spill[g]) for n, g in enumerate(groups)]
    q0, q1, m0_, m1_, ksw, kvc = tl[:6]
    gates = tl[6:]
    rope = sb("rope", [128, 2, T], c=c3_)
    d_rope = load(sp, lane("l_rope"), rope[:, :, :], inp["rope"])
    cw1 = sb("cw1", [128, 32, 64], c=c3_)
    cw2 = sb("cw2", [128, 128], c=c3_)
    cpos = sb("cpos", [128, 32], c=c3_)
    cmask = sb("cmask", [128, 2, 8, 64], c=c3_)
    gb = sb("gb", [128, 12], c=c3_)
    d_cw = [load(act, lane("l_cw1"), cw1[:, :, :], inp["cw1"]), load(sp, lane("l_cw2"), cw2[:, :], inp["cw2"]),
            load(act, lane("l_cpos"), cpos[:, :], inp["cpos"])]
    d_cm = load(act, lane("l_cm"), cmask[:, :, :, :], inp["cmask"])
    d_gb = load(sp, lane("l_gb"), gb[:, :], inp["gb"].partition_broadcast(128))
    qr = [sb(f"qr{i}", [128, T], c=c3_) for i in range(2)]
    kr = sb("kr", [128, T], c=c3_)
    kx = sb("kx", [128, T], c=c3_)
    hid = sb("hid", [128, 64], c=c3_)
    hb_ = sb("hb_", [128, 1], c=c3_)
    kcC = sb("kcC", [128, 64], c=c3_)
    vcm = sb("vcm", [64, 64], c=c3_)
    g4 = sb("g4", [128, 8, 4, 4], c=c3_)
    rs = sb("rs", [128, 2, 8, 4, 4], c=c3_)
    mx = sb("mx", [128, 2, 8, 4, 4], c=c3_)
    Pr = Ring([sb(f"Pr{i}", [128, T], c=c3_) for i in range(3)])
    PTr = Ring([sb(f"PT{i}", [128, 8, 128], c=c3_) for i in range(2)])
    o3 = Ring([sb(f"o3{i}", [128, 4, 4, 64], c=c3_) for i in range(2)])
    ot = Ring([sb(f"ot{i}", [128, 512], c=c3_) for i in range(2)])
    osq = sb("osq", [128, 512], c=c3_)
    oss = Ring([sb(f"oss{i}", [128, 8], c=c3_) for i in range(2)])

    bA, fA, iA = banks.take()
    bB, fB, iB = banks.take()
    for lo, b, f in ((0, bA, fA), (64, bB, fB)):
        hs = slice(lo, lo + 64)
        for j in range(32):
            mm(b[hs, 0:63], cw1[hs, j, :], kvc[hs, j:j + 16 * 62 + 1:16], j == 0, j == 31, d_tl[5], d_cw[0], f)
        for j in range(32):
            t = mm(b[hs, 64:65], cw1[hs, j, :], cpos[hs, j:j + 1], j == 0, j == 31, d_cw[2])
        if lo == 0:
            tA = t
    x = cp(act, hb_[0:64, :], bA[0:64, 64:65], tA)
    y = cp(act, hb_[64:128, :], bB[64:128, 64:65], t)
    x = af(hid[0:64, 0:63], bA[0:64, 0:63], ACT.Silu, x, bias=hb_[0:64, 0:1])
    y = af(hid[64:128, 0:63], bB[64:128, 0:63], ACT.Silu, y, bias=hb_[64:128, 0:1])
    banks.give(iA, x)
    banks.give(iB, y)
    b, f, bi = banks.take()
    t = mm(b[:, 0:63], cw2[0:64, :], hid[0:64, 0:63], True, True, x, d_cw[1], f)
    d_kc = cp(act, kcC[:, 0:63], b[:, 0:63], t)
    banks.give(bi, d_kc)
    b, f, bi = banks.take()
    t = mm(b[0:63, 0:64], hid[64:128, 0:63], cw2[64:128, 0:64], True, True, y, f)
    d_vc = cp(act, vcm[0:63, :], b[0:63, 0:64], t)
    banks.give(bi, d_vc)
    d_gate = []
    for c in range(4):
        x = af(gates[c][:, :], gates[c][:, :], ACT.Silu, d_tl[6 + c])
        d_gate.append(ts(pool, gates[c][:, :], gates[c][:, :], P("nsag", c), None, ALU.mult, None, x))
    z = ms(dve, g4[:, :, :, :], 1.0)
    zr = ms(dve, rs[:, :, :, :, :], 0.0)
    x = tt(dve, vtok[:, :, 128:140], vtok[:, :, 128:140], gb[:, :].unsqueeze(1).to_broadcast([128, 8, 12]), ALU.add, d_gb)
    d_g4 = af(g4[:, :, :, 0:3], vtok[:, :, 128:140].rearrange("p j (h b) -> p j h b", h=4), ACT.Sigmoid, x, z)
    d_q = [ts(dve, a[:, :], a[:, :], 0.125, None, ALU.mult, None, d_tl[n]) for n, a in enumerate((q0, q1, m0_, m1_))]
    d_qr = []
    for n, (src, dst, dd) in enumerate(((q0, qr[0], d_q[0]), (q1, qr[1], d_q[1]), (ksw, kr, d_tl[4]))):
        a = tt(pool, dst[:, :], src[:, :], rope[:, 0, :], ALU.mult, dd, d_rope)
        for h in range(2):
            hn = slice(h * 512, (h + 1) * 512)
            b, f, bi = banks.take()
            t = mm(b[:, :], C("perm"), src[:, hn], True, True, dd, f)
            pb_, pf_, pi_ = Pr.take()
            t = tt(dve, pb_[:, 0:512], b[:, :], rope[:, 1, hn], ALU.mult, t, d_rope, pf_)
            banks.give(bi, t)
            t = tt(dve, dst[:, hn], dst[:, hn], pb_[:, 0:512], ALU.add, t, a)
            Pr.give(pi_, t)
        d_qr.append(t)
    d_kx = [load(sp, lane("l_kx0"), kx[64:128, :], kr[0:64, :], d_qr[2]),
            load(act, lane("l_kx1"), kx[0:64, :], kr[64:128, :], d_qr[2])]
    def job(br, h, j):
        hs = slice(64 * (h % 2), 64 * (h % 2) + 64)
        js = slice(j * 128, (j + 1) * 128)
        if br == 0:
            return (q0, q1)[h // 2][hs, js], kcC[hs, 0:63], 63, {0: cmask[:, 0, j, 0:63]}, [vcm[0:63, :]], [d_q, d_kc, d_vc, d_cm]
        if br == 3:
            return ((m0_, m1_)[h // 2][hs, js], mk[hs, h // 2, :], 256, {},
                    [mv[:, g, 64 * h:64 * h + 64] for g in range(2)], [d_q, d_mk, d_mv])
        lo = 0 if br == 1 else max(0, j - 4)
        own = (h % 2 == 0) == (br == 1)
        kt = (kr if own else kx)[hs, lo * 128:(j + 1) * 128]
        masks = {j - lo: C("diag")}
        if br == 2 and j >= 4:
            masks[0] = C("far")
        vs = [vtok[:, t_, 64 * (br - 1):64 * br] for t_ in range(lo, j + 1)]
        return qr[h // 2][hs, js], kt, (j + 1 - lo) * 128, masks, vs, [d_qr, d_kx]

    jobs = [(br, h, j) for j in range(8) for h in range(4) for br in (1, 2, 0, 3)]
    st = {}

    def scores(n):
        br, h, j = jobs[n]
        q, k, nk, masks, vs, w = job(br, h, j)
        nb = (nk + 511) // 512
        pb_, pf_, pi_ = Pr.take()
        bk = []
        for u in range(nb):
            b, f, bi = banks.take()
            n0, n1 = u * 512, min(nk, u * 512 + 512)
            mine = [m for m in sorted(masks) if n0 <= m * 128 < n1]
            t = mm(b[:, 0:n1 - n0], q, k[:, n0:n1], True, not mine, w, f)
            for m in mine:
                wd = min(128, n1 - m * 128)
                t = mm(b[:, m * 128 - n0:m * 128 - n0 + wd], ident, masks[m], False, m == mine[-1])
            x = red(mx[:, u, j, h, br:br + 1], b[:, 0:n1 - n0], ALU.max, t, negate=True)
            bk.append((b, bi, n0, n1, x))
        if nb == 2:
            x = tt(dve, mx[:, 0, j, h, br:br + 1], mx[:, 0, j, h, br:br + 1], mx[:, 1, j, h, br:br + 1], ALU.min, x)
        e = []
        for u, (b, bi, n0, n1, _) in enumerate(bk):
            kw = {} if br == 0 else {"accum_out": rs[:, u, j, h, br:br + 1]}
            t = af(pb_[:, n0:n1], b[:, 0:n1 - n0], ACT.Exp, x, pf_, zr, bias=mx[:, 0, j, h, br:br + 1], **kw)
            banks.give(bi, t)
            e.append(t)
        if br == 0:
            t = tt(dve, pb_[:, 0:63], pb_[:, 0:63], cmask[:, 1, j, 0:63], ALU.mult, t)
            st[("rs", j, h)] = red(rs[:, 0, j, h, 0:1], pb_[:, 0:63], ALU.add, t)
        st[n] = (pb_, pi_, nk, vs, t)

    def turns(n):
        pb_, pi_, nk, vs, t0 = st[n]
        pt, ptf, pti = PTr.take()
        last = []
        for u in range((nk + 511) // 512):
            b, f, bi = banks.take()
            m = min(4, (nk - u * 512 + 127) // 128)
            for a in range(m):
                k0 = u * 512 + a * 128
                wd = min(128, nk - k0)
                t = tr(b[0:wd, a * 128:(a + 1) * 128], pb_[:, k0:k0 + wd], ident, t0, f)
            wd = min(128, nk)
            x = cp(ev[(n + u) % 2], pt[0:wd, u * 4:u * 4 + m, :], b[0:wd, 0:m * 128].rearrange("p (a n) -> p a n", a=m), t, ptf)
            banks.give(bi, x)
            last.append(x)
        Pr.give(pi_, t, st.get(("rs", jobs[n][2], jobs[n][1])) if jobs[n][0] == 0 else None)
        st[n] = (pt, pti, nk, vs, last)

    osl = {}

    def values(n):
        br, h, j = jobs[n]
        pt, pti, nk, vs, w = st.pop(n)
        b, f, bi = banks.take()
        wd = min(128, nk)
        for a, v_ in enumerate(vs):
            t = mm(b[:, 0:64], pt[0:wd, a, :], v_, a == 0, a == len(vs) - 1, w, f)
        PTr.give(pti, t)
        if h == 0 and br == 1:
            osl[j] = o3.take()
        o, of, _ = osl[j]
        x = cp(ev[(n + 1) % 2], o[:, h, br, :], b[:, 0:64], t, of)
        banks.give(bi, x)
        osl.setdefault(("d", j), []).append(x)
        if h == 3 and br == 3:
            merge(j)

    def merge(j):
        o, _, oi = osl[j]
        a = tt(dve, rs[:, 0, j, :, :], rs[:, 0, j, :, :], rs[:, 1, j, :, :], ALU.add,
               osl[("d", j)], [st[("rs", j, h)] for h in range(4)])
        a = ts(dve, rs[:, 0, j, :, :], rs[:, 0, j, :, :], 1e-30, None, ALU.max, None, a)
        a = dve.do(lambda e: e.reciprocal(rs[:, 0, j, :, :], rs[:, 0, j, :, :]), a)
        a = tt(dve, rs[:, 0, j, :, :], rs[:, 0, j, :, :], g4[:, j, :, :], ALU.mult, a, d_g4)
        ov = o[:, :, :, :].rearrange("p h b d -> p (h b) d")
        a = tt(dve, ov, ov, rs[:, 0, j, :, :].rearrange("p h b -> p (h b)").unsqueeze(2).to_broadcast([128, 16, 64]),
               ALU.mult, a)
        tk, tf, ti = ot.take()
        t4 = tk[:, 0:256].rearrange("p (h d) -> p h d", h=4)
        x1 = tt(pool, t4, o[:, :, 0, :], o[:, :, 1, :], ALU.add, a, tf)
        x1 = tt(pool, t4, t4, o[:, :, 2, :], ALU.add, x1)
        x2 = cp(pool, tk[:, 256:512].rearrange("p (h d) -> p h d", h=4), o[:, :, 3, :], a, tf)
        o3.give(oi, x1, x2)
        s_, sf, si = oss.take()
        a = af(osq[:, :], tk[:, :], ACT.Square, x1, x2, st.get("osq"))
        a = red(s_[:, :], osq[:, :].rearrange("p (h d) -> p h d", h=8), ALU.add, a, sf)
        st["osq"] = a
        a = rms_scale(s_[:, :], s_[:, :], 64, 1e-6, a)
        t8 = tk[:, :].rearrange("p (h d) -> p h d", h=8)
        a = tt(pool, t8, t8, s_[:, :].unsqueeze(2).to_broadcast([128, 8, 64]), ALU.mult, a)
        oss.give(si, a)
        b, f, bi = banks.take()
        for c in range(4):
            t = tr(b[:, c * 128:(c + 1) * 128], tk[:, c * 128:(c + 1) * 128], ident, a, f)
        ot.give(ti, t)
        for c in range(4):
            js = slice(j * 128, (j + 1) * 128)
            x = tt(dve, yT[:, 4 + c, js], b[:, c * 128:(c + 1) * 128], gates[c][:, js], ALU.mult, t, d_gate)
        banks.give(bi, x)

    for n in range(len(jobs) + 2):
        if n < len(jobs):
            scores(n)
        if 1 <= n <= len(jobs):
            turns(n - 1)
        if n >= 2:
            values(n - 2)
    barrier()
    c3_.close()
    toks.close()

    high = Scope(1)
    xres = sb("xres", [128, 8, D], c=high)
    small = sb("small", [128, 64], c=high)
    junk = sb("junk3", [128, D], c=high)
    h1s = Scope(1)
    h1T = sb("h1T", [128, 8, T], c=h1s)
    c5 = Scope()
    xs_ = Ring([sb(f"xs{i}", [128, D], c=c5) for i in range(3)])
    hs_ = Ring([sb(f"hs{i}", [128, D], c=c5) for i in range(2)])
    l_xs = [lane(f"l_xs{i}") for i in range(3)]
    nfg = sb("nfg", [128, D], c=c5)
    wo = sb("wo", [128, 8, D], c=c5)
    d_nf = load(act, lane("l_nf"), nfg[:, :], inp["nfg"].partition_broadcast(128))
    d_wo = [load(sp if c % 2 else act, lane(f"l_wo{c}"), wo[:, c, :], inp["wo"][c * 128:(c + 1) * 128, :]) for c in range(8)]
    jk = None
    for j in range(8):
        xb, xf, xi = xs_.take()
        dx = load(sp, l_xs[xi], xb[:, :], inp["x"][j * 128:(j + 1) * 128, :], xf)
        for n in range(2):
            ns = slice(n * 512, (n + 1) * 512)
            b, f, bi = banks.take()
            for c in range(8):
                t = mm(b[:, :], yT[:, c, j * 128:(j + 1) * 128], wo[:, c, ns], c == 0, c == 7, d_wo[c], f)
            t = tt(dve, xb[:, ns], xb[:, ns], b[:, :], ALU.add, t, dx)
            banks.give(bi, t)
        a = af(junk[:, :], xb[:, :], ACT.Square, t, jk, accum_out=small[:, j:j + 1])
        a = rms_scale(small[:, j:j + 1], small[:, j:j + 1], D, 1e-6, a)
        a = stt(xres[:, j, :], xb[:, :], small[:, j:j + 1], nfg[:, :], ALU.mult, ALU.mult, a, d_nf)
        xs_.give(xi, a)
        jk = af(junk[:, :], xres[:, j, :], ACT.Square, a, accum_out=small[:, 8 + j:9 + j])
        x = rms_scale(small[:, 8 + j:9 + j], small[:, 8 + j:9 + j], D, 1e-6, jk)
        hb, hf_, hi_ = hs_.take()
        x = ts(pool, hb[:, :], xres[:, j, :], small[:, 8 + j:9 + j], None, ALU.mult, None, x, hf_)
        e_ = transposed(h1T, hb, j * 128, PAR["n1"], x)
        hs_.give(hi_, *e_)
    barrier()
    c5.close()

    c6 = Scope()
    w2r = Ring([sb(f"w2r{i}", [128, 8, 128], c=c6) for i in range(4)])
    l_w2 = [lane(f"l_w2{i}") for i in range(4)]
    rt = sb("rt", [128, 2, T], c=c6)
    rc = sb("rc", [128, NRC], c=c6)
    qb, kb, qs_, ks_ = (sb(n, [128, T], c=c6) for n in ("qb", "kb", "qs_", "ks_"))
    vt = sb("vt", [128, 8, 128], c=c6)
    gt = sb("gt", [128, T], c=c6)
    scT = sb("scT", [128, 8, 128], c=c6)
    kd = sb("kd", [128, 8, 128], c=c6)
    Sr = sb("Sr", [128, 8, 128], c=c6)
    Or = sb("Or", [128, T], c=c6)
    cu = sb("cu", [128, T + 2], c=c6)
    cg = sb("cg", [128, T], c=c6)
    ca = sb("ca", [128, T], c=c6)
    st8 = sb("st8", [128, 8], c=c6)
    d_rt = load(sp, lane("l_rt"), rt[:, :, :], inp["rot"])
    d_rc = load(act, lane("l_rc"), rc[:, :], inp["rc"])
    z2 = ms(dve, cu[:, 0:2], 0.0)
    l_sw = [lane(f"l_sw{i}") for i in range(4)]

    def project(g):
        w, f, wi = w2r.take()
        dw = load(sp, l_w2[wi], w[:, :, :], inp["w2"][g], f)
        res = []
        for n in range(2):
            b, f, bi = banks.take()
            for c in range(8):
                t = mm(b[:, :], w[:, c, :], h1T[:, c, n * 512:(n + 1) * 512], c == 0, c == 7, dw, f)
            res.append((b, bi, t, slice(n * 512, (n + 1) * 512)))
        w2r.give(wi, t)
        return res

    def to(res, q, dst, *w):
        ends = []
        for b, bi, t, ns in res:
            x = cp(q, dst[:, ns], b[:, :], t, w)
            banks.give(bi, x)
            ends.append(x)
        return ends

    fr = None
    cfr = None
    for h in range(4):
        d_qb = to(project(4 * h), act, qb, fr)
        d_kb = to(project(4 * h + 1), act, kb, fr)
        sw = [load(act, l_sw[0], qs_[0:64, :], qb[64:128, :], d_qb, fr), load(act, l_sw[1], qs_[64:128, :], qb[0:64, :], d_qb),
              load(act, l_sw[2], ks_[0:64, :], kb[64:128, :], d_kb), load(act, l_sw[3], ks_[64:128, :], kb[0:64, :], d_kb)]
        w, f, wi = w2r.take()
        dw = load(sp, l_w2[wi], w[:, :, :], inp["w2"][4 * h + 2], f)
        for hf in range(2):
            b, f, bi = banks.take()
            for jj in range(4):
                j = 4 * hf + jj
                for c in range(8):
                    t = mm(b[:, jj * 128:(jj + 1) * 128], h1T[:, c, j * 128:(j + 1) * 128], w[:, c, :], c == 0, c == 7, dw, f)
            x = cp(act, vt[:, 4 * hf:4 * hf + 4, :], b[:, :].rearrange("p (a n) -> p a n", a=4), t, fr)
            banks.give(bi, x)
        w2r.give(wi, t)
        d_v = x
        d_gt = []
        for b, bi, t, ns in project(4 * h + 3):
            x = af(gt[:, ns], b[:, :], ACT.Silu, t, fr)
            banks.give(bi, x)
            d_gt.append(x)
        a = tt(pool, qb[:, :], qb[:, :], rt[:, 0, :], ALU.mult, d_rt, sw)
        x = tt(dve, qs_[:, :], qs_[:, :], rt[:, 1, :], ALU.mult, d_rt, sw)
        d_qq = tt(dve, qb[:, :], qb[:, :], qs_[:, :], ALU.add, a, x)
        a = tt(pool, kb[:, :], kb[:, :], rt[:, 0, :], ALU.mult, sw)
        x = tt(dve, ks_[:, :], ks_[:, :], rt[:, 1, :], ALU.mult, sw)
        d_kq = tt(dve, kb[:, :], kb[:, :], ks_[:, :], ALU.add, a, x)
        c8 = lambda v_: v_.rearrange("p (a n) -> p a n", a=8)
        qdec = rc[:, RC_QD + 128 * h:RC_QD + 128 * h + 128].unsqueeze(1).to_broadcast([128, 8, 128])
        d_qd = tt(pool, c8(qs_[:, :]), c8(qb[:, :]), qdec, ALU.mult, d_qq)
        x = to(project(16 + 3 * h), act, cg, cfr)
        d_u = to(project(17 + 3 * h), act, ca, cfr)
        for b, bi, t, ns in project(18 + 3 * h):
            y = tt(dve, cu[:, 2 + ns.start:2 + ns.stop], ca[:, ns], b[:, :], ALU.mult, t, d_u, z2, cfr)
            banks.give(bi, y)
        y = ts(dve, ca[:, :], cu[:, 2:T + 2], P("cw", 8 + h), None, ALU.mult, None, y)
        y = stt(ca[:, :], cu[:, 1:T + 1], P("cw", 4 + h), ca[:, :], ALU.mult, ALU.add, y)
        y = stt(ca[:, :], cu[:, 0:T], P("cw", h), ca[:, :], ALU.mult, ALU.add, y)
        cfr = tt(pool, yT[:, 4 + h, :], ca[:, :], cg[:, :], ALU.mult, x, y)
        dk = []
        dsc = []
        for hf in range(2):
            b, f, bi = banks.take()
            for jj in range(4):
                ns = slice((4 * hf + jj) * 128, (4 * hf + jj + 1) * 128)
                t = mm(b[:, jj * 128:(jj + 1) * 128], kb[:, ns], qb[:, ns], True, True, d_qq, d_kq, f)
            dec = rc[:, RC_DM + 128 * h:RC_DM + 128 * h + 128].unsqueeze(1).to_broadcast([128, 4, 128])
            x = tt(dve, scT[:, 4 * hf:4 * hf + 4, :], b[:, :].rearrange("p (a n) -> p a n", a=4), dec, ALU.mult, t, d_rc, fr)
            banks.give(bi, x)
            dsc.append(x)
            b, f, bi = banks.take()
            for jj in range(4):
                ns = slice((4 * hf + jj) * 128, (4 * hf + jj + 1) * 128)
                t = tr(b[:, jj * 128:(jj + 1) * 128], kb[:, ns], ident, d_kq, f)
            x = ts(dve, kd[:, 4 * hf:4 * hf + 4, :], b[:, :].rearrange("p (a n) -> p a n", a=4),
                   rc[:, RC_KD + h:RC_KD + h + 1], None, ALU.mult, None, t, d_rc, fr)
            banks.give(bi, x)
            dk.append(x)
        cd = float(np.exp(retention_log(h) * np.float32(128)))
        ds = ms(dve, Sr[:, 0, :], 0.0, fr)
        dS = [ds]
        for hf in range(2):
            b, f, bi = banks.take()
            m = 4 if hf == 0 else 3
            for jj in range(m):
                n = 4 * hf + jj
                t = mm(b[:, jj * 128:(jj + 1) * 128], kd[:, n, :], vt[:, n, :], True, True, dk[hf], d_v, f)
            for jj in range(m):
                n = 4 * hf + jj
                ds = stt(Sr[:, n + 1, :], Sr[:, n, :], cd, b[:, jj * 128:(jj + 1) * 128], ALU.mult, ALU.add, t, ds)
                dS.append(ds)
            banks.give(bi, ds)
        ends = []
        for hf in range(2):
            b, f, bi = banks.take()
            for jj in range(4):
                n = 4 * hf + jj
                o = b[:, jj * 128:(jj + 1) * 128]
                mm(o, vt[:, n, :], scT[:, n, :], True, False, dsc[hf], d_v, f)
                t = mm(o, Sr[:, n, :], qs_[:, n * 128:(n + 1) * 128], False, True, dS[n], d_qd)
            x = cp(act, Or[:, hf * 512:(hf + 1) * 512], b[:, :], t, fr)
            banks.give(bi, x)
            ends.append(x)
        x = group_norm(Or[:, :], kb[:, :], C("on128"), 1, 1e-6, st8, ends, dk)
        fr = [stt(yT[:, h, :], Or[:, :], P("gn", h), gt[:, :], ALU.mult, ALU.mult, x, d_gt), t]
    barrier()
    c6.close()
    h1s.close()

    c7 = Scope(1)
    con2 = sb("con2", [128, NC2], c=c7)
    LG = sb("LG", [128, 8, 72], c=c7)
    c8_ = Scope()
    wo2 = sb("wo2", [128, 8, D], c=c8_)
    n2b = sb("n2b", [128, D], c=c8_)
    rw = sb("rw", [128, 8, 72], c=c8_)
    rb_ = sb("rb_", [128, 72], c=c8_)
    h2 = Ring([sb(f"h2{i}", [128, D], c=c8_) for i in range(3)])
    h2T = Ring([sb(f"h2T{i}", [128, 8, 128], c=c8_) for i in range(2)])
    l_h2 = [lane(f"l_h2{i}") for i in range(3)]
    h2d = nc.dram_tensor("h2d", [2 * T, 512], F32).ap()
    yb = nc.dram_tensor("yb", [4 * T, 512], F32).ap()
    d_c2 = load(sp, lane("l_c2"), con2[:, :], inp["con2"])
    d_wo2 = [load(sp if c % 2 else act, lane(f"l_wo2{c}"), wo2[:, c, :], inp["wo2"][c * 128:(c + 1) * 128, :]) for c in range(8)]
    d_n2 = load(act, lane("l_n2"), n2b[:, :], inp["n2"].partition_broadcast(128))
    d_rw = load(sp, lane("l_rw"), rw[:, :, :], inp["rw"])
    d_rb = load(act, lane("l_rb"), rb_[:, :], inp["rb"].partition_broadcast(128))
    jk = None
    d_h2 = []
    for j in range(8):
        for n in range(2):
            ns = slice(n * 512, (n + 1) * 512)
            b, f, bi = banks.take()
            for c in range(8):
                t = mm(b[:, :], yT[:, c, j * 128:(j + 1) * 128], wo2[:, c, ns], c == 0, c == 7, d_wo2[c], f)
            t = tt(dve, xres[:, j, ns], xres[:, j, ns], b[:, :], ALU.add, t)
            banks.give(bi, t)
        jk = af(junk[:, :], xres[:, j, :], ACT.Square, t, jk, accum_out=small[:, 16 + j:17 + j])
        a = rms_scale(small[:, 16 + j:17 + j], small[:, 16 + j:17 + j], D, 1e-6, jk)
        hb, hf_, hi_ = h2.take()
        a = stt(hb[:, :], xres[:, j, :], small[:, 16 + j:17 + j], n2b[:, :], ALU.mult, ALU.mult, a, d_n2, hf_)
        x = load(sp, l_h2[hi_], h2d[j * 256:(j + 1) * 256, :].rearrange("(p a) n -> p (a n)", a=2), hb[:, :], a)
        d_h2.append(x)
        tb, tf, ti = h2T.take()
        e_ = []
        for half in range(2):
            b, f, bi = banks.take()
            for c in range(4):
                k_ = 4 * half + c
                t = tr(b[:, c * 128:(c + 1) * 128], hb[:, k_ * 128:(k_ + 1) * 128], ident, a, f)
            y = cp(act, tb[:, 4 * half:4 * half + 4, :], b[:, :].rearrange("p (c n) -> p c n", c=4), t, tf)
            banks.give(bi, y)
            e_.append(y)
        h2.give(hi_, x, t)
        b, f, bi = banks.take()
        for c in range(8):
            t = mm(b[:, 0:72], tb[:, c, :], rw[:, c, :], c == 0, c == 7, e_, d_rw, f)
        h2T.give(ti, t)
        d_lg = tt(dve, LG[:, j, :], b[:, 0:72], rb_[:, :], ALU.add, t, d_rb)
        banks.give(bi, d_lg)
    sp.add(None, d_h2, Done(sp.sem), 1)
    barrier()
    c8_.close()
    mid.close()

    c9 = Scope()
    gix = sb("gix", [128, NBLK], I32, c=c9)
    six = sb("six", [128, NBLK], I32, c=c9)
    gat = sb("gat", [128, NBLK], c=c9)
    eid = sb("eid", [128, 1], I32, c=c9)
    nov_i = sb("nov_i", [128, 1], I32, c=c9)
    c10 = Scope()

    def K2(name, n=None):
        return con2[:, CN2[name][0]:CN2[name][0] + (n or CN2[name][1])]

    g8 = sb("g8", [128, 8, 8], c=c10)
    g8i = sb("g8i", [128, 8, 8], U32, c=c10)
    gi_ = sb("gi_", [128, 8], c=c10)
    oh8 = sb("oh8", [128, 8, 8], c=c10)
    eg = sb("eg", [128, 8, 8], c=c10)
    pg = sb("pg", [128, 8], c=c10)
    Em = sb("Em", [128, 8, 64], c=c10)
    l8 = sb("l8", [128, 8, 8], c=c10)
    l8i = sb("l8i", [128, 8, 8], U32, c=c10)
    ee = sb("ee", [128, 2, 8], c=c10)
    gk = sb("gk", [128, 2, 8], c=c10)
    OH = sb("OH", [128, 2, 8, 64], c=c10)
    Ah = sb("Ah", [128, 8, 64], c=c10)
    tmp = sb("tmp", [128, 8, 64], c=c10)
    rk_ = sb("rk_", [128, 2, 8], c=c10)
    rki = sb("rki", [128, 2, 8], I32, c=c10)
    qf = sb("qf", [128, 2, 8], c=c10)
    mf_ = sb("mf_", [128, 2, 8], c=c10)
    cnt = sb("cnt", [128, 64], c=c10)
    cnti = sb("cnti", [128, 64], I32, c=c10)
    nov = sb("nov", [128, 64], c=c10)
    ove = sb("ove", [128, 64], c=c10)
    ovb = sb("ovb", [128, 64], c=c10)
    ovk = sb("ovk", [128, 2, 8], c=c10)
    blk_ = sb("blk_", [128, 2, 8], c=c10)
    eif = sb("eif", [128, 64], c=c10)
    vals = Ring([sb(f"vals{i}", [128, 3, NBLK], c=c10) for i in range(4)])
    ohm = Ring([sb(f"ohm{i}", [128, 128], c=c10) for i in range(4)])
    tbs = sb("tbs", [128, 3, NBLK], c=c10)
    a = d_c2
    for j in range(8):
        x = dve.do(lambda e, j=j: e.max(g8[:, j, :], LG[:, j, 0:8]), a)
        a = dve.do(lambda e, j=j: e.max_index(g8i[:, j, :], g8[:, j, :], LG[:, j, 0:8]), x)
    a = cp(dve, gi_[:, :], g8i[:, :, 0:1].rearrange("p a b -> p (a b)"), a)
    a = tt(dve, oh8[:, :, :], K2("i64", 8).unsqueeze(1).to_broadcast([128, 8, 8]),
           gi_[:, :].unsqueeze(2).to_broadcast([128, 8, 8]), ALU.is_equal, a)
    x = tt(dve, eg[:, :, :], LG[:, :, 0:8], g8[:, :, 0:1].to_broadcast([128, 8, 8]), ALU.subtract, a)
    x = af(eg[:, :, :], eg[:, :, :], ACT.Exp, x)
    x = red(pg[:, :], eg[:, :, :], ALU.add, x)
    d_pg = dve.do(lambda e: e.reciprocal(pg[:, :], pg[:, :]), x)
    a = ts(dve, oh8[:, :, :], oh8[:, :, :], -1.0, BIG, ALU.add, ALU.mult, a)
    E4_ = Em[:, :, :].rearrange("p j (g e) -> p j g e", g=8)
    a = tt(dve, E4_, LG[:, :, 8:72].rearrange("p j (g e) -> p j g e", g=8),
           oh8[:, :, :].unsqueeze(3).to_broadcast([128, 8, 8, 8]), ALU.add, a)
    for j in range(8):
        x = dve.do(lambda e, j=j: e.max(l8[:, j, :], Em[:, j, :]), a)
        a = dve.do(lambda e, j=j: e.max_index(l8i[:, j, :], l8[:, j, :], Em[:, j, :]), x)
    for k_ in range(2):
        d_ee = cp(dve, ee[:, k_, :], l8i[:, :, k_:k_ + 1].rearrange("p a b -> p (a b)"), a)
    l1, l2 = (l8[:, :, k_:k_ + 1].rearrange("p a b -> p (a b)") for k_ in range(2))
    x = tt(dve, gk[:, 1, :], l2, l1, ALU.subtract, x)
    x = af(gk[:, 1, :], gk[:, 1, :], ACT.Exp, x)
    y = ts(dve, gk[:, 0, :], gk[:, 1, :], 1.0, None, ALU.add, None, x)
    y = dve.do(lambda e: e.reciprocal(gk[:, 0, :], gk[:, 0, :]), y)
    y = tt(dve, gk[:, 0, :], gk[:, 0, :], pg[:, :], ALU.mult, y, d_pg)
    d_gk = tt(dve, gk[:, 1, :], gk[:, 1, :], gk[:, 0, :], ALU.mult, y)
    for k_ in range(2):
        x = tt(dve, OH[:, k_, :, :], K2("i64").unsqueeze(1).to_broadcast([128, 8, 64]),
               ee[:, k_, :].unsqueeze(2).to_broadcast([128, 8, 64]), ALU.is_equal, d_ee)
    d_oh = x
    d_A = tt(dve, Ah[:, :, :], OH[:, 0, :, :], OH[:, 1, :, :], ALU.add, d_oh)
    br_, fr_, ir_ = banks.take()
    bc_, fc_, ic_ = banks.take()
    for j in range(8):
        for i in range(j):
            mm(br_[:, j * 64:j * 64 + 64], C("ones"), Ah[:, i, :], i == 0, False, d_A, fr_)
        t = mm(br_[:, j * 64:j * 64 + 64], K2("tri"), Ah[:, j, :], j == 0, True, d_A, fr_)
    for j in range(8):
        t2 = mm(bc_[:, 0:64], C("ones"), Ah[:, j, :], j == 0, j == 7, fc_)
    rank = br_[:, :].rearrange("p (j e) -> p j e", j=8)
    x = ts(dve, cnt[:, :], bc_[:, 0:64], -1.0, None, ALU.add, None, t2)
    banks.give(ic_, x)
    x = cp(dve, cnti[:, :], cnt[:, :], x)
    x = ts(dve, cnti[:, :], cnti[:, :], 6, None, ALU.arith_shift_right, None, x)
    x = cp(dve, nov[:, :], cnti[:, :], x)
    x = ts(dve, nov[:, :], nov[:, :], 0.0, None, ALU.max, None, x)
    x = dve.do(lambda e: e.tensor_tensor_scan(ove[:, :], C("ones", 0, 64), nov[:, :], 0.0, ALU.mult, ALU.add), x)
    d_ove = x
    d_ovb = tt(dve, ovb[:, :], ove[:, :], nov[:, :], ALU.subtract, x)
    d_nov = cp(dve, nov_i[:, :], ove[:, 63:64], d_ove)
    x = ts(dve, eif[:, :], ove[:, :], K2("ip"), None, ALU.is_le, None, d_ove)
    x = red(eif[:, 0:1], eif[:, :], ALU.add, x)
    x = ts(dve, eif[:, 0:1], eif[:, 0:1], 63.0, None, ALU.min, None, x)
    d_eid = cp(dve, eid[:, :], eif[:, 0:1], x)
    a = d_oh
    for k_ in range(2):
        x = tt(dve, tmp[:, :, :], OH[:, k_, :, :], rank, ALU.mult, t, a)
        x = red(rk_[:, k_, :], tmp[:, :, :], ALU.add, x)
        x = tt(dve, tmp[:, :, :], OH[:, k_, :, :], ovb[:, :].unsqueeze(1).to_broadcast([128, 8, 64]), ALU.mult, x, d_ovb)
        a = red(ovk[:, k_, :], tmp[:, :, :], ALU.add, x)
    banks.give(ir_, a)
    x = cp(dve, rki[:, :, :], rk_[:, :, :], a)
    x = ts(dve, rki[:, :, :], rki[:, :, :], 6, None, ALU.arith_shift_right, None, x)
    x = cp(dve, qf[:, :, :], rki[:, :, :], x)
    d_m = stt(mf_[:, :, :], qf[:, :, :], -64.0, rk_[:, :, :], ALU.mult, ALU.add, x)
    x = tt(dve, ovk[:, :, :], ovk[:, :, :], qf[:, :, :], ALU.add, d_m)
    x = ts(dve, ovk[:, :, :], ovk[:, :, :], 63.0, None, ALU.add, None, x)
    x = tt(dve, ovk[:, :, :], ovk[:, :, :], ee[:, :, :], ALU.subtract, x)
    x = ts(dve, qf[:, :, :], qf[:, :, :], 0.0, None, ALU.is_gt, None, x)
    x = tt(dve, ovk[:, :, :], ovk[:, :, :], qf[:, :, :], ALU.mult, x)
    d_bl = tt(dve, blk_[:, :, :], ovk[:, :, :], ee[:, :, :], ALU.add, x)
    bt, ft, it = banks.take()
    for k_ in range(2):
        for j in range(8):
            va, vf, vi = vals.take()
            oa, of_, oi_ = ohm.take()
            bcol = blk_[:, k_, j:j + 1]
            srcs = [K2("tok")[:, j:j + 1], K2("dst")[:, 8 * k_ + j:8 * k_ + j + 1], gk[:, k_, j:j + 1]]
            for n, sc_ in enumerate(srcs):
                x = ts(dve, va[:, n, :], K2("i96"), bcol, sc_, ALU.is_equal, ALU.mult, d_bl, d_gk, vf)
            y = ts(dve, oa[:, :], K2("im"), mf_[:, k_, j:j + 1], None, ALU.is_equal, None, d_m, of_)
            t = mm(bt[:, 0:3 * NBLK], oa[:, :], va[:, :, :].rearrange("p a n -> p (a n)"),
                   k_ == 0 and j == 0, k_ == 1 and j == 7, x, y, ft)
            vals.give(vi, t)
            ohm.give(oi_, t)
    x = cp(dve, tbs[:, :, :], bt[:, 0:3 * NBLK].rearrange("p (a n) -> p a n", a=3), t)
    banks.give(it, x)
    d_ix = [ts(dve, o_[:, :], tbs[:, n, :], 2.0, K2("half"), ALU.mult, ALU.add, x) for n, o_ in ((0, gix), (1, six))]
    d_ga = cp(dve, gat[:, :], tbs[:, 2, :], x)
    barrier()
    c10.close()
    c7.close()

    c11 = Scope()
    NCH = 7
    wch = Ring([sb(f"wch{i}", [128, 4096], c=c11) for i in range(NCH)])
    l_ch = [lane(f"l_ch{i}") for i in range(NCH)]
    xg = Ring([sb(f"xg{i}", [128, 512], c=c11) for i in range(3)])
    l_xg = [lane(f"l_xg{i}") for i in range(3)]
    xT = Ring([sb(f"xT{i}", [128, 4, 128], c=c11) for i in range(2)])
    Gs = Ring([sb(f"Gs{i}", [128, 512], c=c11) for i in range(2)])
    sg_ = Ring([sb(f"sg{i}", [128, 4, 64], c=c11) for i in range(2)])
    ys = Ring([sb(f"ys{i}", [128, 512], c=c11) for i in range(2)])
    l_ys = [lane(f"l_ys{i}") for i in range(2)]
    zx = [ms(pool, xg.bufs[i][:, :], 0.0) for i in range(3)]

    def gather(q, ln, dst, col, *w):
        return q.dma(ln, lambda e: e.indirect_dma_start(
            dst[:, :], None, h2d, bass.IndirectOffsetOnAxis(ap=gix[:, col:col + 1].bitcast(U32), axis=0),
            bounds_check=2 * T - 1, oob_is_err=False), *w)

    def scatter(q, ln, src, col, *w):
        return q.dma(ln, lambda e: e.indirect_dma_start(
            yb, bass.IndirectOffsetOnAxis(ap=six[:, col:col + 1].bitcast(U32), axis=0), src[:, :], None,
            bounds_check=4 * T - 1, oob_is_err=False), *w)

    def weights(e):
        res = []
        for name in ("wg", "wu", "wd"):
            w, f, wi = wch.take()
            if name == "wd":
                src = inp[name][e].rearrange("(p c) n -> p (c n)", c=4)
                dst = w
            else:
                src = inp[name][e].rearrange("(h p q) n -> p h (q n)", h=2, q=4)
                dst = w.rearrange("p (h n) -> p h n", h=2)
            res.append((w, wi, load(sp, l_ch[wi], dst, src, f)))
        return res

    def turn_x(qs, x, dst, *w):
        pe_, ev_, bk = qs
        b, f, bi = bk.take()
        for q in range(4):
            t = pe_.do(lambda e, q=q: e.transpose(b[:, q * 128:(q + 1) * 128], x[:, q:512:4], ident), w, f)
        y = cp(ev_, dst[:, :, :], b[:, :].rearrange("p (a n) -> p a n", a=4), t)
        bk.give(bi, y)
        return t, y

    def hidden(qs, w, xt_, *wt):
        pe_, _, bk = qs
        b, f, bi = bk.take()
        for i in range(8):
            h, q = i // 4, i % 4
            o = b[64 * (i % 2):64 * (i % 2) + 64, :]
            t = pe_.do(lambda e, o=o, h=h, q=q, i=i: e.matmul(
                o, xt_[:, q, 64 * h:64 * h + 64], w[:, (4 * h + q) * 512:(4 * h + q + 1) * 512], start=i < 2, stop=i > 5), wt, f)
        return b, bi, t

    def turn_h(pe_, b, off, gs, *w):
        for c in range(4):
            t = pe_.do(lambda e, c=c: e.matmul(b[:, off + c * 64:off + c * 64 + 64], gs[:, c:512:4], C("id2", 0, 64),
                                               start=True, stop=True), *w)
        return t

    def down(pe_, b, w, hT_, *wt):
        for c in range(4):
            for n in range(2):
                t = pe_.do(lambda e, c=c, n=n: e.matmul(b[64 * n:64 * n + 64, :], hT_[:, c, :],
                                                        w[:, c * 1024 + n * 512:c * 1024 + n * 512 + 512],
                                                        start=c == 0, stop=c == 3), *wt)
        return t

    W, X, XT, HT, last_sc = {}, {}, {}, {}, []

    def fetch(e):
        x, f, xi = xg.take()
        X[e] = (x, xi, gather(pool, l_xg[xi], x, e, f, zx))

    def prepare(e):
        x, xi, dx = X.pop(e)
        o, f, oi = xT.take()
        t, y = turn_x((pe, act, banks), x, o, dx, f)
        xg.give(xi, t)
        XT[e] = (o, oi, y)

    def finish_expert(e):
        h_, hi_, dh = HT.pop(e)
        w, wi, dw = W[e][2]
        b, f, bi = banks.take()
        t = down(pe, b, w, h_, dh, dw, f)
        wch.give(wi, t)
        sg_.give(hi_, t)
        y, f, yi = ys.take()
        x = ts(dve, y[:, :], b[:, :], gat[:, e:e + 1], None, ALU.mult, None, t, f)
        banks.give(bi, x)
        d = scatter(pool, l_ys[yi], y, e, x)
        ys.give(yi, d)
        last_sc.append(d)

    W[0] = weights(0)
    fetch(0)
    fetch(1)
    prepare(0)
    for e in range(NEXP):
        if e + 1 < NEXP:
            W[e + 1] = weights(e + 1)
        if e + 2 < NEXP:
            fetch(e + 2)
        xt_, xi, dx = XT.pop(e)
        (wg_, gi1, dg), (wu_, ui1, du), _ = W[e]
        bg, ig, tg = hidden((pe, None, banks), wg_, xt_, dx, dg)
        wch.give(gi1, tg)
        bu, iu, tu = hidden((pe, None, banks), wu_, xt_, du)
        wch.give(ui1, tu)
        xT.give(xi, tu)
        g1, f1, i1 = Gs.take()
        yg = cp(act, g1[:, :], bg[:, :], tg, f1)
        banks.give(ig, yg)
        u1, f2, i2 = Gs.take()
        yu = cp(dve, u1[:, :], bu[:, :], tu, f2)
        banks.give(iu, yu)
        if e + 1 < NEXP:
            prepare(e + 1)
        if e > 0:
            finish_expert(e - 1)
        b, f, bi = banks.take()
        t1 = turn_h(pe, b, 0, g1, yg, f)
        t2 = turn_h(pe, b, 256, u1, yu)
        Gs.give(i1, t1)
        Gs.give(i2, t2)
        s1, f3, i3 = sg_.take()
        b4 = b[:, :].rearrange("p (a n) -> p a n", a=8)
        x = af(s1[:, :, :], b4[:, 0:4, :], ACT.Silu, t2, f3)
        x = tt(dve, s1[:, :, :], s1[:, :, :], b4[:, 4:8, :], ALU.mult, x, t2)
        banks.give(bi, x)
        HT[e] = (s1, i3, x)
    finish_expert(NEXP - 1)
    pool.add(None, last_sc, Done(pool.sem), 1)
    barrier()

    oq = {n: Queue(sem(f"o_{n}")) for n in ("pe", "act", "dve", "pool", "sp")}
    ol = {n: lane(f"o_l{n}") for n in ("g", "u", "d", "x", "y")}
    wts = [wch.bufs[i] for i in range(3)]
    ox, oxT, og, ou = xg.bufs[0], xT.bufs[0], Gs.bufs[0], Gs.bufs[1]
    osg, oy = sg_.bufs[0], ys.bufs[0]
    regs = {}
    before = [None]

    def further(n):
        col = NEXP + n
        q = oq if n == 0 else {k_: Queue(oq[k_].sem) for k_ in oq}
        last = before[0]

        def wload(nm, ln, dst, view):
            def fn(e):
                v = e.value_load(eid[n:n + 1, 0:1], min_val=0, max_val=NEXP - 1)
                return e.dma_start(dst, view(inp[nm][bass.ds(v, 1)]))
            return q["sp"].dma(ol[ln], fn, last)

        dws = [wload(nm, ln, wts[k_].rearrange("p (h n) -> p h n", h=2),
                     lambda v: v.rearrange("a (h p q) n -> p (a h) (q n)", h=2, q=4))
               for k_, (nm, ln) in enumerate((("wg", "g"), ("wu", "u")))]
        dws.append(wload("wd", "d", wts[2], lambda v: v.rearrange("a (p c) n -> p (a c n)", c=4)))
        dx = gather(q["pool"], ol["x"], ox, col, last)
        bk = Ring([banks.bufs[i] for i in range(8)])
        t, y = turn_x((q["pe"], q["dve"], bk), ox, oxT, dx)
        bg, _, tg = hidden((q["pe"], None, bk), wts[0], oxT, y, dws[0])
        bu, _, tu = hidden((q["pe"], None, bk), wts[1], oxT, dws[1])
        yg = cp(q["dve"], og[:, :], bg[:, :], tg)
        yu = cp(q["dve"], ou[:, :], bu[:, :], tu)
        b, _, _ = bk.take()
        t1 = turn_h(q["pe"], b, 0, og, yg)
        t2 = turn_h(q["pe"], b, 256, ou, yu)
        b4 = b[:, :].rearrange("p (a n) -> p a n", a=8)
        x = q["act"].do(lambda e: e.activation(osg[:, :, :], b4[:, 0:4, :], ACT.Silu), t2)
        x = tt(q["dve"], osg[:, :, :], osg[:, :, :], b4[:, 4:8, :], ALU.mult, x, t2)
        b, _, _ = bk.take()
        t = down(q["pe"], b, wts[2], osg, x, dws[2])
        x = ts(q["dve"], oy[:, :], b[:, :], gat[:, col:col + 1], None, ALU.mult, None, t)
        d = scatter(q["pool"], ol["y"], oy, col, x)
        before[0] = q["pool"].do(lambda e: e.nop(), d)
        return q

    for nm, q in (("pe", pe), ("act", act), ("dve", dve), ("pool", pool), ("sp", sp)):
        def ld(e, nm=nm):
            regs[nm] = e.alloc_register(f"n_{nm}")
            return e.reg_load(regs[nm], nov_i[0:1, 0:1])
        q.do(ld)
    bodies = [further(n) for n in range(NOVER)]
    for nm, q in (("pe", pe), ("act", act), ("dve", dve), ("pool", pool), ("sp", sp)):
        outer = Queue(oq[nm].sem)
        for n in range(NOVER):
            outer.when(lambda e, nm=nm: regs[nm], n, bodies[n][nm])
        q.when(lambda e, nm=nm: regs[nm], 0, outer)
        q.do(lambda e: e.nop())
    barrier()
    c11.close()

    c12 = Scope()
    fnb = sb("fnb", [128, D], c=c12)
    d_fn = load(act, lane("l_fn"), fnb[:, :], inp["fn"].partition_broadcast(128))
    yl = Ring([sb(f"yl{i}", [128, 2 * D], c=c12) for i in range(4)])
    l_yl = [lane(f"l_yl{i}") for i in range(4)]
    for j in range(8):
        y, f, yi = yl.take()
        dy = load(sp, l_yl[yi], y[:, :], yb[j * 512:(j + 1) * 512, :].rearrange("(p a) n -> p (a n)", a=4), f)
        x = tt(pool, y[:, 0:D], y[:, 0:D], y[:, D:2 * D], ALU.add, dy)
        x = tt(dve, y[:, 0:D], y[:, 0:D], xres[:, j, :], ALU.add, x)
        a = af(y[:, D:2 * D], y[:, 0:D], ACT.Square, x, accum_out=small[:, 24 + j:25 + j])
        a = rms_scale(small[:, 24 + j:25 + j], small[:, 24 + j:25 + j], D, 1e-6, a)
        a = stt(y[:, 0:D], y[:, 0:D], small[:, 24 + j:25 + j], fnb[:, :], ALU.mult, ALU.mult, a, d_fn)
        d = load(act, lane(f"l_out{j}"), out[j * 128:(j + 1) * 128, :], y[:, 0:D], a)
        yl.give(yi, d)
        outs.append(d)
    return finish(nc, ctx, (pe, act, dve, pool, sp), outs)


def finish(nc, ctx, queues, outs):
    pe, act, dve, pool, sp = queues
    sp.add(None, outs, Done(sp.sem), 1)
    counts = {}
    for q in queues:
        q.number(counts)
    block = ctx.enter_context(nc.Block())

    @block.tensor
    def _(eng):
        pe.emit(eng)

    @block.scalar
    def _(eng):
        act.emit(eng)

    @block.vector
    def _(eng):
        dve.emit(eng)

    @block.gpsimd
    def _(eng):
        pool.emit(eng)

    @block.sync
    def _(eng):
        sp.emit(eng)

    ctx.close()


def constants():
    p = np.arange(128)
    s, t = p[:, None], p[None, :]
    c = np.zeros((128, NCON), np.float32)

    def put(name, a, at=0):
        a = np.asarray(a, np.float32)
        c[:, CON[name] + at:CON[name] + at + a.shape[1]] = a

    same = s // 64 == t // 64
    put("id", s == t)
    put("sc", (s < t) & same, 0)
    put("sc", (s <= t) & same, 128)
    put("sc", (s < t) & same, 256)
    put("sc", (s <= t) & same, 384)
    m1 = (s % 2 == 1) & (t == s - 1)
    put("m1", m1)
    put("m1t", m1.T)
    for n in range(5):
        m = 2 << n
        put("lv", (s // (2 * m) == t // (2 * m)) & ((s // m) % 2 == 1) & ((t // m) % 2 == 0), n * 128)
    put("blk", same)
    put("blkm", same / 64.0)
    pm = np.zeros((128, 128))
    for h in (0, 64):
        for m in range(8):
            pm[h + m + 8, h + m] = -1.0
            pm[h + m, h + m + 8] = 1.0
    put("perm", pm)
    put("diag", np.where(t > s, -BIG, 0.0))
    put("far", np.where(t <= s, -BIG, 0.0))
    put("ones", np.ones((128, 128)))
    put("on128", np.full((128, 128), 1 / 128.0))
    put("id2", s[:, :1] % 64 == t[:, :64])
    return c


def layout(i):
    w = i["w_in"][0]
    cols = []
    for g in range(16):
        cols.append(np.arange(g * 128, (g + 1) * 128))
    cols.append(np.arange(2048, 2176))
    n0 = 2176
    cols += [np.arange(n0 + k * 128, n0 + (k + 1) * 128) for k in range(4)]
    kc, vc, ks, vs, kw, vw = (np.arange(n0 + 524 + k * 64, n0 + 588 + k * 64) for k in range(6))
    cols.append(np.concatenate([ks, kw]))
    cols.append(np.concatenate([kc, vc]))
    m0 = 2176 + 908
    cols += [np.arange(m0 + k * 128, m0 + (k + 1) * 128) for k in range(4)]
    a = {"x": i["x"][0], "mem": i["mem"][0]}
    a["w1"] = np.stack([w[:, c].reshape(8, 128, 128).transpose(1, 0, 2) for c in cols])
    vcol = np.concatenate([vs, vw, np.arange(n0 + 512, n0 + 524)])
    a["wv"] = np.ascontiguousarray(w[:, vcol].reshape(8, 128, 140).transpose(1, 0, 2))
    a["up"] = np.concatenate([i["rwkv_w_up"][0], i["rwkv_a_up"][0]], axis=0)
    par = [("mu", "rwkv_mu"), ("w0", "rwkv_w0"), ("a0", "rwkv_a0"), ("kk", "rwkv_k_k"), ("ka", "rwkv_k_a"),
           ("rk", "rwkv_r_k"), ("lnw", "rwkv_ln_w"), ("lnb", "rwkv_ln_b"), ("nin", "norm_in_g"),
           ("nmem", "mem_norm_g"), ("nsag", "nsa_out_g"), ("memg", "mem_out_g"), ("gn", "ret_gn_w_2"),
           ("cw", "conv_w_2"), ("n1", "norm1_w_2")]
    a["par"] = np.ascontiguousarray(np.concatenate([i[k].reshape(-1, 128) for _, k in par], axis=0).T)
    a["con"] = constants()
    pos = np.arange(T, dtype=np.float32)
    inv = np.float32(500000.0) ** (-np.arange(8, dtype=np.float32) / np.float32(8))
    ang = pos[None, :] * inv.astype(np.float32)[:, None]
    rope = np.zeros((128, 2, T), np.float32)
    rope[:, 0] = 1.0
    for h in (0, 64):
        for o in (0, 8):
            rope[h + o:h + o + 8, 0] = np.cos(ang)
            rope[h + o:h + o + 8, 1] = np.sin(ang)
    a["rope"] = rope
    w1 = [i[f"nsa_cmp_{n}_w1"][0].reshape(32, 64, 64).transpose(1, 0, 2) for n in "kv"]
    a["cw1"] = np.ascontiguousarray(np.concatenate(w1, axis=0))
    a["cw2"] = np.concatenate([np.concatenate([i[f"nsa_cmp_{n}_w2"][0]] * 2, axis=1) for n in "kv"], axis=0)
    a["cpos"] = np.ascontiguousarray(np.concatenate([i["nsa_cmp_pos"][0].T] * 2, axis=0))
    a["wmem"] = i["w_mem_kv"][0]
    seen = (16 * np.arange(64) + 31)[None, None, :] <= (128 * np.arange(8)[None, :] + np.arange(128)[:, None])[:, :, None]
    a["cmask"] = np.stack([np.where(seen, 0.0, -BIG), seen], axis=1).astype(np.float32)
    a["gb"] = i["nsa_gate_b"][0]
    a["nfg"] = i["norm_final_g"]
    a["wo"] = i["w_out"][0]

    w = i["w_in_2"][0]
    starts = []
    for h in range(4):
        starts += [h * 128 + 512 * k for k in range(4)]
    for h in range(4):
        starts += [2048 + h * 128 + 512 * k for k in range(3)]
    a["w2"] = np.stack([w[:, c:c + 128].reshape(8, 128, 128).transpose(1, 0, 2) for c in starts])
    inv = np.float32(10000.0) ** (-np.arange(64, dtype=np.float32) / np.float32(64))
    ang = pos[None, :] * inv.astype(np.float32)[:, None]
    co, si = np.cos(ang), np.sin(ang)
    a["rot"] = np.ascontiguousarray(np.stack([np.concatenate([co, co]), np.concatenate([-si, si])], axis=1).astype(np.float32))
    rc = np.zeros((128, NRC), np.float32)
    idx = np.arange(128, dtype=np.float32)
    scale = np.float32(128 ** -0.5)
    for h in range(4):
        lg = retention_log(h)
        rel = idx[None, :] - idx[:, None]
        rc[:, RC_DM + 128 * h:RC_DM + 128 * h + 128] = np.where(rel >= 0, np.exp(lg * np.where(rel >= 0, rel, 0)), 0) * scale
        rc[:, RC_QD + 128 * h:RC_QD + 128 * h + 128] = (np.exp(lg * (idx + 1)) * scale)[None, :]
        rc[:, RC_KD + h] = np.exp(lg * (127 - idx))
    a["rc"] = rc
    a["wo2"] = i["w_o_2"][0]
    a["n2"] = i["norm2_w_2"][0]
    re = i["router_e_w_2"][0].transpose(1, 0, 2).reshape(1024, 64)
    rw = np.concatenate([i["router_g_w_2"][0], re], axis=1)
    a["rw"] = np.ascontiguousarray(rw.reshape(8, 128, 72).transpose(1, 0, 2))
    a["rb"] = np.concatenate([i["router_g_b_2"].reshape(-1), i["router_e_b_2"].reshape(-1)])
    a["wg"], a["wu"], a["wd"] = i["w_gate_2"][0], i["w_up_2"][0], i["w_down_2"][0]
    a["fn"] = i["final_norm_w_2"]
    c2 = np.zeros((128, NC2), np.float32)
    p = np.arange(128)[:, None]

    def put(name, v):
        o, k = CN2[name]
        c2[:, o:o + k] = v

    put("i64", np.arange(64)[None, :])
    put("i96", np.arange(NBLK)[None, :])
    put("im", (np.arange(128) % 64)[None, :])
    put("tri", p < np.arange(128)[None, :])
    tok = 128 * np.arange(8)[None, :] + p
    put("tok", tok + 1)
    put("dst", np.concatenate([2 * tok + 1, 2 * tok + 2], axis=1))
    put("half", p // 64 - 2)
    put("ip", p)
    a["con2"] = c2
    return a


def kernel(**inputs):
    import concourse.bacc as bacc
    from concourse.bass_utils import run_bass_kernel_spmd

    arrays = {f"in_{k}": np.ascontiguousarray(v) for k, v in layout({k: np.asarray(v) for k, v in inputs.items()}).items()}
    nc = bacc.Bacc("TRN2", target_bir_lowering=False, num_devices=1)
    inp = {k[3:]: nc.dram_tensor(k, v.shape, mybir.dt.from_np(v.dtype), kind="ExternalInput").ap()
           for k, v in arrays.items()}
    out = nc.dram_tensor("out_x", (T, D), F32, kind="ExternalOutput").ap()
    program(nc, inp, out)
    r = run_bass_kernel_spmd(nc, [arrays], core_ids=[0])
    return r.results[0]["out_x"].reshape(1, T, D)
```

```python
from contextlib import ExitStack

import numpy as np

import concourse.bass as bass
from concourse import mybir

F32 = mybir.dt.float32
I32 = mybir.dt.int32
U32 = mybir.dt.uint32
F32R = mybir.dt.float32r
BF16 = mybir.dt.bfloat16
ALU = mybir.AluOpType
ACT = mybir.ActivationFunctionType
AX = mybir.AxisListType

T = 1024
D = 1024
CAP = 64
NEXP = 64
NOVER = 31
NBLK = NEXP + NOVER
ARENA = 50600
BIG = 1e30

R0, K0, V0, G0, WA, NQ, NG, KSW, KVC, MQ, MG = 0, 4, 8, 12, 16, 17, 19, 21, 22, 23, 25
NGRP = 27

PAR = {}
_at = 0
for _n, _k in (("mu", 17), ("w0", 4), ("a0", 4), ("kk", 4), ("ka", 4), ("rk", 4), ("lnw", 4), ("lnb", 4),
               ("nin", 8), ("nmem", 8), ("nsag", 2), ("memg", 2), ("gn", 4), ("cw", 12), ("n1", 8)):
    PAR[_n] = _at
    _at += _k
NPAR = _at

CON = {}
_at = 0
for _n, _k in (("id", 128), ("sc", 512), ("m1", 128), ("m1t", 128), ("lv", 640), ("blk", 128),
               ("blkm", 128), ("perm", 128), ("diag", 128), ("far", 128), ("ones", 128), ("on128", 128), ("id2", 64)):
    CON[_n] = _at
    _at += _k
NCON = _at


RC_DM, RC_QD, RC_KD, NRC = 0, 512, 1024, 1028
CN2 = {}
_at = 0
for _n, _k in (("i64", 64), ("i96", NBLK), ("im", 128), ("tri", 128), ("tok", 8), ("dst", 16), ("half", 1), ("ip", 1)):
    CN2[_n] = (_at, _k)
    _at += _k
NC2 = _at


def retention_log(h):
    return np.log1p(-(np.float32(2.0) ** (np.float32(-5.0) - np.float32(h)))).astype(np.float32)


class Done:

    def __init__(self, sem, n=None):
        self.sem, self.n, self.used = sem, n, n is not None


def flat(waits):
    out = []
    for w in waits:
        out += flat(w) if isinstance(w, (list, tuple)) else [] if w is None else [w]
    return out


class Queue:

    def __init__(self, sem, raises=True):
        self.sem, self.items = sem, []
        self.last = None

    def add(self, fn, waits, d, step):
        ws = flat(waits)
        for x in ws:
            x.used = True
        self.items.append((fn, ws, d, step))
        self.last = d
        return d

    def do(self, fn, *waits):
        return self.add(fn, waits, Done(self.sem), 1)

    def dma(self, lane, fn, *waits):
        lane[1] += 16
        return self.add(fn, waits, Done(lane[0], lane[1]), 16)

    def when(self, load, limit, body):
        self.items.append((load, limit, body, 0))

    def number(self, counts):
        for fn, ws, d, step in self.items:
            if step == 0:
                d.number(counts)
            elif d.n is None and d.used:
                counts[d.sem.name] = counts.get(d.sem.name, 0) + 1
                d.n = counts[d.sem.name]

    def emit(self, eng, seen=None):
        seen = {} if seen is None else seen
        for fn, ws, d, step in self.items:
            if step == 0:
                with eng.If_cmp(fn(eng), ws, "IS_GT"):
                    d.emit(eng, dict(seen))
                continue
            for w in ws:
                if seen.get(w.sem.name, 0) < w.n:
                    eng.wait_ge(w.sem, w.n)
                    seen[w.sem.name] = w.n
            if fn is None and not d.used:
                continue
            if fn is None:
                eng.nop().then_inc(d.sem, 1)
                continue
            ins = fn(eng)
            if step == 16:
                ins.then_inc(d.sem, 16)
            elif d.used:
                ins.then_inc(d.sem, 1)


class Ring:

    def __init__(self, bufs):
        self.bufs, self.free, self.at = bufs, [[] for _ in bufs], 0

    def take(self):
        i = self.at
        while self.free[i] is None:
            i = (i + 1) % len(self.bufs)
            assert i != self.at, "none is free"
        self.at = (i + 1) % len(self.bufs)
        f, self.free[i] = self.free[i], None
        return self.bufs[i], f, i

    def give(self, i, *ends):
        self.free[i] = list(ends)


def program(nc, inp, out):
    ctx = ExitStack()

    with nc.sbuf_tensor("arena", [128, ARENA], F32) as arena:
        pass
    edge = [0, ARENA]

    class Scope:

        def __init__(self, side=0):
            self.side, self.mark = side, edge[side]

        def close(self):
            edge[self.side] = self.mark

    low = Scope()

    def rounded(name, at, n):
        with nc.sbuf_tensor(name + "_at", [128, at], F32), nc.sbuf_tensor(name, [128, n], F32R) as r:
            return r

    def sb(name, shape, dt=F32, c=None):
        n = 1
        for k in shape[1:]:
            n *= k
        if dt is BF16:
            n //= 2
        n = (n + 7) // 8 * 8
        side = (c or low).side
        if side == 0:
            a = edge[0]
            edge[0] += n
        else:
            edge[1] -= n
            a = edge[1]
        assert edge[0] <= edge[1], (name, edge)
        n = int(np.prod(shape[1:])) // (2 if dt is BF16 else 1)
        v = rounded(name, a, n)[0:shape[0], 0:n] if dt is F32R else arena[0:shape[0], a:a + n]
        if dt is not F32 and dt is not F32R:
            v = v.bitcast(dt)
        if len(shape) > 2:
            ax = " ".join("abcd"[k] for k in range(len(shape) - 1))
            v = v.rearrange(f"p ({ax}) -> p {ax}", **{"abcd"[k]: shape[k + 1] for k in range(len(shape) - 1)})
        return v

    def again(at):
        return [rounded(f"r{at}_{c}", at + c * T, T)[:, :] for c in range(8)]

    def sem(name):
        return ctx.enter_context(nc.semaphore(name))

    def lane(name):
        return [sem(name), 0]

    pe, act, dve, pool, sp = (Queue(sem(n)) for n in ("s_pe", "s_act", "s_dve", "s_pool", "s_sp"))
    banks = Ring([ctx.enter_context(nc.psum_tensor(f"bank{i}", [128, 512], F32)) for i in range(8)])

    def mm(o, l, r, start, stop, *w, skip=False):
        return pe.do(lambda e: e.matmul(o, l, r, start=start, stop=stop, skip_group_check=skip), *w)

    def tr(o, i, ident, *w):
        return pe.do(lambda e: e.transpose(o, i, ident), *w)

    def tt(q, o, a, b, op, *w):
        return q.do(lambda e: e.tensor_tensor(o, a, b, op), *w)

    def ts(q, o, a, s1, s2, op0, op1, *w):
        if op1 is None:
            return q.do(lambda e: e.tensor_scalar(o, a, s1, None, op0), *w)
        return q.do(lambda e: e.tensor_scalar(o, a, s1, s2, op0, op1), *w)

    def stt(o, a, s, b, op0, op1, *w):
        return dve.do(lambda e: e.scalar_tensor_tensor(o, a, s, b, op0, op1), *w)

    def cp(q, o, a, *w):
        if q is act:
            return q.do(lambda e: e.activation(o, a, ACT.Copy), *w)
        return q.do(lambda e: e.tensor_copy(o, a), *w)

    def af(o, a, f, *w, **k):
        return act.do(lambda e: e.activation(o, a, f, **k), *w)

    def ms(q, o, v, *w):
        return q.do(lambda e: e.memset(o, v), *w)

    def red(o, a, op, *w, **k):
        return dve.do(lambda e: e.tensor_reduce(o, a, AX.X, op, **k), *w)

    def load(q, ln, o, i, *w):
        return q.dma(ln, lambda e: e.dma_start(o, i), *w)

    def split_hi(o, a, *w, q=dve):
        return cp(q, o, a, *w)

    def split_lo(o, a, hi, *w, q=pool):
        return tt(q, o, a, hi.bitcast(F32), ALU.subtract, *w)

    def mm3(o, l, r, start, stop, *w):
        (lh, ll), (rh, rl) = l, r
        mm(o, lh, rh, start, False, *w)
        mm(o, lh, rl, False, False)
        return mm(o, ll, rh, False, stop)

    outs = []

    def barrier(*before):
        lasts = [q.last for q in before or (pe, act, dve, pool, sp)]
        for q in (pe, act, dve, pool, sp):
            q.add(None, [x for x in lasts if x is not None], Done(q.sem), 1)
            q.last = None
        for i in range(8):
            if banks.free[i] is not None:
                banks.free[i] = []

    par = sb("par", [128, NPAR])
    con = sb("con", [128, NCON])
    ev = [act, dve]
    l_par, l_con = lane("l_par"), lane("l_con")
    d_par = load(sp, l_par, par[:, :], inp["par"][:, :])
    d_con = load(act, l_con, con[:, :], inp["con"][:, :])
    for q in (pe, act, dve, pool):
        q.add(None, [d_par, d_con], Done(q.sem), 1)

    def P(name, i=0):
        return par[:, PAR[name] + i:PAR[name] + i + 1]

    def C(name, a=0, n=128):
        return con[:, CON[name] + a:CON[name] + a + n]

    ident = C("id")
    spill = nc.dram_tensor("spill", [NGRP, 128, T], F32).ap()
    d_sp = [None] * NGRP

    mid = Scope()
    at_yT = edge[0]
    yT = sb("yT", [128, 8, T])
    toks = Scope()
    vtok = sb("vtok", [128, 8, 140])
    mk = sb("mk", [128, 2, 256])
    mv = sb("mv", [128, 2, 256])
    hctx = Scope()
    memT = sb("memT", [128, 8, 256], c=hctx)
    at_hT = edge[0]
    hT = sb("hT", [128, 8, T], c=hctx)

    def transposed(dst, src, col, scale, *w):
        ends = []
        for half in range(2):
            b, f, bi = banks.take()
            for c in range(4):
                k = 4 * half + c
                t = tr(b[:, c * 128:(c + 1) * 128], src[:, k * 128:(k + 1) * 128], ident, *w, f)
            g = par[:, scale + 4 * half:scale + 4 * half + 4].unsqueeze(2).to_broadcast([128, 4, 128])
            t = tt(dve, dst[:, 4 * half:4 * half + 4, col:col + 128],
                   b[:, :].rearrange("p (c n) -> p c n", c=4), g, ALU.mult, t)
            banks.give(bi, t)
            ends.append(t)
        return ends

    def rms_scale(dst, ss, n, eps, *w):
        a = ts(dve, dst, ss, 1.0 / n, eps, ALU.mult, ALU.add, *w)
        a = af(dst, dst, ACT.Sqrt, a)
        return dve.do(lambda e: e.reciprocal(dst, dst), a)

    c1 = Scope()
    NW = 4
    wr = Ring([sb(f"wr{i}", [128, 8, 128], c=c1) for i in range(NW)])
    l_w = [lane(f"l_w{i}") for i in range(NW)]
    wv = sb("wv", [128, 8, 140], c=c1)
    wmem = sb("wmem", [128, 8, 512], c=c1)
    c0 = Scope()
    xt = sb("xt", [128, 10, D], c=c0)
    junk = sb("junk", [128, D], c=c0)
    ssq = sb("ssq", [128, 10], c=c0)
    rst = sb("rst", [128, 10], c=c0)
    d_x = [load(sp if j % 2 else act, lane(f"l_x{j}"), xt[:, j, :],
                inp["x"][j * 128:(j + 1) * 128, :] if j < 8 else inp["mem"][(j - 8) * 128:(j - 7) * 128, :])
           for j in range(10)]
    d_wm = load(act, lane("l_wmem"), wmem[:, :, :], inp["wmem"].rearrange("(c p) n -> p c n", p=128))
    d_wv = load(act, lane("l_wv"), wv[:, :, :], inp["wv"])
    ORDER = [WA] + list(range(16)) + list(range(17, NGRP))
    wq = []

    def load_w1():
        if len(wq) < NGRP:
            w, f, wi = wr.take()
            wq.append((w, wi, load(sp, l_w[wi], w[:, :, :], inp["w1"][ORDER[len(wq)]], f)))

    for n in range(NW):
        load_w1()
    s_ = None
    for j in range(10):
        s_ = af(junk[:, :], xt[:, j, :], ACT.Square, d_x[j], s_, accum_out=ssq[:, j:j + 1])
    d_r = rms_scale(rst[:, :], ssq[:, :], D, 1e-6, s_)
    hdone = []
    for j in range(10):
        a = ts(pool if j % 2 else dve, xt[:, j, :], xt[:, j, :], rst[:, j:j + 1], None, ALU.mult, None, d_r)
        if j < 8:
            hdone += transposed(hT, xt[:, j, :], j * 128, PAR["nin"], a)
        else:
            hdone += transposed(memT, xt[:, j, :], (j - 8) * 128, PAR["nmem"], a)
    barrier()
    c0.close()

    raw = Ring([sb(f"raw{i}", [128, T + 1], c=c1) for i in range(3)])
    dif = Ring([sb(f"dif{i}", [128, T], c=c1) for i in range(2)])
    mix = Ring([sb(f"mix{i}", [128, T], c=c1) for i in range(3)])
    l_sp = [lane(f"l_sp{i}") for i in range(3)]
    zs = [ms(dve, raw.bufs[i][:, 0:1], 0.0) for i in range(3)]
    wlo = Ring([sb(f"wlo{i}", [128, 2, 8, 128], F32R, c=c1) for i in range(2)])
    for j in range(8):
        b, f, bi = banks.take()
        for c in range(8):
            t = mm(b[:, 0:140], hT[:, c, j * 128:(j + 1) * 128], wv[:, c, :], c == 0, c == 7, d_wv, f)
        t_v = t
        d_vt = cp(act, vtok[:, j, :], b[:, 0:140], t)
        banks.give(bi, d_vt)
    b, f, bi = banks.take()
    for g in range(2):
        for c in range(8):
            t = mm(b[:, g * 256:(g + 1) * 256], wmem[:, c, g * 128:(g + 1) * 128], memT[:, c, :], c == 0, c == 7, d_wm, f)
    d_mk = cp(act, mk[:, :, :], b[:, :].rearrange("p (g n) -> p g n", g=2), t)
    banks.give(bi, d_mk)
    b, f, bi = banks.take()
    for g in range(2):
        for c in range(8):
            t = mm(b[:, g * 256:(g + 1) * 256], memT[:, c, g * 128:(g + 1) * 128], wmem[:, c, 256:512], c == 0, c == 7, f)
    d_mv = cp(act, mv[:, :, :], b[:, :].rearrange("p (g n) -> p g n", g=2), t)
    banks.give(bi, d_mv)

    hH, hL = again(at_yT), again(at_hT)
    hs_ = []
    for c in range(8):
        a = split_hi(hH[c], hT[:, c, :], hdone)
        hs_.append(split_lo(hL[c], hT[:, c, :], hH[c], a, t_v, q=pool if c % 2 else dve))
    wsplit = []

    def prepare_w1(n):
        if n < NGRP:
            w, wi, dw = wq[n]
            wl, wlf, wli = wlo.take()
            a = split_hi(wl[:, 0, :, :], w[:, :, :], dw, wlf)
            a = split_lo(wl[:, 1, :, :], w[:, :, :], wl[:, 0, :, :], a)
            wr.give(wi, a)
            load_w1()
            wsplit.append((wl, wli, a))

    prepare_w1(0)
    for at_, g in enumerate(ORDER):
        half = []
        wl, wli, wsp = wsplit[at_]
        prepare_w1(at_ + 1)
        rb, rf, ri = raw.take()
        for n in range(2):
            b, f, bi = banks.take()
            for c in range(8):
                ns = slice(n * 512, (n + 1) * 512)
                t = mm3(b[:, :], (wl[:, 0, c, :], wl[:, 1, c, :]), (hH[c][:, ns], hL[c][:, ns]), c == 0, c == 7, wsp, hs_[c], f)
            e = cp(act, rb[:, 1 + n * 512:513 + n * 512], b[:, :], t, rf, zs)
            banks.give(bi, e)
            half.append(e)
        wlo.give(wli, t)
        if g <= WA:
            db, df, di = dif.take()
            a = tt(pool, db[:, :], rb[:, 0:T], rb[:, 1:T + 1], ALU.subtract, half[1], df)
            mb, mf, mi = mix.take()
            a = stt(mb[:, :], db[:, :], P("mu", g), rb[:, 1:T + 1], ALU.mult, ALU.add, a, mf)
            dif.give(di, a)
            raw.give(ri, a)
            d_sp[g] = load(sp, l_sp[mi], spill[g], mb[:, :], a)
            mix.give(mi, d_sp[g])
        else:
            mb, mf, mi = mix.take()
            a = cp(pool, mb[:, :], rb[:, 1:T + 1], half[1], mf)
            raw.give(ri, a)
            d_sp[g] = load(sp, l_sp[mi], spill[g], mb[:, :], a)
            mix.give(mi, d_sp[g])
    spills = [d_sp[g] for g in range(NGRP)]
    sp.add(None, spills, Done(sp.sem), 1)
    barrier()
    c1.close()
    hctx.close()

    c2 = Scope()
    wdad = sb("wdad", [128, T], c=c2)
    up = sb("up", [128, 512], c=c2)
    rmask = sb("rmask", [128, T], BF16, c=c2)
    quad = Ring([sb("quad0", [128, 4, T], c=c2)])
    l_q = [[lane(f"l_q{i}{k}") for k in range(4)] for i in range(2)]
    E1, E2, E3, E4, E6 = (sb(f"E{i}", [128, T], c=c2) for i in (1, 2, 3, 4, 6))
    AR = sb("AR", [128, 2, T], c=c2)
    Bt = sb("Bt", [128, T], c=c2)
    Kt = sb("Kt", [128, T], c=c2)
    TL = sb("TL", [128, 4, 4, 128], c=c2)
    SC = sb("SC", [128, 2, 4, 4, 128], c=c2)
    Tm = sb("Tm", [128, 2, 4, 128], c=c2)
    TT = sb("TT", [128, 2, 4, 128], c=c2)
    Fm = sb("Fm", [128, 2, 4, 128], c=c2)
    XX = sb("XX", [128, 2, 4, 64], c=c2)
    WU = sb("WU", [128, 2, 4, 128], c=c2)
    at_tail = edge[0]
    quad = Ring([quad.bufs[0], sb("quad1", [128, 4, T], c=c2)])
    E5 = sb("E5", [128, T], c=c2)
    Gm = sb("Gm", [128, 16, 128], c=c2)
    Hm = sb("Hm", [128, 16, 128], c=c2)
    Sm = sb("Sm", [128, 2, 128], c=c2)
    Qs = sb("Qs", [128, T], c=c2)
    Yi = sb("Yi", [128, T], c=c2)
    rkb = Kt[:, 0:128]
    st16 = sb("st16", [128, 16], c=c2)
    st16b = sb("st16b", [128, 16], c=c2)
    nz1 = ms(pool, Gm[:, :, :], 0.0)
    nz2 = ms(pool, Hm[:, :, :], 0.0)
    a = ms(pool, rmask[:, :], 1.0)
    nz3 = ms(pool, rmask[:, 0:T:64], 0.0, a)
    d_wd = load(sp, lane("l_wd"), wdad[:, :], spill[WA])
    d_up = load(act, lane("l_up"), up[:, :], inp["up"][:, :])
    d_th = af(wdad[0:64, :], wdad[0:64, :], ACT.Tanh, d_wd)

    def inverse_norm(sq, heads, scale, eps, floor, st, *w):
        hd = 128 // heads
        b, f, bi = banks.take()
        for j in range(8):
            t = mm(b[:, heads * j:heads * j + heads], sq[:, j * 128:(j + 1) * 128],
                   (C("blk") if heads == 2 else C("ones"))[:, 0:128:hd], True, True, *w, f)
        n = 8 * heads
        x = ts(dve, st[:, 0:n], b[:, 0:n], scale, eps, ALU.mult, ALU.add, t)
        banks.give(bi, x)
        x = af(st[:, 0:n], st[:, 0:n], ACT.Sqrt, x)
        x = ts(dve, st[:, 0:n], st[:, 0:n], floor, None, ALU.max, None, x)
        x = dve.do(lambda e: e.reciprocal(st[:, 0:n], st[:, 0:n]), x)
        x = cp(act, sq.rearrange("p (a n) -> p a n", a=n), st[:, 0:n].unsqueeze(2).to_broadcast([128, n, hd]), x, t)
        res = []
        for half in range(2):
            b, f, bi = banks.take()
            for jj in range(4):
                j = 4 * half + jj
                t = mm(b[:, jj * 128:(jj + 1) * 128], sq[:, j * 128:(j + 1) * 128], ident, True, True, x, f)
            res.append((b, bi, t))
        return res

    def group_norm(*a):
        g_ = group_norm_steps(*a)
        while True:
            try:
                next(g_)
            except StopIteration as e:
                return e.value

    def group_norm_steps(y, tmp, mean_m, heads, eps, st, *w):
        ends = []
        for n in range(2):
            b, f, bi = banks.take()
            t = mm(b[:, :], mean_m, y[:, n * 512:(n + 1) * 512], True, True, *w, f)
            t = tt(dve, y[:, n * 512:(n + 1) * 512], y[:, n * 512:(n + 1) * 512], b[:, :], ALU.subtract, t)
            banks.give(bi, t)
            ends.append(t)
        x = af(tmp, y, ACT.Square, ends)
        yield
        r = inverse_norm(tmp, heads, heads / 128.0, eps, 0.0, st, x)
        for n in range(2):
            b, bi, t = r[n]
            x = tt(dve, y[:, n * 512:(n + 1) * 512], y[:, n * 512:(n + 1) * 512], b[:, :], ALU.mult, t, x)
            banks.give(bi, x)
        return x

    qloads = {}

    def load_pair(i):
        q, f, qi = quad.take()
        qloads[i] = (q, qi, [load(sp, l_q[qi][k], q[:, k, :], spill[(R0, K0, V0, G0)[k] + i], f) for k in range(4)])

    def prologue(i, S, fm):
        q, qi, dq = qloads[i]
        E5_ = (E5, yT[:, 7, :])[i % 2]
        r, k, v, g = (q[:, n, :] for n in range(4))
        cs = slice(i * 128, (i + 1) * 128)
        sg = []
        for n in range(2):
            ns = slice(n * 512, (n + 1) * 512)
            b, f, bi = banks.take()
            t = mm(b[:, :], up[0:64, cs], wdad[0:64, ns], True, True, d_up, d_th, f)
            x = af(E1[:, ns], b[:, :], ACT.Sigmoid, t, fm, bias=P("w0", i))
            banks.give(bi, x)
            b, f, bi = banks.take()
            t = mm(b[:, :], up[64:128, cs], wdad[64:128, ns], True, True, d_up, d_wd, f)
            y = af(E2[:, ns], b[:, :], ACT.Sigmoid, t, fm, bias=P("a0", i))
            banks.give(bi, y)
            yield
        d_g = af(g, g, ACT.Silu, dq[3])
        d_L = ts(dve, E1[:, :], E1[:, :], -float(np.exp(np.float32(-0.5))), None, ALU.mult, None, x)
        d_cum = dve.do(lambda e: e.tensor_tensor_scan(E3[:, :], rmask[:, :], E1[:, :], 0.0, ALU.mult, ALU.add),
                       d_L, nz3)
        yield
        x = ts(dve, E4[:, :], k, P("kk", i), None, ALU.mult, None, dq[1])
        x2 = af(E5_[:, :], E4[:, :], ACT.Square, x, fm)
        yield
        res = inverse_norm(E5_[:, :], 2, 1.0, 0.0, 1e-12, st16, x2)
        for n in range(2):
            b, bi, t = res[n]
            x = tt(dve, E4[:, n * 512:(n + 1) * 512], E4[:, n * 512:(n + 1) * 512], b[:, :], ALU.mult, t, x)
            banks.give(bi, x)
        d_kk = x
        yield
        x = ts(dve, E5_[:, :], E2[:, :], -1.0, P("ka", i), ALU.add, ALU.mult, y, res[1][2])
        d_k = stt(k, E5_[:, :], 1.0, k, ALU.add, ALU.mult, x)
        yield
        a0_ = ts(pool, rkb[:, :], C("blk"), P("rk", i), None, ALU.mult, None, fm)
        x = tt(pool, E5_[:, :], r, k, ALU.mult, d_k, dq[0])
        bon = []
        for n in range(2):
            b, f, bi = banks.take()
            bon.append((b, bi, mm(b[:, :], rkb[:, :], E5_[:, n * 512:(n + 1) * 512], True, True, x, a0_, f)))
        for n in range(2):
            b, bi, t = bon[n]
            d_bon = tt(dve, E5_[:, n * 512:(n + 1) * 512], v[:, n * 512:(n + 1) * 512], b[:, :], ALU.mult, t, bon[1][2], dq[2])
            banks.give(bi, d_bon)
        yield
        d_b = tt(pool, E2[:, :], E2[:, :], E4[:, :], ALU.mult, d_kk, x)
        yield
        x = tt(pool, E6[:, :], E3[:, :], E1[:, :], ALU.subtract, d_cum)
        e6 = af(E6[:, :], E6[:, :], ACT.Exp, x)
        yield
        d_A = stt(AR[:, 0, :], E4[:, :], -1.0, E6[:, :], ALU.mult, ALU.mult, e6, d_kk, d_b)
        e1 = af(E1[:, :], E3[:, :], ACT.Exp, d_cum, x)
        d_R = tt(dve, AR[:, 1, :], r, E1[:, :], ALU.mult, e1)
        e6 = af(E6[:, :], E3[:, :], ACT.Exp, d_A, scale=-1.0)
        yield
        d_B = tt(dve, Bt[:, :], E2[:, :], E6[:, :], ALU.mult, e6, d_b)
        d_K = tt(dve, Kt[:, :], k, E6[:, :], ALU.mult, e6, d_k, bon[1][2])
        pc = E1[:, 63:T:64]
        pcb = pc.unsqueeze(2).to_broadcast([128, 16, 64])
        c3 = lambda a: a.rearrange("p (c t) -> p c t", c=16)
        d_Bh = tt(dve, c3(E2[:, :]), c3(Bt[:, :]), pcb, ALU.mult, d_B)
        d_Kh = tt(pool, c3(E6[:, :]), c3(Kt[:, :]), pcb, ALU.mult, d_K, d_B)
        yield
        d_D = tt(pool, c3(E3[:, :]), C("id2", 0, 64).unsqueeze(1).to_broadcast([128, 16, 64]), pcb, ALU.mult, e6, e1)
        S.update(v=v, g=g, d_A=d_A, d_R=d_R, d_B=d_B, d_K=d_K, d_Bh=d_Bh, d_Kh=d_Kh, d_D=d_D, d_bon=d_bon, d_g=d_g,
                 dq=dq, E5_=E5_, qi=qi)

    def main(i, S, prev):
        v, g, d_A, d_R, d_B, d_K, d_Bh = (S[n] for n in "v g d_A d_R d_B d_K d_Bh".split())
        d_Kh, d_D, d_bon, d_g, dq, E5_, qi = (S[n] for n in "d_Kh d_D d_bon d_g dq E5_ qi".split())
        done_half = None
        gh = []
        for hf in range(2):
            dTL = []
            for jj in range(4):
                j = 4 * hf + jj
                js = slice(j * 128, (j + 1) * 128)
                b, f, bi = banks.take()
                tr(b[:, 0:128], AR[:, 0, js], ident, d_A, f)
                tr(b[:, 128:256], E2[:, js], ident, d_Bh)
                tr(b[:, 256:384], E6[:, js], ident, d_Kh)
                t = tr(b[:, 384:512], v[:, js], ident, dq[2])
                t = cp(act, TL[:, jj, :, :], b[:, :].rearrange("p (a n) -> p a n", a=4), t, done_half)
                banks.give(bi, t)
                dTL.append(t)
            dSC = [[None] * 4, [None] * 4]
            dT, dTT = [None] * 2, [None] * 2
            scm = con[:, CON["sc"]:CON["sc"] + 512]
            for h in range(2):
                hs = slice(64 * h, 64 * h + 64)
                for jj in range(4):
                    js = slice((4 * hf + jj) * 128, (4 * hf + jj + 1) * 128)
                    b, f, bi = banks.take()
                    mm(b[:, 0:256].rearrange("p (a n) -> p a n", a=2), Bt[hs, js], AR[hs, :, js], True, True, d_B, d_A, d_R, f)
                    t = mm(b[:, 256:512].rearrange("p (a n) -> p a n", a=2), Kt[hs, js], AR[hs, :, js], True, True, d_K)
                    t = tt(dve, SC[:, h, jj, :, :].rearrange("p a n -> p (a n)"), b[:, :], scm, ALU.mult, t, done_half)
                    banks.give(bi, t)
                    dSC[h][jj] = t
                b, f, bi = banks.take()
                for jj in range(4):
                    js = slice((4 * hf + jj) * 128, (4 * hf + jj + 1) * 128)
                    t = mm(b[:, jj * 128:(jj + 1) * 128], AR[hs, 0, js], Bt[hs, js], True, True, f)
                b4 = b[:, :].rearrange("p (a n) -> p a n", a=4)
                bc = lambda m: m.unsqueeze(1).to_broadcast([128, 4, 128])
                x = tt(dve, Tm[:, h, :, :], b4, bc(C("m1")), ALU.mult, t, done_half)
                banks.give(bi, x)
                dT[h] = tt(pool, Tm[:, h, :, :], Tm[:, h, :, :], bc(ident), ALU.add, x)
                x = tt(pool, TT[:, h, :, :], SC[:, h, :, 0, :], bc(C("m1t")), ALU.mult, dSC[h][3], done_half)
                dTT[h] = tt(pool, TT[:, h, :, :], TT[:, h, :, :], bc(ident), ALU.add, x)
            for lv in range(5):
                lm = bc(C("lv", lv * 128))
                dF = [None] * 2
                for h in range(2):
                    b, f, bi = banks.take()
                    for jj in range(4):
                        t = mm(b[:, jj * 128:(jj + 1) * 128], SC[:, h, jj, 0, :], Tm[:, h, jj, :], True, True,
                               dT[h], dSC[h][3], f)
                    dF[h] = tt(dve, Fm[:, h, :, :], b[:, :].rearrange("p (a n) -> p a n", a=4), lm, ALU.mult, t)
                    banks.give(bi, dF[h])
                for h in range(2):
                    if lv < 4:
                        b, f, bi = banks.take()
                        for jj in range(4):
                            t = mm(b[:, jj * 128:(jj + 1) * 128], TT[:, h, jj, :], Fm[:, h, jj, :], True, True,
                                   dF[h], dTT[h], f)
                    b2, f2, bi2 = banks.take()
                    for jj in range(4):
                        t2 = mm(b2[:, jj * 128:(jj + 1) * 128], Fm[:, h, jj, :], TT[:, h, jj, :], True, True,
                                dF[h], dTT[h], f2)
                    if lv < 4:
                        dT[h] = tt(dve, Tm[:, h, :, :], Tm[:, h, :, :], b[:, :].rearrange("p (a n) -> p a n", a=4),
                                   ALU.add, t, t2)
                        banks.give(bi, dT[h])
                    dTT[h] = tt(dve, TT[:, h, :, :], TT[:, h, :, :], b2[:, :].rearrange("p (a n) -> p a n", a=4),
                                ALU.add, t2)
                    banks.give(bi2, dTT[h])
            dWU = [None] * 2
            for h in range(2):
                hc = slice(64 * h, 64 * h + 64)
                b, f, bi = banks.take()
                for jj in range(4):
                    t = mm(b[:, jj * 64:jj * 64 + 64], SC[:, h, jj, 2, :], TL[:, jj, 3, hc], True, True, dTL[3], f)
                dX = cp(act, XX[:, h, :, :], b[:, 0:256].rearrange("p (a n) -> p a n", a=4), t, done_half)
                banks.give(bi, dX)
                b, f, bi = banks.take()
                for jj in range(4):
                    mm(b[:, jj * 128:jj * 128 + 64], TT[:, h, jj, :], TL[:, jj, 0, hc], True, True, dTT[h], f)
                    t = mm(b[:, jj * 128 + 64:jj * 128 + 128], TT[:, h, jj, :], XX[:, h, jj, :], True, True, dX)
                dWU[h] = cp(act, WU[:, h, :, :], b[:, :].rearrange("p (a n) -> p a n", a=4), t, done_half)
                banks.give(bi, dWU[h])
            by, fy, iy = banks.take()
            bq, fq, iq = banks.take()
            for h in range(2):
                hs = slice(64 * h, 64 * h + 64)
                for jj in range(4):
                    n = slice(jj * 128, (jj + 1) * 128)
                    mm(by[hs, n], WU[:, h, jj, 64:128], SC[:, h, jj, 1, :], True, False, dWU[h], fy)
                    ty = mm(by[hs, n], TL[:, jj, 3, hs], SC[:, h, jj, 3, :], False, True)
                    tq = mm(bq[hs, n], WU[:, h, jj, 0:64], SC[:, h, jj, 1, :], True, True, fq)
            hn = slice(hf * 512, (hf + 1) * 512)
            dYi = cp(act, Yi[:, hn], by[:, :], ty, prev)
            banks.give(iy, dYi)
            dQ = tt(dve, Qs[:, hn], bq[:, :], AR[:, 1, hn], ALU.add, tq, prev)
            banks.give(iq, dQ)
            for par_ in range(2):
                rs = slice(64 * par_, 64 * par_ + 64)
                bg, fg, ig = banks.take()
                bh, fh, ih = banks.take()
                for h in range(2):
                    hs = slice(64 * h, 64 * h + 64)
                    for jj in range(4):
                        n = slice(jj * 64, jj * 64 + 64)
                        tg = mm(bg[hs, n], WU[rs, h, jj, 0:64], TL[rs, jj, 1, hs], True, True, dWU[h], fg)
                        mm(bh[hs, n], TL[rs, jj, 1, hs], WU[rs, h, jj, 64:128], True, False, fh)
                        th = mm(bh[hs, n], TL[rs, jj, 2, hs], TL[rs, jj, 3, hs], False, True)
                for h in range(2):
                    hs = slice(64 * h, 64 * h + 64)
                    cc = slice(8 * hf + par_, 8 * hf + 8, 2)
                    x = tt(dve, Gm[hs, cc, hs], bg[hs, 0:256].rearrange("p (a n) -> p a n", a=4),
                           E3[hs, :].rearrange("p (c t) -> p c t", c=16)[:, cc, :], ALU.add, tg, d_D, nz1, prev)
                    y_ = cp(act, Hm[hs, cc, hs], bh[hs, 0:256].rearrange("p (a n) -> p a n", a=4), th, nz2, prev)
                banks.give(ig, x)
                banks.give(ih, y_)
                gh += [x, y_]
            done_half = th
        S.update(dQ=dQ, dYi=dYi, gh=gh, th=th, ty=ty)

    def tail(i, S, prev):
        v, g, d_A, d_R, d_B, d_K, d_Bh = (S[n] for n in "v g d_A d_R d_B d_K d_Bh".split())
        d_Kh, d_D, d_bon, d_g, dq, E5_, qi = (S[n] for n in "d_Kh d_D d_bon d_g dq E5_ qi".split())
        dQ, dYi, gh, ty = S["dQ"], S["dYi"], S["gh"], S["ty"]
        s0 = ms(dve, Sm[:, 0, :], 0.0, prev)
        ds = s0
        rd = [None, None]
        ends = []
        for c in range(16):
            if c % 8 == 0:
                by, fy, iy = banks.take()
            n = slice((c % 8) * 64, (c % 8) * 64 + 64)
            ty = mm(by[:, n], Sm[:, c % 2, :], Qs[:, c * 64:c * 64 + 64], True, True, ds, dQ, fy)
            if c < 15:
                b, f, bi = banks.take()
                t = mm(b[:, 0:128], Gm[:, c, :], Sm[:, c % 2, :], True, True, ds, gh, f)
                ds = tt(dve, Sm[:, (c + 1) % 2, :], b[:, 0:128], Hm[:, c, :], ALU.add, t)
                banks.give(bi, ds)
            yield
            if c % 8 == 7:
                hn = slice((c // 8) * 512, (c // 8) * 512 + 512)
                x = tt(dve, Yi[:, hn], Yi[:, hn], by[:, :], ALU.add, ty, dYi)
                banks.give(iy, x)
                ends.append(x)
        yield
        x = yield from group_norm_steps(Yi[:, :], yT[:, 6, :], C("blkm"), 2, 64e-5, st16b, ends, gh, ty)
        x = ts(dve, Yi[:, :], Yi[:, :], P("lnw", i), P("lnb", i), ALU.mult, ALU.add, x)
        x = tt(pool, Yi[:, :], Yi[:, :], E5_, ALU.add, x, d_bon)
        x = tt(pool, yT[:, i, :], Yi[:, :], g, ALU.mult, x, d_g)
        quad.give(qi, x)
        S["end"] = x

    def together(*gens, first=1):
        gens = list(gens)
        while gens:
            for g_ in gens[:1] * (first - 1) + gens:
                if g_ in gens and next(g_, "end") == "end":
                    gens.remove(g_)

    load_pair(0)
    prev = fm = None
    S = {}
    together(prologue(0, S, None))
    for i in range(4):
        if i < 3:
            load_pair(i + 1)
        main(i, S, prev)
        nxt = {}
        fm = [S["th"], S["dQ"], S["gh"], S["ty"], S["dYi"]]
        if i == 3:
            break
        together(prologue(i + 1, nxt, fm), tail(i, S, prev), first=2)
        prev = S["end"]
        S = nxt
    barrier()
    c2.close()

    c3_ = Scope()
    tl = [sb(f"tl{i}", [128, T], c=c3_) for i in range(10)]
    groups = [NQ, NQ + 1, MQ, MQ + 1, KSW, KVC, NG, NG + 1, MG, MG + 1]
    d_tl = [None] * 10

    def load_tiles(*ns):
        for n in ns:
            d_tl[n] = load(sp if n % 2 else act, lane(f"l_tl{n}"), tl[n][:, :], spill[groups[n]])

    load_tiles(5)
    q0, q1, m0_, m1_, ksw, kvc = tl[:6]
    gates = tl[6:]
    rope = sb("rope", [128, 2, T], c=c3_)
    cw1 = sb("cw1", [128, 32, 64], c=c3_)
    cw2 = sb("cw2", [128, 128], c=c3_)
    cpos = sb("cpos", [128, 32], c=c3_)
    cmask = sb("cmask", [128, 2, 8, 64], c=c3_)
    gb = sb("gb", [128, 12], c=c3_)
    d_cw = [load(act, lane("l_cw1"), cw1[:, :, :], inp["cw1"]), load(sp, lane("l_cw2"), cw2[:, :], inp["cw2"]),
            load(act, lane("l_cpos"), cpos[:, :], inp["cpos"])]
    load_tiles(4, 0, 1)
    d_rope = load(sp, lane("l_rope"), rope[:, :, :], inp["rope"])
    load_tiles(2, 3, 6, 7, 8, 9)
    d_cm = load(act, lane("l_cm"), cmask[:, :, :, :], inp["cmask"])
    d_gb = load(sp, lane("l_gb"), gb[:, :], inp["gb"].partition_broadcast(128))
    qr = [sb(f"qr{i}", [128, T], c=c3_) for i in range(2)]
    kr = sb("kr", [128, T], c=c3_)
    kx = sb("kx", [128, T], c=c3_)
    hid = sb("hid", [128, 64], c=c3_)
    hb_ = sb("hb_", [128, 1], c=c3_)
    kcC = sb("kcC", [128, 64], c=c3_)
    vcm = sb("vcm", [64, 64], c=c3_)
    g4 = sb("g4", [128, 8, 4, 4], c=c3_)
    rs = sb("rs", [128, 2, 8, 4, 4], c=c3_)
    mx = sb("mx", [128, 2, 8, 4, 4], c=c3_)
    Pr = Ring([sb(f"Pr{i}", [128, T], c=c3_) for i in range(3)])
    PTr = Ring([sb(f"PT{i}", [128, 8, 128], c=c3_) for i in range(2)])
    assert edge[0] <= at_tail
    d_kc = d_vc = d_g4 = d_q = d_kx = zr = None
    d_gate, d_qr = [], []

    def prepare_nsa():
        nonlocal d_kc, d_vc, d_g4, d_q, d_kx, zr
        bA, fA, iA = banks.take()
        bB, fB, iB = banks.take()
        for lo, b, f in ((0, bA, fA), (64, bB, fB)):
            hs = slice(lo, lo + 64)
            for j in range(32):
                mm(b[hs, 0:63], cw1[hs, j, :], kvc[hs, j:j + 16 * 62 + 1:16], j == 0, j == 31, d_tl[5], d_cw[0], f)
                if j % 4 == 3:
                    yield
            for j in range(32):
                t = mm(b[hs, 64:65], cw1[hs, j, :], cpos[hs, j:j + 1], j == 0, j == 31, d_cw[2])
                if j % 8 == 7:
                    yield
            if lo == 0:
                tA = t
        x = cp(act, hb_[0:64, :], bA[0:64, 64:65], tA)
        y = cp(act, hb_[64:128, :], bB[64:128, 64:65], t)
        x = af(hid[0:64, 0:63], bA[0:64, 0:63], ACT.Silu, x, bias=hb_[0:64, 0:1])
        y = af(hid[64:128, 0:63], bB[64:128, 0:63], ACT.Silu, y, bias=hb_[64:128, 0:1])
        banks.give(iA, x)
        banks.give(iB, y)
        yield
        b, f, bi = banks.take()
        t = mm(b[:, 0:63], cw2[0:64, :], hid[0:64, 0:63], True, True, x, d_cw[1], f)
        d_kc = cp(act, kcC[:, 0:63], b[:, 0:63], t)
        banks.give(bi, d_kc)
        yield
        b, f, bi = banks.take()
        t = mm(b[0:63, 0:64], hid[64:128, 0:63], cw2[64:128, 0:64], True, True, y, f)
        d_vc = cp(act, vcm[0:63, :], b[0:63, 0:64], t)
        banks.give(bi, d_vc)
        z = ms(dve, g4[:, :, :, :], 1.0)
        zr = ms(dve, rs[:, :, :, :, :], 0.0)
        x = tt(dve, vtok[:, :, 128:140], vtok[:, :, 128:140], gb[:, :].unsqueeze(1).to_broadcast([128, 8, 12]), ALU.add, d_gb)
        d_g4 = af(g4[:, :, :, 0:3], vtok[:, :, 128:140].rearrange("p j (h b) -> p j h b", h=4), ACT.Sigmoid, x, z)
        d_q = [ts(dve, a[:, :], a[:, :], 0.125, None, ALU.mult, None, d_tl[n]) for n, a in enumerate((q0, q1, m0_, m1_))]
        for n, (src, dst, dd) in enumerate(((q0, qr[0], d_q[0]), (q1, qr[1], d_q[1]), (ksw, kr, d_tl[4]))):
            a = tt(pool if n < 2 else dve, dst[:, :], src[:, :], rope[:, 0, :], ALU.mult, dd, d_rope)
            yield
            for h in range(2):
                hn = slice(h * 512, (h + 1) * 512)
                b, f, bi = banks.take()
                t = mm(b[:, :], C("perm"), src[:, hn], True, True, dd, f)
                pb_, pf_, pi_ = Pr.take()
                t = tt(dve, pb_[:, 0:512], b[:, :], rope[:, 1, hn], ALU.mult, t, d_rope, pf_)
                banks.give(bi, t)
                t = tt(dve, dst[:, hn], dst[:, hn], pb_[:, 0:512], ALU.add, t, a)
                Pr.give(pi_, t)
            d_qr.append(t)
        d_kx = [load(sp, lane("l_kx0"), kx[64:128, :], kr[0:64, :], d_qr[2]),
                load(act, lane("l_kx1"), kx[0:64, :], kr[64:128, :], d_qr[2])]
        for c in range(4):
            d_gate.append(af(gates[c][:, :], gates[c][:, :], ACT.Silu, d_tl[6 + c]))

    tail3 = tail(3, S, prev)
    for _ in range(12):
        next(tail3)
    together(tail3, prepare_nsa())
    barrier()
    high = Scope(1)
    small = sb("small", [128, 64], c=high)
    woc = Scope(1)
    wo = sb("wo", [128, 8, D], c=woc)
    d_wo = [load(sp if c % 2 else act, lane(f"l_wo{c}"), wo[:, c, :], inp["wo"][c * 128:(c + 1) * 128, :]) for c in range(8)]
    o3 = Ring([sb(f"o3{i}", [128, 4, 4, 64], c=c3_) for i in range(2)])
    ot = Ring([sb(f"ot{i}", [128, 512], c=c3_) for i in range(2)])
    osq = sb("osq", [128, 512], c=c3_)
    oss = Ring([sb(f"oss{i}", [128, 8], c=c3_) for i in range(2)])

    def job(br, h, j):
        hs = slice(64 * (h % 2), 64 * (h % 2) + 64)
        js = slice(j * 128, (j + 1) * 128)
        if br == 0:
            return (q0, q1)[h // 2][hs, js], kcC[hs, 0:63], 63, {0: cmask[:, 0, j, 0:63]}, [vcm[0:63, :]], [d_q, d_kc, d_vc, d_cm]
        if br == 3:
            return ((m0_, m1_)[h // 2][hs, js], mk[hs, h // 2, :], 256, {},
                    [mv[:, g, 64 * h:64 * h + 64] for g in range(2)], [d_q, d_mk, d_mv])
        lo = 0 if br == 1 else max(0, j - 4)
        own = (h % 2 == 0) == (br == 1)
        kt = (kr if own else kx)[hs, lo * 128:(j + 1) * 128]
        masks = {j - lo: C("diag")}
        if br == 2 and j >= 4:
            masks[0] = C("far")
        vs = [vtok[:, t_, 64 * (br - 1):64 * br] for t_ in range(lo, j + 1)]
        return qr[h // 2][hs, js], kt, (j + 1 - lo) * 128, masks, vs, [d_qr, d_kx]

    jobs = [(br, h, j) for j in range(8) for h in range(4) for br in (1, 2, 0, 3)]
    st = {}

    def scores(n):
        br, h, j = jobs[n]
        q, k, nk, masks, vs, w = job(br, h, j)
        nb = (nk + 511) // 512
        pb_, pf_, pi_ = Pr.take()
        bk = []
        for u in range(nb):
            b, f, bi = banks.take()
            n0, n1 = u * 512, min(nk, u * 512 + 512)
            mine = [m for m in sorted(masks) if n0 <= m * 128 < n1]
            t = mm(b[:, 0:n1 - n0], q, k[:, n0:n1], True, not mine, w, f)
            for m in mine:
                wd = min(128, n1 - m * 128)
                t = mm(b[:, m * 128 - n0:m * 128 - n0 + wd], ident, masks[m], False, m == mine[-1])
            x = red(mx[:, u, j, h, br:br + 1], b[:, 0:n1 - n0], ALU.max, t, negate=True)
            bk.append((b, bi, n0, n1, x))
        if nb == 2:
            x = tt(dve, mx[:, 0, j, h, br:br + 1], mx[:, 0, j, h, br:br + 1], mx[:, 1, j, h, br:br + 1], ALU.min, x)
        e = []
        for u, (b, bi, n0, n1, _) in enumerate(bk):
            kw = {} if br == 0 else {"accum_out": rs[:, u, j, h, br:br + 1]}
            t = af(pb_[:, n0:n1], b[:, 0:n1 - n0], ACT.Exp, x, pf_, zr, bias=mx[:, 0, j, h, br:br + 1], **kw)
            banks.give(bi, t)
            e.append(t)
        if br == 0:
            t = tt(dve, pb_[:, 0:63], pb_[:, 0:63], cmask[:, 1, j, 0:63], ALU.mult, t)
            st[("rs", j, h)] = red(rs[:, 0, j, h, 0:1], pb_[:, 0:63], ALU.add, t)
        st[n] = (pb_, pi_, nk, vs, t)

    def turns(n):
        pb_, pi_, nk, vs, t0 = st[n]
        pt, ptf, pti = PTr.take()
        last = []
        for u in range((nk + 511) // 512):
            b, f, bi = banks.take()
            m = min(4, (nk - u * 512 + 127) // 128)
            for a in range(m):
                k0 = u * 512 + a * 128
                wd = min(128, nk - k0)
                t = tr(b[0:wd, a * 128:(a + 1) * 128], pb_[:, k0:k0 + wd], ident, t0, f)
            wd = min(128, nk)
            x = cp(ev[(n + u) % 2], pt[0:wd, u * 4:u * 4 + m, :], b[0:wd, 0:m * 128].rearrange("p (a n) -> p a n", a=m), t, ptf)
            banks.give(bi, x)
            last.append(x)
        Pr.give(pi_, t, st.get(("rs", jobs[n][2], jobs[n][1])) if jobs[n][0] == 0 else None)
        st[n] = (pt, pti, nk, vs, last)

    osl = {}

    def values(n):
        br, h, j = jobs[n]
        pt, pti, nk, vs, w = st.pop(n)
        b, f, bi = banks.take()
        wd = min(128, nk)
        for a, v_ in enumerate(vs):
            t = mm(b[:, 0:64], pt[0:wd, a, :], v_, a == 0, a == len(vs) - 1, w, f)
        PTr.give(pti, t)
        if h == 0 and br == 1:
            osl[j] = o3.take()
        o, of, _ = osl[j]
        x = cp(ev[(n + 1) % 2], o[:, h, br, :], b[:, 0:64], t, of)
        banks.give(bi, x)
        osl.setdefault(("d", j), []).append(x)
        if h == 3 and br == 3:
            merges.append(merge(j))
            next(merges[-1])

    def merge(j):
        o, _, oi = osl[j]
        a = tt(dve, rs[:, 0, j, :, :], rs[:, 0, j, :, :], rs[:, 1, j, :, :], ALU.add,
               osl[("d", j)], [st[("rs", j, h)] for h in range(4)])
        a = ts(dve, rs[:, 0, j, :, :], rs[:, 0, j, :, :], 1e-30, None, ALU.max, None, a)
        a = dve.do(lambda e: e.reciprocal(rs[:, 0, j, :, :], rs[:, 0, j, :, :]), a)
        a = tt(dve, rs[:, 0, j, :, :], rs[:, 0, j, :, :], g4[:, j, :, :], ALU.mult, a, d_g4)
        ov = o[:, :, :, :].rearrange("p h b d -> p (h b) d")
        a = tt(dve, ov, ov, rs[:, 0, j, :, :].rearrange("p h b -> p (h b)").unsqueeze(2).to_broadcast([128, 16, 64]),
               ALU.mult, a)
        tk, tf, ti = ot.take()
        t4 = tk[:, 0:256].rearrange("p (h d) -> p h d", h=4)
        x1 = tt(pool, t4, o[:, :, 0, :], o[:, :, 1, :], ALU.add, a, tf)
        x1 = tt(pool, t4, t4, o[:, :, 2, :], ALU.add, x1)
        x2 = cp(pool, tk[:, 256:512].rearrange("p (h d) -> p h d", h=4), o[:, :, 3, :], a, tf)
        o3.give(oi, x1, x2)
        s_, sf, si = oss.take()
        a = tt(pool, osq[:, :], tk[:, :], tk[:, :], ALU.mult, x1, x2, st.get("osq"))
        yield
        a = red(s_[:, :], osq[:, :].rearrange("p (h d) -> p h d", h=8), ALU.add, a, sf)
        st["osq"] = a
        yield
        a = rms_scale(s_[:, :], s_[:, :], 64, 1e-6, a)
        yield
        t8 = tk[:, :].rearrange("p (h d) -> p h d", h=8)
        a = tt(pool, t8, t8, s_[:, :].unsqueeze(2).to_broadcast([128, 8, 64]), ALU.mult, a)
        oss.give(si, a)
        yield
        b, f, bi = banks.take()
        for c in range(4):
            t = tr(b[:, c * 128:(c + 1) * 128], tk[:, c * 128:(c + 1) * 128], ident, a, f)
        ot.give(ti, t)
        for c in range(4):
            js = slice(j * 128, (j + 1) * 128)
            x = stt(yT[:, 4 + c, js], b[:, c * 128:(c + 1) * 128], P("nsag", c), gates[c][:, js], ALU.mult, ALU.mult,
                    t, d_gate)
        banks.give(bi, x)

    merges = []
    for n in range(len(jobs) + 2):
        for g in list(merges) if n % 2 else []:
            if next(g, "end") == "end":
                merges.remove(g)
        if n < len(jobs):
            scores(n)
        if 1 <= n <= len(jobs):
            turns(n - 1)
        if n >= 2:
            values(n - 2)
    for g in merges:
        for _ in g:
            pass
    barrier()
    c3_.close()
    toks.close()

    h1s = Scope()
    at_h1T = edge[0]
    h1T = sb("h1T", [128, 8, T], c=h1s)
    c5 = Scope()
    junk = sb("junk3", [128, D], c=c5)
    x1 = Ring([sb(f"x1{i}", [128, D], c=c5) for i in range(3)])
    l_x1 = [lane(f"l_x1{i}") for i in range(3)]
    x1d = nc.dram_tensor("x1d", [T, D], F32).ap()
    d_x1 = []
    xs_ = Ring([sb(f"xs{i}", [128, D], c=c5) for i in range(3)])
    hs_ = Ring([sb(f"hs{i}", [128, D], c=c5) for i in range(2)])
    l_xs = [lane(f"l_xs{i}") for i in range(3)]
    nfg = sb("nfg", [128, D], c=c5)
    d_nf = load(act, lane("l_nf"), nfg[:, :], inp["nfg"].partition_broadcast(128))
    jk = None
    later = None
    for j in range(8):
        xb, xf, xi = xs_.take()
        dx = load(sp, l_xs[xi], xb[:, :], inp["x"][j * 128:(j + 1) * 128, :], xf)
        for n in range(2):
            ns = slice(n * 512, (n + 1) * 512)
            b, f, bi = banks.take()
            for c in range(8):
                t = mm(b[:, :], yT[:, c, j * 128:(j + 1) * 128], wo[:, c, ns], c == 0, c == 7, d_wo[c], f)
            t = tt(dve, xb[:, ns], xb[:, ns], b[:, :], ALU.add, t, dx)
            banks.give(bi, t)
        if later:
            later()
        a = af(junk[:, :], xb[:, :], ACT.Square, t, jk, accum_out=small[:, j:j + 1])
        a = rms_scale(small[:, j:j + 1], small[:, j:j + 1], D, 1e-6, a)
        x1b, x1f, x1i = x1.take()
        a = stt(x1b[:, :], xb[:, :], small[:, j:j + 1], nfg[:, :], ALU.mult, ALU.mult, a, d_nf, x1f)
        xs_.give(xi, a)
        d_x1.append(load(sp, l_x1[x1i], x1d[j * 128:(j + 1) * 128, :], x1b[:, :], a))
        jk = af(junk[:, :], x1b[:, :], ACT.Square, a, accum_out=small[:, 8 + j:9 + j])
        x = rms_scale(small[:, 8 + j:9 + j], small[:, 8 + j:9 + j], D, 1e-6, jk)
        hb, hf_, hi_ = hs_.take()
        x = ts(pool, hb[:, :], x1b[:, :], small[:, 8 + j:9 + j], None, ALU.mult, None, x, hf_)
        x1.give(x1i, x, d_x1[j])

        def later(hb=hb, hi_=hi_, j=j, x=x):
            e_ = transposed(h1T, hb, j * 128, PAR["n1"], x)
            hs_.give(hi_, *e_)
    later()
    sp.add(None, d_x1, Done(sp.sem), 1)
    barrier()
    c5.close()
    woc.close()

    c6 = Scope()
    w2r = Ring([sb(f"w2r{i}", [128, 8, 128], c=c6) for i in range(2)])
    l_w2 = [lane(f"l_w2{i}") for i in range(2)]
    w2s = Ring([sb(f"w2s{i}", [128, 2, 8, 128], F32R, c=c6) for i in range(2)])
    at_h1H = edge[0]
    sb("h1H", [128, 8, T], c=c6)
    h1H, h1L = again(at_h1H), again(at_h1T)
    hs_ = []
    for c in range(8):
        a = split_hi(h1H[c], h1T[:, c, :], q=act)
        hs_.append(split_lo(h1L[c], h1T[:, c, :], h1H[c], a, q=pool if c % 2 else dve))
    rt = sb("rt", [128, 2, T], c=c6)
    rc = sb("rc", [128, NRC], c=c6)
    qb, kb, qs_, ks_ = (sb(n, [128, T], c=c6) for n in ("qb", "kb", "qs_", "ks_"))
    vt = sb("vt", [128, 8, 128], c=c6)
    gt = sb("gt", [128, T], c=c6)
    scT = sb("scT", [128, 8, 128], c=c6)
    kd = sb("kd", [128, 8, 128], c=c6)
    Sr = sb("Sr", [128, 8, 128], c=c6)
    Or = sb("Or", [128, T], c=c6)
    cu = sb("cu", [128, T + 2], c=c6)
    cg = sb("cg", [128, T], c=c6)
    ca = sb("ca", [128, T], c=c6)
    st8 = sb("st8", [128, 8], c=c6)
    d_rt = load(sp, lane("l_rt"), rt[:, :, :], inp["rot"])
    d_rc = load(act, lane("l_rc"), rc[:, :], inp["rc"])
    z2 = ms(dve, cu[:, 0:2], 0.0)
    l_sw = [lane(f"l_sw{i}") for i in range(4)]

    order2 = [g for h in range(4) for g in (*range(4 * h, 4 * h + 4), *range(16 + 3 * h, 19 + 3 * h))]
    w2q, w2p = [], []

    def load_w2():
        if len(w2q) < 28:
            w, f, wi = w2r.take()
            w2q.append((w, wi, load(sp, l_w2[wi], w[:, :, :], inp["w2"][order2[len(w2q)]], f)))

    def prepare_w2():
        if len(w2p) < 28:
            w, wi, dw = w2q[len(w2p)]
            wl, wlf, wli = w2s.take()
            a = split_hi(wl[:, 0, :, :], w[:, :, :], dw, wlf)
            a = split_lo(wl[:, 1, :, :], w[:, :, :], wl[:, 0, :, :], a)
            w2r.give(wi, a)
            load_w2()
            w2p.append((wl, wli, a))

    for n in range(2):
        load_w2()
    prepare_w2()
    at2 = [0]

    def project(g):
        assert order2[at2[0]] == g
        wl, wli, wsp = w2p[at2[0]]
        at2[0] += 1
        prepare_w2()
        res = []
        for n in range(2):
            b, f, bi = banks.take()
            for c in range(8):
                ns = slice(n * 512, (n + 1) * 512)
                t = mm3(b[:, :], (wl[:, 0, c, :], wl[:, 1, c, :]), (h1H[c][:, ns], h1L[c][:, ns]), c == 0, c == 7,
                        wsp, hs_[c], f)
            res.append((b, bi, t, ns))
        w2s.give(wli, t)
        return res

    def to(res, q, dst, *w):
        ends = []
        for b, bi, t, ns in res:
            x = cp(q, dst[:, ns], b[:, :], t, w)
            banks.give(bi, x)
            ends.append(x)
        return ends

    fr = free_q = None
    cfr = None
    for h in range(4):
        d_qb = to(project(4 * h), act, qb, free_q)
        if h:
            fr = norm_later()
        d_kb = to(project(4 * h + 1), act, kb, fr)
        sw = [load(act, l_sw[0], qs_[0:64, :], qb[64:128, :], d_qb, free_q), load(act, l_sw[1], qs_[64:128, :], qb[0:64, :], d_qb, free_q),
              load(act, l_sw[2], ks_[0:64, :], kb[64:128, :], d_kb), load(act, l_sw[3], ks_[64:128, :], kb[0:64, :], d_kb)]
        d_vc = to(project(4 * h + 2), act, cg, cfr)
        d_gt = []
        for b, bi, t, ns in project(4 * h + 3):
            x = af(gt[:, ns], b[:, :], ACT.Silu, t, fr)
            banks.give(bi, x)
            d_gt.append(x)
        for hf in range(2):
            b, f, bi = banks.take()
            for jj in range(4):
                j = 4 * hf + jj
                t = tr(b[:, jj * 128:(jj + 1) * 128], cg[:, j * 128:(j + 1) * 128], ident, d_vc, f)
            x = cp(act, vt[:, 4 * hf:4 * hf + 4, :], b[:, :].rearrange("p (a n) -> p a n", a=4), t, fr)
            banks.give(bi, x)
        d_v = x
        d_vt_ = t
        a = tt(pool, qb[:, :], qb[:, :], rt[:, 0, :], ALU.mult, d_rt, sw)
        x = tt(dve, qs_[:, :], qs_[:, :], rt[:, 1, :], ALU.mult, d_rt, sw)
        d_qq = tt(dve, qb[:, :], qb[:, :], qs_[:, :], ALU.add, a, x)
        a = tt(pool, kb[:, :], kb[:, :], rt[:, 0, :], ALU.mult, sw)
        x = tt(dve, ks_[:, :], ks_[:, :], rt[:, 1, :], ALU.mult, sw)
        d_kq = tt(dve, kb[:, :], kb[:, :], ks_[:, :], ALU.add, a, x)
        c8 = lambda v_: v_.rearrange("p (a n) -> p a n", a=8)
        qdec = rc[:, RC_QD + 128 * h:RC_QD + 128 * h + 128].unsqueeze(1).to_broadcast([128, 8, 128])
        d_qd = tt(pool, c8(qs_[:, :]), c8(qb[:, :]), qdec, ALU.mult, d_qq)
        d_cg = to(project(16 + 3 * h), act, cg, cfr, d_vt_)
        dk = []
        dsc = []
        for hf in range(2):
            b, f, bi = banks.take()
            for jj in range(4):
                ns = slice((4 * hf + jj) * 128, (4 * hf + jj + 1) * 128)
                t = mm(b[:, jj * 128:(jj + 1) * 128], kb[:, ns], qb[:, ns], True, True, d_qq, d_kq, f)
            dec = rc[:, RC_DM + 128 * h:RC_DM + 128 * h + 128].unsqueeze(1).to_broadcast([128, 4, 128])
            x = tt(dve, scT[:, 4 * hf:4 * hf + 4, :], b[:, :].rearrange("p (a n) -> p a n", a=4), dec, ALU.mult, t, d_rc, fr)
            banks.give(bi, x)
            dsc.append(x)
            b, f, bi = banks.take()
            for jj in range(4):
                ns = slice((4 * hf + jj) * 128, (4 * hf + jj + 1) * 128)
                t = tr(b[:, jj * 128:(jj + 1) * 128], kb[:, ns], ident, d_kq, f)
            x = ts(dve, kd[:, 4 * hf:4 * hf + 4, :], b[:, :].rearrange("p (a n) -> p a n", a=4),
                   rc[:, RC_KD + h:RC_KD + h + 1], None, ALU.mult, None, t, d_rc, fr)
            banks.give(bi, x)
            dk.append(x)
        d_u = to(project(17 + 3 * h), act, ca, cfr)
        cd = float(np.exp(retention_log(h) * np.float32(128)))
        ds = ms(dve, Sr[:, 0, :], 0.0, fr)
        dS = [ds]
        for hf in range(2):
            b, f, bi = banks.take()
            m = 4 if hf == 0 else 3
            for jj in range(m):
                n = 4 * hf + jj
                t = mm(b[:, jj * 128:(jj + 1) * 128], kd[:, n, :], vt[:, n, :], True, True, dk[hf], d_v, f)
            for jj in range(m):
                n = 4 * hf + jj
                ds = stt(Sr[:, n + 1, :], Sr[:, n, :], cd, b[:, jj * 128:(jj + 1) * 128], ALU.mult, ALU.add, t, ds)
                dS.append(ds)
            banks.give(bi, ds)
        for b, bi, t, ns in project(18 + 3 * h):
            y = tt(dve, cu[:, 2 + ns.start:2 + ns.stop], ca[:, ns], b[:, :], ALU.mult, t, d_u, z2, cfr)
            banks.give(bi, y)
        y = ts(dve, ca[:, :], cu[:, 2:T + 2], P("cw", 8 + h), None, ALU.mult, None, y)
        y = stt(ca[:, :], cu[:, 1:T + 1], P("cw", 4 + h), ca[:, :], ALU.mult, ALU.add, y)
        y = stt(ca[:, :], cu[:, 0:T], P("cw", h), ca[:, :], ALU.mult, ALU.add, y)
        cfr = tt(pool, yT[:, 4 + h, :], ca[:, :], cg[:, :], ALU.mult, d_cg, y)
        ends = []
        for hf in range(2):
            b, f, bi = banks.take()
            for jj in range(4):
                n = 4 * hf + jj
                o = b[:, jj * 128:(jj + 1) * 128]
                mm(o, vt[:, n, :], scT[:, n, :], True, False, dsc[hf], d_v, f)
                t = mm(o, Sr[:, n, :], qs_[:, n * 128:(n + 1) * 128], False, True, dS[n], d_qd)
            x = cp(act, Or[:, hf * 512:(hf + 1) * 512], b[:, :], t, fr)
            banks.give(bi, x)
            ends.append(x)
        free_q = [t, dsc]

        def norm_later(ends=ends, dk=dk, h=h, d_gt=d_gt, t=t):
            x = group_norm(Or[:, :], kb[:, :], C("on128"), 1, 1e-6, st8, ends, dk)
            return [stt(yT[:, h, :], Or[:, :], P("gn", h), gt[:, :], ALU.mult, ALU.mult, x, d_gt), t]
    norm_later()
    barrier()
    c6.close()
    h1s.close()

    xres = sb("xres", [128, 8, D], c=high)
    l_xr = [lane(f"l_xr{j}") for j in range(8)]
    NCH = 7
    wch = Ring([sb(f"wch{i}", [128, 4096], c=high) for i in range(2)])
    l_ch = [lane(f"l_ch{i}") for i in range(NCH)]

    def chunk(e, name):
        w, f, wi = wch.take()
        if name == "wd":
            src = inp[name][e].rearrange("(p c) n -> p (c n)", c=4)
            dst = w
        else:
            src = inp[name][e].rearrange("(h p q) n -> p h (q n)", h=2, q=4)
            dst = w.rearrange("p (h n) -> p h n", h=2)
        return w, wi, load(sp, l_ch[wi], dst, src, f)

    def weights(e):
        return [chunk(e, name) for name in ("wg", "wu", "wd")]

    c7 = Scope(1)
    con2 = sb("con2", [128, NC2], c=c7)
    LG = sb("LG", [128, 8, 72], c=c7)
    def K2(name, n=None):
        return con2[:, CN2[name][0]:CN2[name][0] + (n or CN2[name][1])]

    g8 = sb("g8", [128, 8, 8], c=c7)
    g8i = sb("g8i", [128, 8, 8], U32, c=c7)
    gi_ = sb("gi_", [128, 8], c=c7)
    oh8 = sb("oh8", [128, 8, 8], c=c7)
    eg = sb("eg", [128, 8, 8], c=c7)
    pg = sb("pg", [128, 8], c=c7)
    Em = sb("Em", [128, 8, 64], c=c7)
    l8 = sb("l8", [128, 8, 8], c=c7)
    l8i = sb("l8i", [128, 8, 8], U32, c=c7)
    ee = sb("ee", [128, 2, 8], c=c7)
    gk = sb("gk", [128, 2, 8], c=c7)
    OH = sb("OH", [128, 2, 8, 64], c=c7)
    Ah = sb("Ah", [128, 8, 64], c=c7)
    tmp = sb("tmp", [128, 8, 64], c=c7)
    rk_ = sb("rk_", [128, 2, 8], c=c7)
    rki = sb("rki", [128, 2, 8], I32, c=c7)
    qf = sb("qf", [128, 2, 8], c=c7)
    mf_ = sb("mf_", [128, 2, 8], c=c7)
    cnt = sb("cnt", [128, 64], c=c7)
    cnti = sb("cnti", [128, 64], I32, c=c7)
    nov = sb("nov", [128, 64], c=c7)
    ove = sb("ove", [128, 64], c=c7)
    ovb = sb("ovb", [128, 64], c=c7)
    ovk = sb("ovk", [128, 2, 8], c=c7)
    blk_ = sb("blk_", [128, 2, 8], c=c7)
    eif = sb("eif", [128, 64], c=c7)
    vals = Ring([sb(f"vals{i}", [128, 3, NBLK], c=c7) for i in range(4)])
    ohm = Ring([sb(f"ohm{i}", [128, 128], c=c7) for i in range(6)])
    tbs = sb("tbs", [128, 3, NBLK], c=c7)
    c8_ = Scope()
    wo2 = sb("wo2", [128, 8, D], c=c8_)
    n2b = sb("n2b", [128, D], c=c8_)
    rw = sb("rw", [128, 8, 72], c=c8_)
    rb_ = sb("rb_", [128, 72], c=c8_)
    junk = sb("junk5", [128, D], c=c8_)
    h2 = Ring([sb(f"h2{i}", [128, D], c=c8_) for i in range(3)])
    h2T = Ring([sb(f"h2T{i}", [128, 8, 128], c=c8_) for i in range(2)])
    l_h2 = [lane(f"l_h2{i}") for i in range(3)]
    h2d = nc.dram_tensor("h2d", [2 * T, 512], F32).ap()
    yb = nc.dram_tensor("yb", [4 * T, 512], F32).ap()
    d_wo2 = [load(sp if c % 2 else act, lane(f"l_wo2{c}"), wo2[:, c, :], inp["wo2"][c * 128:(c + 1) * 128, :]) for c in range(8)]
    d_xr = [load(act if j % 2 else sp, l_xr[j], xres[:, j, :], x1d[j * 128:(j + 1) * 128, :], d_x1) for j in range(8)]
    d_n2 = load(act, lane("l_n2"), n2b[:, :], inp["n2"].partition_broadcast(128))
    d_rw = load(sp, lane("l_rw"), rw[:, :, :], inp["rw"])
    d_rb = load(act, lane("l_rb"), rb_[:, :], inp["rb"].partition_broadcast(128))
    d_c2 = load(sp, lane("l_c2"), con2[:, :], inp["con2"])
    first = [chunk(0, "wg"), chunk(0, "wu")]
    br_, fr_, ir_ = banks.take()
    bc_, fc_, ic_ = banks.take()
    R = {}

    def route(j, a):
        j1 = slice(j, j + 1)
        i64 = K2("i64").unsqueeze(1)
        x = dve.do(lambda e: e.max(g8[:, j, :], LG[:, j, 0:8]), a)
        x = dve.do(lambda e: e.max_index(g8i[:, j, :], g8[:, j, :], LG[:, j, 0:8]), x)
        x = cp(dve, gi_[:, j1], g8i[:, j, 0:1], x)
        y = tt(dve, eg[:, j, :], LG[:, j, 0:8], g8[:, j, 0:1].to_broadcast([128, 8]), ALU.subtract, x)
        y = af(eg[:, j, :], eg[:, j, :], ACT.Exp, y)
        x = tt(dve, oh8[:, j, :], K2("i64", 8), gi_[:, j1].to_broadcast([128, 8]), ALU.is_equal, x, d_c2)
        x = ts(dve, oh8[:, j, :], oh8[:, j, :], -1.0, BIG, ALU.add, ALU.mult, x)
        x = tt(dve, Em[:, j, :].rearrange("p (g e) -> p g e", g=8), LG[:, j, 8:72].rearrange("p (g e) -> p g e", g=8),
               oh8[:, j, :].unsqueeze(2).to_broadcast([128, 8, 8]), ALU.add, x)
        x = dve.do(lambda e: e.max(l8[:, j, :], Em[:, j, :]), x)
        x = dve.do(lambda e: e.max_index(l8i[:, j, :], l8[:, j, :], Em[:, j, :]), x)
        z = tt(dve, gk[:, 1, j1], l8[:, j, 1:2], l8[:, j, 0:1], ALU.subtract, x)
        z = af(gk[:, 1, j1], gk[:, 1, j1], ACT.Exp, z)
        for k_ in range(2):
            x = cp(dve, ee[:, k_, j1], l8i[:, j, k_:k_ + 1], x)
            x = tt(dve, OH[:, k_, j, :], K2("i64"), ee[:, k_, j1].to_broadcast([128, 64]), ALU.is_equal, x)
        d_A = tt(dve, Ah[:, j, :], OH[:, 0, j, :], OH[:, 1, j, :], ALU.add, x)
        y = red(pg[:, j1], eg[:, j, :], ALU.add, y)
        y = dve.do(lambda e: e.reciprocal(pg[:, j1], pg[:, j1]), y)
        z = ts(dve, gk[:, 0, j1], gk[:, 1, j1], 1.0, None, ALU.add, None, z)
        z = dve.do(lambda e: e.reciprocal(gk[:, 0, j1], gk[:, 0, j1]), z)
        z = tt(dve, gk[:, 0, j1], gk[:, 0, j1], pg[:, j1], ALU.mult, z, y)
        d_gk = tt(dve, gk[:, 1, j1], gk[:, 1, j1], gk[:, 0, j1], ALU.mult, z)
        R.update(d_oh=d_A, d_gk=d_gk)
        R[j] = d_A

    def count(j):
        for i in range(j):
            mm(br_[:, j * 64:j * 64 + 64], C("ones"), Ah[:, i, :], i == 0, False, fr_)
        R["rank"] = mm(br_[:, j * 64:j * 64 + 64], K2("tri"), Ah[:, j, :], j == 0, True, R[j], d_c2, fr_)
        R["count"] = mm(bc_[:, 0:64], C("ones"), Ah[:, j, :], j == 0, j == 7, fc_)

    jk = None
    later = None
    lgs = []
    d_h2 = []
    for j in range(8):
        for n in range(2):
            ns = slice(n * 512, (n + 1) * 512)
            b, f, bi = banks.take()
            for c in range(8):
                t = mm(b[:, :], yT[:, c, j * 128:(j + 1) * 128], wo2[:, c, ns], c == 0, c == 7, d_wo2[c], f)
            t = tt(dve, xres[:, j, ns], xres[:, j, ns], b[:, :], ALU.add, t, d_xr[j])
            banks.give(bi, t)
        if later:
            later()
        jk = af(junk[:, :], xres[:, j, :], ACT.Square, t, jk, accum_out=small[:, 16 + j:17 + j])
        a = rms_scale(small[:, 16 + j:17 + j], small[:, 16 + j:17 + j], D, 1e-6, jk)
        hb, hf_, hi_ = h2.take()
        a = stt(hb[:, :], xres[:, j, :], small[:, 16 + j:17 + j], n2b[:, :], ALU.mult, ALU.mult, a, d_n2, hf_)
        x = load(sp, l_h2[hi_], h2d[j * 256:(j + 1) * 256, :].rearrange("(p a) n -> p (a n)", a=2), hb[:, :], a)
        d_h2.append(x)
        def later(hb=hb, hi_=hi_, j=j, a=a, x=x):
            tb, tf, ti = h2T.take()
            e_ = []
            for half in range(2):
                b, f, bi = banks.take()
                for c in range(4):
                    k_ = 4 * half + c
                    t = tr(b[:, c * 128:(c + 1) * 128], hb[:, k_ * 128:(k_ + 1) * 128], ident, a, f)
                y = cp(act, tb[:, 4 * half:4 * half + 4, :], b[:, :].rearrange("p (c n) -> p c n", c=4), t, tf)
                banks.give(bi, y)
                e_.append(y)
            h2.give(hi_, x, t)
            b, f, bi = banks.take()
            for c in range(8):
                t = mm(b[:, 0:72], tb[:, c, :], rw[:, c, :], c == 0, c == 7, e_, d_rw, f)
            h2T.give(ti, t)
            lgs.append(tt(dve, LG[:, j, :], b[:, 0:72], rb_[:, :], ALU.add, t, d_rb))
            banks.give(bi, lgs[-1])
            if j:
                count(j - 1)
            route(j, lgs[-1])
    later()
    count(7)
    sp.add(None, d_h2, Done(sp.sem), 1)
    barrier()
    c8_.close()
    mid.close()

    c9 = Scope()
    gix = sb("gix", [128, NBLK], I32, c=c9)
    six = sb("six", [128, NBLK], I32, c=c9)
    gat = sb("gat", [128, NBLK], c=c9)
    eid = sb("eid", [128, 1], I32, c=c9)
    nov_i = sb("nov_i", [128, 1], I32, c=c9)
    c11 = Scope()
    wch.bufs += [sb(f"wch{i}", [128, 4096], c=c11) for i in range(2, NCH)]
    wch.free += [[] for i in range(2, NCH)]
    W = {0: [*first, chunk(0, "wd")], 1: weights(1)}

    t, t2, d_oh, d_gk = R["rank"], R["count"], R["d_oh"], R["d_gk"]
    rank = br_[:, :].rearrange("p (j e) -> p j e", j=8)
    x = ts(dve, cnt[:, :], bc_[:, 0:64], -1.0, None, ALU.add, None, t2)
    banks.give(ic_, x)
    x = cp(dve, cnti[:, :], cnt[:, :], x)
    x = ts(dve, cnti[:, :], cnti[:, :], 6, None, ALU.arith_shift_right, None, x)
    x = cp(dve, nov[:, :], cnti[:, :], x)
    x = ts(dve, nov[:, :], nov[:, :], 0.0, None, ALU.max, None, x)
    x = dve.do(lambda e: e.tensor_tensor_scan(ove[:, :], C("ones", 0, 64), nov[:, :], 0.0, ALU.mult, ALU.add), x)
    d_ove = x
    d_ovb = tt(dve, ovb[:, :], ove[:, :], nov[:, :], ALU.subtract, x)
    d_nov = cp(dve, nov_i[:, :], ove[:, 63:64], d_ove)
    x = ts(dve, eif[:, :], ove[:, :], K2("ip"), None, ALU.is_le, None, d_ove)
    x = red(eif[:, 0:1], eif[:, :], ALU.add, x)
    x = ts(dve, eif[:, 0:1], eif[:, 0:1], 63.0, None, ALU.min, None, x)
    d_eid = cp(dve, eid[:, :], eif[:, 0:1], x)
    a = d_oh
    for k_ in range(2):
        x = tt(dve, tmp[:, :, :], OH[:, k_, :, :], rank, ALU.mult, t, a)
        x = red(rk_[:, k_, :], tmp[:, :, :], ALU.add, x)
        x = tt(dve, tmp[:, :, :], OH[:, k_, :, :], ovb[:, :].unsqueeze(1).to_broadcast([128, 8, 64]), ALU.mult, x, d_ovb)
        a = red(ovk[:, k_, :], tmp[:, :, :], ALU.add, x)
    banks.give(ir_, a)
    x = cp(dve, rki[:, :, :], rk_[:, :, :], a)
    x = ts(dve, rki[:, :, :], rki[:, :, :], 6, None, ALU.arith_shift_right, None, x)
    x = cp(dve, qf[:, :, :], rki[:, :, :], x)
    d_m = stt(mf_[:, :, :], qf[:, :, :], -64.0, rk_[:, :, :], ALU.mult, ALU.add, x)
    x = tt(dve, ovk[:, :, :], ovk[:, :, :], qf[:, :, :], ALU.add, d_m)
    x = ts(dve, ovk[:, :, :], ovk[:, :, :], 63.0, None, ALU.add, None, x)
    x = tt(dve, ovk[:, :, :], ovk[:, :, :], ee[:, :, :], ALU.subtract, x)
    x = ts(dve, qf[:, :, :], qf[:, :, :], 0.0, None, ALU.is_gt, None, x)
    x = tt(dve, ovk[:, :, :], ovk[:, :, :], qf[:, :, :], ALU.mult, x)
    d_bl = tt(dve, blk_[:, :, :], ovk[:, :, :], ee[:, :, :], ALU.add, x)
    bt, ft, it = banks.take()
    for k_ in range(2):
        for j in range(8):
            va, vf, vi = vals.take()
            oa, of_, oi_ = ohm.take()
            bcol = blk_[:, k_, j:j + 1]
            srcs = [K2("tok")[:, j:j + 1], K2("dst")[:, 8 * k_ + j:8 * k_ + j + 1], gk[:, k_, j:j + 1]]
            for n, sc_ in enumerate(srcs):
                x = ts(dve, va[:, n, :], K2("i96"), bcol, sc_, ALU.is_equal, ALU.mult, d_bl, d_gk, vf)
            y = ts(pool, oa[:, :], K2("im"), mf_[:, k_, j:j + 1], None, ALU.is_equal, None, d_m, of_)
            t = mm(bt[:, 0:3 * NBLK], oa[:, :], va[:, :, :].rearrange("p a n -> p (a n)"),
                   k_ == 0 and j == 0, k_ == 1 and j == 7, x, y, ft)
            vals.give(vi, t)
            ohm.give(oi_, t)
    x = cp(dve, tbs[:, :, :], bt[:, 0:3 * NBLK].rearrange("p (a n) -> p a n", a=3), t)
    banks.give(it, x)
    d_ix = [ts(dve, o_[:, :], tbs[:, n, :], 2.0, K2("half"), ALU.mult, ALU.add, x) for n, o_ in ((0, gix), (1, six))]
    d_ga = cp(dve, gat[:, :], tbs[:, 2, :], x)
    barrier(pe, act, dve, pool)
    c7.close()

    xg = Ring([sb(f"xg{i}", [128, 512], c=c11) for i in range(3)])
    l_xg = [lane(f"l_xg{i}") for i in range(3)]
    xT = Ring([sb(f"xT{i}", [128, 4, 128], c=c11) for i in range(2)])
    Gs = Ring([sb(f"Gs{i}", [128, 512], c=c11) for i in range(2)])
    sg_ = Ring([sb(f"sg{i}", [128, 4, 64], c=c11) for i in range(2)])
    ys = Ring([sb(f"ys{i}", [128, 512], c=c11) for i in range(2)])
    l_ys = [lane(f"l_ys{i}") for i in range(2)]
    zx = [ms(pool, xg.bufs[i][:, :], 0.0) for i in range(3)]

    def gather(q, ln, dst, col, *w):
        return q.dma(ln, lambda e: e.indirect_dma_start(
            dst[:, :], None, h2d, bass.IndirectOffsetOnAxis(ap=gix[:, col:col + 1].bitcast(U32), axis=0),
            bounds_check=2 * T - 1, oob_is_err=False), *w)

    def scatter(q, ln, src, col, *w):
        return q.dma(ln, lambda e: e.indirect_dma_start(
            yb, bass.IndirectOffsetOnAxis(ap=six[:, col:col + 1].bitcast(U32), axis=0), src[:, :], None,
            bounds_check=4 * T - 1, oob_is_err=False), *w)

    def turn_x(qs, x, dst, *w):
        pe_, ev_, bk = qs
        b, f, bi = bk.take()
        for q in range(4):
            t = pe_.do(lambda e, q=q: e.transpose(b[:, q * 128:(q + 1) * 128], x[:, q:512:4], ident), w, f)
        y = cp(ev_, dst[:, :, :], b[:, :].rearrange("p (a n) -> p a n", a=4), t)
        bk.give(bi, y)
        return t, y

    def hidden(qs, w, xt_, *wt):
        pe_, _, bk = qs
        b, f, bi = bk.take()
        for i in range(8):
            h, q = i // 4, i % 4
            o = b[64 * (i % 2):64 * (i % 2) + 64, :]
            t = pe_.do(lambda e, o=o, h=h, q=q, i=i: e.matmul(
                o, xt_[:, q, 64 * h:64 * h + 64], w[:, (4 * h + q) * 512:(4 * h + q + 1) * 512], start=i < 2, stop=i > 5), wt, f)
        return b, bi, t

    def turn_h(pe_, b, off, gs, *w):
        for c in range(4):
            t = pe_.do(lambda e, c=c: e.matmul(b[:, off + c * 64:off + c * 64 + 64], gs[:, c:512:4], C("id2", 0, 64),
                                               start=True, stop=True), *w)
        return t

    def down(pe_, b, w, hT_, *wt):
        for c in range(4):
            for n in range(2):
                t = pe_.do(lambda e, c=c, n=n: e.matmul(b[64 * n:64 * n + 64, :], hT_[:, c, :],
                                                        w[:, c * 1024 + n * 512:c * 1024 + n * 512 + 512],
                                                        start=c == 0, stop=c == 3), *wt)
        return t

    X, XT, HT, last_sc = {}, {}, {}, []

    def fetch(e):
        x, f, xi = xg.take()
        X[e] = (x, xi, gather(pool, l_xg[xi], x, e, f, zx))

    def prepare(e):
        x, xi, dx = X.pop(e)
        o, f, oi = xT.take()
        t, y = turn_x((pe, act, banks), x, o, dx, f)
        xg.give(xi, t)
        XT[e] = (o, oi, y)

    def finish_expert(e):
        h_, hi_, dh = HT.pop(e)
        w, wi, dw = W[e][2]
        b, f, bi = banks.take()
        t = down(pe, b, w, h_, dh, dw, f)
        wch.give(wi, t)
        sg_.give(hi_, t)
        y, f, yi = ys.take()
        x = ts(dve, y[:, :], b[:, :], gat[:, e:e + 1], None, ALU.mult, None, t, f)
        banks.give(bi, x)
        d = scatter(pool, l_ys[yi], y, e, x)
        ys.give(yi, d)
        last_sc.append(d)

    fetch(0)
    fetch(1)
    prepare(0)
    for e in range(NEXP):
        if 0 < e < NEXP - 1:
            W[e + 1] = weights(e + 1)
        if e + 2 < NEXP:
            fetch(e + 2)
        xt_, xi, dx = XT.pop(e)
        (wg_, gi1, dg), (wu_, ui1, du), _ = W[e]
        bg, ig, tg = hidden((pe, None, banks), wg_, xt_, dx, dg)
        wch.give(gi1, tg)
        bu, iu, tu = hidden((pe, None, banks), wu_, xt_, du)
        wch.give(ui1, tu)
        xT.give(xi, tu)
        g1, f1, i1 = Gs.take()
        yg = cp(act, g1[:, :], bg[:, :], tg, f1)
        banks.give(ig, yg)
        u1, f2, i2 = Gs.take()
        yu = cp(dve, u1[:, :], bu[:, :], tu, f2)
        banks.give(iu, yu)
        if e + 1 < NEXP:
            prepare(e + 1)
        if e > 0:
            finish_expert(e - 1)
        b, f, bi = banks.take()
        t1 = turn_h(pe, b, 0, g1, yg, f)
        t2 = turn_h(pe, b, 256, u1, yu)
        Gs.give(i1, t1)
        Gs.give(i2, t2)
        s1, f3, i3 = sg_.take()
        b4 = b[:, :].rearrange("p (a n) -> p a n", a=8)
        x = af(s1[:, :, :], b4[:, 0:4, :], ACT.Silu, t2, f3)
        x = tt(dve, s1[:, :, :], s1[:, :, :], b4[:, 4:8, :], ALU.mult, x, t2)
        banks.give(bi, x)
        HT[e] = (s1, i3, x)
    finish_expert(NEXP - 1)
    pool.add(None, last_sc, Done(pool.sem), 1)
    barrier()

    oq = {n: Queue(sem(f"o_{n}")) for n in ("pe", "act", "dve", "pool", "sp")}
    ol = {n: lane(f"o_l{n}") for n in ("g", "u", "d", "x", "y")}
    wts = [wch.bufs[i] for i in range(3)]
    ox, oxT, og, ou = xg.bufs[0], xT.bufs[0], Gs.bufs[0], Gs.bufs[1]
    osg, oy = sg_.bufs[0], ys.bufs[0]
    regs = {}
    before = [None]

    def further(n):
        col = NEXP + n
        q = oq if n == 0 else {k_: Queue(oq[k_].sem) for k_ in oq}
        last = before[0]

        def wload(nm, ln, dst, view):
            def fn(e):
                v = e.value_load(eid[n:n + 1, 0:1], min_val=0, max_val=NEXP - 1)
                return e.dma_start(dst, view(inp[nm][bass.ds(v, 1)]))
            return q["sp"].dma(ol[ln], fn, last)

        dws = [wload(nm, ln, wts[k_].rearrange("p (h n) -> p h n", h=2),
                     lambda v: v.rearrange("a (h p q) n -> p (a h) (q n)", h=2, q=4))
               for k_, (nm, ln) in enumerate((("wg", "g"), ("wu", "u")))]
        dws.append(wload("wd", "d", wts[2], lambda v: v.rearrange("a (p c) n -> p (a c n)", c=4)))
        dx = gather(q["pool"], ol["x"], ox, col, last)
        bk = Ring([banks.bufs[i] for i in range(8)])
        t, y = turn_x((q["pe"], q["dve"], bk), ox, oxT, dx)
        bg, _, tg = hidden((q["pe"], None, bk), wts[0], oxT, y, dws[0])
        bu, _, tu = hidden((q["pe"], None, bk), wts[1], oxT, dws[1])
        yg = cp(q["dve"], og[:, :], bg[:, :], tg)
        yu = cp(q["dve"], ou[:, :], bu[:, :], tu)
        b, _, _ = bk.take()
        t1 = turn_h(q["pe"], b, 0, og, yg)
        t2 = turn_h(q["pe"], b, 256, ou, yu)
        b4 = b[:, :].rearrange("p (a n) -> p a n", a=8)
        x = q["act"].do(lambda e: e.activation(osg[:, :, :], b4[:, 0:4, :], ACT.Silu), t2)
        x = tt(q["dve"], osg[:, :, :], osg[:, :, :], b4[:, 4:8, :], ALU.mult, x, t2)
        b, _, _ = bk.take()
        t = down(q["pe"], b, wts[2], osg, x, dws[2])
        x = ts(q["dve"], oy[:, :], b[:, :], gat[:, col:col + 1], None, ALU.mult, None, t)
        d = scatter(q["pool"], ol["y"], oy, col, x)
        before[0] = q["pool"].do(lambda e: e.nop(), d)
        return q

    for nm, q in (("pe", pe), ("act", act), ("dve", dve), ("pool", pool), ("sp", sp)):
        def ld(e, nm=nm):
            regs[nm] = e.alloc_register(f"n_{nm}")
            return e.reg_load(regs[nm], nov_i[0:1, 0:1])
        q.do(ld)
    bodies = [further(n) for n in range(NOVER)]
    for nm, q in (("pe", pe), ("act", act), ("dve", dve), ("pool", pool), ("sp", sp)):
        outer = Queue(oq[nm].sem)
        for n in range(NOVER):
            outer.when(lambda e, nm=nm: regs[nm], n, bodies[n][nm])
        q.when(lambda e, nm=nm: regs[nm], 0, outer)
        q.do(lambda e: e.nop())
    barrier()
    c11.close()

    c12 = Scope()
    fnb = sb("fnb", [128, D], c=c12)
    d_fn = load(act, lane("l_fn"), fnb[:, :], inp["fn"].partition_broadcast(128))
    yl = [sb(f"yl{i}", [128, 2 * D], c=c12) for i in range(8)]
    for j in range(8):
        y = yl[j]
        dy = load(sp, lane(f"l_yl{j}"), y[:, :], yb[j * 512:(j + 1) * 512, :].rearrange("(p a) n -> p (a n)", a=4))
        x = tt(pool, y[:, 0:D], y[:, 0:D], y[:, D:2 * D], ALU.add, dy)
        x = tt(dve, y[:, 0:D], y[:, 0:D], xres[:, j, :], ALU.add, x)
        a = af(y[:, D:2 * D], y[:, 0:D], ACT.Square, x, accum_out=small[:, 24 + j:25 + j])
        if j % 4 < 3:
            continue
        js = range(j - 3, j + 1)
        a = rms_scale(small[:, 21 + j:25 + j], small[:, 21 + j:25 + j], D, 1e-6, a)
        for n in js:
            x = stt(yl[n][:, 0:D], yl[n][:, 0:D], small[:, 24 + n:25 + n], fnb[:, :], ALU.mult, ALU.mult, a, d_fn)
            outs.append(load(sp if n > 3 else act, lane(f"l_out{n}"), out[n * 128:(n + 1) * 128, :], yl[n][:, 0:D], x))
    return finish(nc, ctx, (pe, act, dve, pool, sp), outs)


def finish(nc, ctx, queues, outs):
    pe, act, dve, pool, sp = queues
    sp.add(None, outs, Done(sp.sem), 1)
    counts = {}
    for q in queues:
        q.number(counts)
    block = ctx.enter_context(nc.Block())

    @block.tensor
    def _(eng):
        pe.emit(eng)

    @block.scalar
    def _(eng):
        act.emit(eng)

    @block.vector
    def _(eng):
        dve.emit(eng)

    @block.gpsimd
    def _(eng):
        pool.emit(eng)

    @block.sync
    def _(eng):
        sp.emit(eng)

    ctx.close()


def constants():
    p = np.arange(128)
    s, t = p[:, None], p[None, :]
    c = np.zeros((128, NCON), np.float32)

    def put(name, a, at=0):
        a = np.asarray(a, np.float32)
        c[:, CON[name] + at:CON[name] + at + a.shape[1]] = a

    same = s // 64 == t // 64
    put("id", s == t)
    put("sc", (s < t) & same, 0)
    put("sc", (s <= t) & same, 128)
    put("sc", (s < t) & same, 256)
    put("sc", (s <= t) & same, 384)
    m1 = (s % 2 == 1) & (t == s - 1)
    put("m1", m1)
    put("m1t", m1.T)
    for n in range(5):
        m = 2 << n
        put("lv", (s // (2 * m) == t // (2 * m)) & ((s // m) % 2 == 1) & ((t // m) % 2 == 0), n * 128)
    put("blk", same)
    put("blkm", same / 64.0)
    pm = np.zeros((128, 128))
    for h in (0, 64):
        for m in range(8):
            pm[h + m + 8, h + m] = -1.0
            pm[h + m, h + m + 8] = 1.0
    put("perm", pm)
    put("diag", np.where(t > s, -BIG, 0.0))
    put("far", np.where(t <= s, -BIG, 0.0))
    put("ones", np.ones((128, 128)))
    put("on128", np.full((128, 128), 1 / 128.0))
    put("id2", s[:, :1] % 64 == t[:, :64])
    return c


def layout(i):
    w = i["w_in"][0]
    cols = []
    for g in range(16):
        cols.append(np.arange(g * 128, (g + 1) * 128))
    cols.append(np.arange(2048, 2176))
    n0 = 2176
    cols += [np.arange(n0 + k * 128, n0 + (k + 1) * 128) for k in range(4)]
    kc, vc, ks, vs, kw, vw = (np.arange(n0 + 524 + k * 64, n0 + 588 + k * 64) for k in range(6))
    cols.append(np.concatenate([ks, kw]))
    cols.append(np.concatenate([kc, vc]))
    m0 = 2176 + 908
    cols += [np.arange(m0 + k * 128, m0 + (k + 1) * 128) for k in range(4)]
    a = {"x": i["x"][0], "mem": i["mem"][0]}
    a["w1"] = np.stack([w[:, c].reshape(8, 128, 128).transpose(1, 0, 2) for c in cols])
    vcol = np.concatenate([vs, vw, np.arange(n0 + 512, n0 + 524)])
    a["wv"] = np.ascontiguousarray(w[:, vcol].reshape(8, 128, 140).transpose(1, 0, 2))
    a["up"] = np.concatenate([i["rwkv_w_up"][0], i["rwkv_a_up"][0]], axis=0)
    par = [("mu", "rwkv_mu"), ("w0", "rwkv_w0"), ("a0", "rwkv_a0"), ("kk", "rwkv_k_k"), ("ka", "rwkv_k_a"),
           ("rk", "rwkv_r_k"), ("lnw", "rwkv_ln_w"), ("lnb", "rwkv_ln_b"), ("nin", "norm_in_g"),
           ("nmem", "mem_norm_g"), ("nsag", "nsa_out_g"), ("memg", "mem_out_g"), ("gn", "ret_gn_w_2"),
           ("cw", "conv_w_2"), ("n1", "norm1_w_2")]
    a["par"] = np.ascontiguousarray(np.concatenate([i[k].reshape(-1, 128) for _, k in par], axis=0).T)
    a["con"] = constants()
    pos = np.arange(T, dtype=np.float32)
    inv = np.float32(500000.0) ** (-np.arange(8, dtype=np.float32) / np.float32(8))
    ang = pos[None, :] * inv.astype(np.float32)[:, None]
    rope = np.zeros((128, 2, T), np.float32)
    rope[:, 0] = 1.0
    for h in (0, 64):
        for o in (0, 8):
            rope[h + o:h + o + 8, 0] = np.cos(ang)
            rope[h + o:h + o + 8, 1] = np.sin(ang)
    a["rope"] = rope
    w1 = [i[f"nsa_cmp_{n}_w1"][0].reshape(32, 64, 64).transpose(1, 0, 2) for n in "kv"]
    a["cw1"] = np.ascontiguousarray(np.concatenate(w1, axis=0))
    a["cw2"] = np.concatenate([np.concatenate([i[f"nsa_cmp_{n}_w2"][0]] * 2, axis=1) for n in "kv"], axis=0)
    a["cpos"] = np.ascontiguousarray(np.concatenate([i["nsa_cmp_pos"][0].T] * 2, axis=0))
    a["wmem"] = i["w_mem_kv"][0]
    seen = (16 * np.arange(64) + 31)[None, None, :] <= (128 * np.arange(8)[None, :] + np.arange(128)[:, None])[:, :, None]
    a["cmask"] = np.stack([np.where(seen, 0.0, -BIG), seen], axis=1).astype(np.float32)
    a["gb"] = i["nsa_gate_b"][0]
    a["nfg"] = i["norm_final_g"]
    a["wo"] = i["w_out"][0]

    w = i["w_in_2"][0]
    starts = []
    for h in range(4):
        starts += [h * 128 + 512 * k for k in range(4)]
    for h in range(4):
        starts += [2048 + h * 128 + 512 * k for k in range(3)]
    a["w2"] = np.stack([w[:, c:c + 128].reshape(8, 128, 128).transpose(1, 0, 2) for c in starts])
    inv = np.float32(10000.0) ** (-np.arange(64, dtype=np.float32) / np.float32(64))
    ang = pos[None, :] * inv.astype(np.float32)[:, None]
    co, si = np.cos(ang), np.sin(ang)
    a["rot"] = np.ascontiguousarray(np.stack([np.concatenate([co, co]), np.concatenate([-si, si])], axis=1).astype(np.float32))
    rc = np.zeros((128, NRC), np.float32)
    idx = np.arange(128, dtype=np.float32)
    scale = np.float32(128 ** -0.5)
    for h in range(4):
        lg = retention_log(h)
        rel = idx[None, :] - idx[:, None]
        rc[:, RC_DM + 128 * h:RC_DM + 128 * h + 128] = np.where(rel >= 0, np.exp(lg * np.where(rel >= 0, rel, 0)), 0) * scale
        rc[:, RC_QD + 128 * h:RC_QD + 128 * h + 128] = (np.exp(lg * (idx + 1)) * scale)[None, :]
        rc[:, RC_KD + h] = np.exp(lg * (127 - idx))
    a["rc"] = rc
    a["wo2"] = i["w_o_2"][0]
    a["n2"] = i["norm2_w_2"][0]
    re = i["router_e_w_2"][0].transpose(1, 0, 2).reshape(1024, 64)
    rw = np.concatenate([i["router_g_w_2"][0], re], axis=1)
    a["rw"] = np.ascontiguousarray(rw.reshape(8, 128, 72).transpose(1, 0, 2))
    a["rb"] = np.concatenate([i["router_g_b_2"].reshape(-1), i["router_e_b_2"].reshape(-1)])
    a["wg"], a["wu"], a["wd"] = i["w_gate_2"][0], i["w_up_2"][0], i["w_down_2"][0]
    a["fn"] = i["final_norm_w_2"]
    c2 = np.zeros((128, NC2), np.float32)
    p = np.arange(128)[:, None]

    def put(name, v):
        o, k = CN2[name]
        c2[:, o:o + k] = v

    put("i64", np.arange(64)[None, :])
    put("i96", np.arange(NBLK)[None, :])
    put("im", (np.arange(128) % 64)[None, :])
    put("tri", p < np.arange(128)[None, :])
    tok = 128 * np.arange(8)[None, :] + p
    put("tok", tok + 1)
    put("dst", np.concatenate([2 * tok + 1, 2 * tok + 2], axis=1))
    put("half", p // 64 - 2)
    put("ip", p)
    a["con2"] = c2
    return a


def kernel(**inputs):
    import concourse.bacc as bacc
    from concourse.bass_utils import run_bass_kernel_spmd

    arrays = {f"in_{k}": np.ascontiguousarray(v) for k, v in layout({k: np.asarray(v) for k, v in inputs.items()}).items()}
    nc = bacc.Bacc("TRN2", target_bir_lowering=False, num_devices=1)
    inp = {k[3:]: nc.dram_tensor(k, v.shape, mybir.dt.from_np(v.dtype), kind="ExternalInput").ap()
           for k, v in arrays.items()}
    out = nc.dram_tensor("out_x", (T, D), F32, kind="ExternalOutput").ap()
    program(nc, inp, out)
    r = run_bass_kernel_spmd(nc, [arrays], core_ids=[0])
    return r.results[0]["out_x"].reshape(1, T, D)
```
